# Optimizing a Trainium2 kernel written in Bass

```python
import jax, jax.numpy as jnp
from jax import lax
import numpy as np

'''Two-layer hybrid decoder trunk (post-norm DeepNorm, adaLN conditioning).

Per layer:
  mixer sub-layer:   u = x*(1+scale1(c)) + shift1(c)
                     one combined projection of u -> [conv B | conv C | conv x | q | k | v | gate_A | gate_B]
                     branch A: short gated conv   yA = W_A( B * dwconv3_causal( C * x_conv ) )
                     branch B: stick-breaking attention (no softmax, no positions), yB = W_B(concat_heads)
                     merged = sigmoid(gate_A)*yA + sigmoid(gate_B)*yB ;  mix = merged @ W_o
                     x = LayerNorm(alpha*x + g1(c)*mix)
  channel sub-layer: u2 = x*(1+scale2(c)) + shift2(c)
                     group-limited top-2 mixture of SwiGLU experts, router shared by all layers
                     x = LayerNorm(alpha*x + g2(c)*moe(u2))
Inputs: x (BATCH, SEQ, D_MODEL) f32, c (BATCH, D_MODEL) f32, per-layer weights stacked on a leading DEPTH axis.
Output: (BATCH, SEQ, D_MODEL).
'''

D_MODEL = 1024
BATCH = 1
SEQ = 2048
DEPTH = 1

CONV_CH = D_MODEL // 2
CONV_K = 3
N_HEADS = 8
HEAD_DIM = 64
ATTN_W = N_HEADS * HEAD_DIM
Q_BLOCK = 128
IN_WIDTH = 3 * CONV_CH + 3 * ATTN_W + 2 * D_MODEL
N_EXPERTS = 16
N_GROUPS = 4
EXPERTS_PER_GROUP = N_EXPERTS // N_GROUPS
TOP_K = 2
EXPERT_FF = 512
MOE_BLOCK = 128
LN_EPS = 1e-5
DN_ALPHA = (2 * DEPTH) ** 0.25
DN_BETA = (8 * DEPTH) ** -0.25

kernel_name = 'hybrid_conv_stickbreak_groupmoe_deepnorm_adaln'

def layer_norm(h, g, b):
    hf = h.astype(jnp.float32)
    mu = jnp.mean(hf, axis=-1, keepdims=True)
    var = jnp.mean(jnp.square(hf - mu), axis=-1, keepdims=True)
    y = (hf - mu) * lax.rsqrt(var + LN_EPS) * g.astype(jnp.float32) + b.astype(jnp.float32)
    return y.astype(h.dtype)

def causal_dwconv(h, w):
    S = h.shape[1]
    hp = jnp.pad(h, ((0, 0), (CONV_K - 1, 0), (0, 0)))
    out = w[CONV_K - 1] * h
    for j in range(CONV_K - 1):
        out = out + w[j] * hp[:, j:j + S]
    return out

def stick_breaking_attention(q, k, v):
    S = q.shape[2]
    scale = HEAD_DIM ** -0.5
    outs = []
    for i in range(S // Q_BLOCK):
        q0 = i * Q_BLOCK
        end = q0 + Q_BLOCK
        qb = q[:, :, q0:end]
        kb = k[:, :, :end]
        vb = v[:, :, :end]
        z = jnp.einsum('bhqd,bhkd->bhqk', qb, kb, preferred_element_type=jnp.float32) * scale
        t_idx = q0 + jnp.arange(Q_BLOCK)[:, None]
        s_idx = jnp.arange(end)[None, :]
        mask = s_idx < t_idx
        log1m = jnp.where(mask, jax.nn.log_sigmoid(-z), 0.0)
        between = lax.cumsum(log1m, axis=3, reverse=True) - log1m
        attn = jnp.where(mask, jnp.exp(jax.nn.log_sigmoid(z) + between), 0.0)
        outs.append(jnp.einsum('bhqk,bhkd->bhqd', attn.astype(vb.dtype), vb))
    return jnp.concatenate(outs, axis=2)

def token_mixer(u, w_in, w_conv, w_a, w_b, w_o):
    Bn, Sn, _ = u.shape
    proj = u @ w_in
    cuts = np.cumsum([CONV_CH, CONV_CH, CONV_CH, ATTN_W, ATTN_W, ATTN_W, D_MODEL])
    cb, cc, cx, q, k, v, ga, gb = jnp.split(proj, cuts, axis=-1)
    y_a = (cb * causal_dwconv(cc * cx, w_conv)) @ w_a
    heads = lambda t: t.reshape(Bn, Sn, N_HEADS, HEAD_DIM).transpose(0, 2, 1, 3)
    o = stick_breaking_attention(heads(q), heads(k), heads(v))
    y_b = o.transpose(0, 2, 1, 3).reshape(Bn, Sn, ATTN_W) @ w_b
    merged = jax.nn.sigmoid(ga) * y_a + jax.nn.sigmoid(gb) * y_b
    return merged @ w_o

def moe_ffn(u, w_router, b_router, w_gate, w_up, w_down):
    Bn, Sn, D = u.shape
    N = Bn * Sn
    xf = u.reshape(N, D)
    aff = jax.nn.sigmoid((xf @ w_router).astype(jnp.float32))
    sel = (aff + b_router.astype(jnp.float32)).reshape(N, N_GROUPS, EXPERTS_PER_GROUP)
    grp_score = lax.top_k(sel, TOP_K)[0].sum(-1)
    g_idx = jnp.argmax(grp_score, axis=-1)
    in_grp = jnp.take_along_axis(sel, g_idx[:, None, None], axis=1)[:, 0]
    _, local = lax.top_k(in_grp, TOP_K)
    e_idx = g_idx[:, None] * EXPERTS_PER_GROUP + local
    gates = jnp.take_along_axis(aff, e_idx, axis=1)
    gates = gates / jnp.sum(gates, axis=-1, keepdims=True)
    A = N * TOP_K
    flat_e = e_idx.reshape(A).astype(jnp.int32)
    flat_tok = jnp.repeat(jnp.arange(N, dtype=jnp.int32), TOP_K)
    flat_w = gates.reshape(A)
    order = jnp.argsort(flat_e)
    s_e = flat_e[order]
    s_tok = flat_tok[order]
    s_w = flat_w[order]
    counts = jnp.bincount(flat_e, length=N_EXPERTS)
    pad_counts = (counts + MOE_BLOCK - 1) // MOE_BLOCK * MOE_BLOCK
    pad_end = jnp.cumsum(pad_counts)
    pad_start = pad_end - pad_counts
    start = jnp.cumsum(counts) - counts
    dest = pad_start[s_e] + (jnp.arange(A, dtype=jnp.int32) - start[s_e])
    n_blocks = -(-A // MOE_BLOCK) + N_EXPERTS
    P = n_blocks * MOE_BLOCK
    row_tok = jnp.full((P,), N, dtype=jnp.int32).at[dest].set(s_tok)
    x_ext = jnp.concatenate([xf, jnp.zeros((1, D), xf.dtype)], axis=0)
    x_blocks = x_ext[row_tok].reshape(n_blocks, MOE_BLOCK, D)
    block_start = jnp.arange(n_blocks, dtype=jnp.int32) * MOE_BLOCK
    block_exp = jnp.clip(jnp.searchsorted(pad_end, block_start, side='right'), 0, N_EXPERTS - 1)

    def expert_block(args):
        xb, e = args
        h = jax.nn.silu(xb @ w_gate[e]) * (xb @ w_up[e])
        return h @ w_down[e]

    y_blocks = lax.map(expert_block, (x_blocks, block_exp))
    y_sorted = y_blocks.reshape(P, D)[dest]
    out = jax.ops.segment_sum(y_sorted.astype(jnp.float32) * s_w[:, None], s_tok, num_segments=N)
    return out.astype(u.dtype).reshape(Bn, Sn, D)

def setup_inputs(seed: int = 0) -> dict:
    key = jax.random.key(seed)
    ks = jax.random.split(key, 20)
    nrm = lambda k, shape: jax.random.normal(k, shape, jnp.float32)
    col_scale = jnp.concatenate([
        jnp.ones((2 * CONV_CH,), jnp.float32), jnp.full((CONV_CH,), DN_BETA, jnp.float32),
        jnp.ones((2 * ATTN_W,), jnp.float32), jnp.full((ATTN_W,), DN_BETA, jnp.float32),
        jnp.ones((2 * D_MODEL,), jnp.float32)])
    return {
        'x': nrm(ks[0], (BATCH, SEQ, D_MODEL)),
        'c': nrm(ks[1], (BATCH, D_MODEL)),
        'w_ada': nrm(ks[2], (DEPTH, D_MODEL, 6 * D_MODEL)) * D_MODEL ** -0.5,
        'b_ada': 0.02 * nrm(ks[3], (DEPTH, 6 * D_MODEL)),
        'w_in': nrm(ks[4], (DEPTH, D_MODEL, IN_WIDTH)) * D_MODEL ** -0.5 * col_scale,
        'w_conv': nrm(ks[5], (DEPTH, CONV_K, CONV_CH)) * CONV_K ** -0.5,
        'w_a': nrm(ks[6], (DEPTH, CONV_CH, D_MODEL)) * CONV_CH ** -0.5,
        'w_b': nrm(ks[7], (DEPTH, ATTN_W, D_MODEL)) * ATTN_W ** -0.5,
        'w_o': nrm(ks[8], (DEPTH, D_MODEL, D_MODEL)) * D_MODEL ** -0.5 * DN_BETA,
        'ln1_g': 1.0 + 0.02 * nrm(ks[9], (DEPTH, D_MODEL)),
        'ln1_b': 0.02 * nrm(ks[10], (DEPTH, D_MODEL)),
        'w_router': nrm(ks[11], (D_MODEL, N_EXPERTS)) * D_MODEL ** -0.5,
        'b_router': 0.01 * nrm(ks[12], (N_EXPERTS,)),
        'w_gate': nrm(ks[13], (DEPTH, N_EXPERTS, D_MODEL, EXPERT_FF)) * D_MODEL ** -0.5,
        'w_up': nrm(ks[14], (DEPTH, N_EXPERTS, D_MODEL, EXPERT_FF)) * D_MODEL ** -0.5,
        'w_down': nrm(ks[15], (DEPTH, N_EXPERTS, EXPERT_FF, D_MODEL)) * EXPERT_FF ** -0.5 * DN_BETA,
        'ln2_g': 1.0 + 0.02 * nrm(ks[16], (DEPTH, D_MODEL)),
        'ln2_b': 0.02 * nrm(ks[17], (DEPTH, D_MODEL)),
    }

def reference(x, c, w_ada, b_ada, w_in, w_conv, w_a, w_b, w_o, ln1_g, ln1_b,
              w_router, b_router, w_gate, w_up, w_down, ln2_g, ln2_b):
    for l in range(DEPTH):
        mod = jax.nn.silu(c) @ w_ada[l] + b_ada[l]
        sh1, sc1, g1, sh2, sc2, g2 = [m[:, None, :] for m in jnp.split(mod, 6, axis=-1)]
        u = x * (1.0 + sc1) + sh1
        mix = token_mixer(u, w_in[l], w_conv[l], w_a[l], w_b[l], w_o[l])
        x = layer_norm(DN_ALPHA * x + g1 * mix, ln1_g[l], ln1_b[l])
        u2 = x * (1.0 + sc2) + sh2
        ffn = moe_ffn(u2, w_router, b_router, w_gate[l], w_up[l], w_down[l])
        x = layer_norm(DN_ALPHA * x + g2 * ffn, ln2_g[l], ln2_b[l])
    return x


_drawn_inputs = setup_inputs


def setup_inputs(seed=0):
    import zlib

    import numpy as np

    out = dict(_drawn_inputs(seed))
    spreads = {}
    factors = {}
    for name, (base, spread) in spreads.items():
        noise = np.random.default_rng([zlib.crc32(name.encode()), seed]).standard_normal(out[name].shape)
        drawn = base * np.exp(spread * noise) if base else spread * noise
        out[name] = __import__('jax').numpy.asarray(drawn.astype(out[name].dtype))
    for name, factor in factors.items():
        out[name] = (out[name] * factor).astype(out[name].dtype)
    return out
```

```python
from contextlib import ExitStack

import concourse.bass as bass
from concourse import mybir

F32 = mybir.dt.float32
F32R = mybir.dt.float32r
I32 = mybir.dt.int32
U32 = mybir.dt.uint32
ALU = mybir.AluOpType
ACT = mybir.ActivationFunctionType
AX = mybir.AxisListType

P = 128
NB = 512
D = 1024
S = 2048
KD = D // P
NT = S // P
TB = S // NB
CH = 512
HEADS = 8
HD = 64
AW = HEADS * HD
KC = CH // P
E = 16
G = 4
EG = E // G
FF = 512
KF = FF // P
CAP = S + P
BLOCKS = 2 * S // P + E
EPS = 1e-5
ALPHA = 2.0 ** 0.25
BIG = 1e30

SH1, SC1, G1, SH2, SC2, G2 = (KD * i for i in range(6))


class Scope:

    def __init__(self, nc, ctx, tag):
        self.nc, self.ctx, self.tag = nc, ctx, tag

    def sb(self, name, shape, dt=F32):
        return self.ctx.enter_context(self.nc.sbuf_tensor(f"{self.tag}_{name}", shape, dt))

    def ps(self, name, shape, dt=F32):
        return self.ctx.enter_context(self.nc.psum_tensor(f"{self.tag}_{name}", shape, dt))

    def sem(self, name):
        return self.ctx.enter_context(self.nc.semaphore(f"{self.tag}_{name}"))


def f32(ap):
    return ap.bitcast(F32)


def wait_apart(eng, mark, sem, value):
    eng.wait_ge(sem, value)
    eng.sem_inc(mark, 1)


def product(pe, out, pairs, first, last):
    for n, (a, b) in enumerate(pairs):
        mm = pe.matmul(out, a, b, start=first and n == 0, stop=last and n == len(pairs) - 1,
                       skip_group_check=True)
    return mm


def modulation(nc, keep, c, w_ada, b_ada, w_conv, mod_rows):
    ident, mod, conv_cols = keep["ident"], keep["mod"], keep["conv_cols"]
    NJ = 6 * KD
    VR = NJ + KD + 3 * KC
    RING = 4
    with ExitStack() as ctx:
        s = Scope(nc, ctx, "ada")
        vec = s.sb("vec", [VR, P])
        cols = s.sb("cols", [P, VR])
        csilu = s.sb("csilu", [P, KD])
        w = s.sb("w", [P, RING, KD, NB])
        mod_t = s.sb("mod_t", [NJ, P])
        p_vec = s.ps("p_vec", [P, NB])
        p_mod = s.ps("p_mod", [P, NB])
        p_row = s.ps("p_row", [P, NB])
        vec_in, vec_turned, cols_out = s.sem("vec_in"), s.sem("vec_turned"), s.sem("cols_out")
        ident_zero, ident_done = s.sem("ident_zero"), s.sem("ident_done")
        silu_done, w_used = s.sem("silu_done"), s.sem("w_used")
        w_in = [s.sem(f"w_in{i}") for i in range(RING)]
        mod_summed, mod_done, row_turned = s.sem("mod_summed"), s.sem("mod_done"), s.sem("row_turned")
        row_out, row_stored, plus_one = s.sem("row_out"), s.sem("row_stored"), s.sem("plus_one")
        block = ctx.enter_context(nc.Block())
        w_view = w_ada.rearrange("l (k p) (b n) -> (l p) b k n", p=P, n=NB)
        rounds = NJ * P // NB // RING

        @block.gpsimd
        def _(pool):
            pool.memset(ident[:], 0.0).then_inc(ident_zero, 1)
            pool.wait_ge(ident_zero, 1)
            pool.affine_select(out=ident[:], in_=ident[:], compare_op=ALU.not_equal, fill=1.0, base=0,
                               pattern=[[-1, P]], channel_multiplier=1).then_inc(ident_done, 1)

        @block.sync
        def _(sp):
            sp.dma_start(vec[0:NJ, :], b_ada.rearrange("l (r p) -> (l r) p", p=P)).then_inc(vec_in, 16)
            sp.dma_start(vec[NJ:NJ + KD, :], c.rearrange("b (r p) -> (b r) p", p=P)).then_inc(vec_in, 16)
            sp.dma_start(vec[NJ + KD:VR, :], w_conv.rearrange("l t (r p) -> (l t r) p", p=P)).then_inc(vec_in, 16)
            for i in range(RING):
                sp.dma_start(w[:, i], w_view[:, i]).then_inc(w_in[i], 16)
            with sp.Fori(1, rounds) as r:
                for i in range(RING):
                    sp.wait_ge(w_used, (r - 1) * RING + i + 1)
                    sp.dma_start(w[:, i], w_view[:, bass.ds(r * RING + i, 1)].rearrange("p b k n -> p (b k) n")
                                 ).then_inc(w_in[i], 16)
            sp.wait_ge(row_out, 1)
            sp.dma_start(mod_rows.rearrange("(r p) -> r p", p=P), mod_t[:]).then_inc(row_stored, 16)
            sp.wait_ge(row_stored, 16)

        @block.tensor
        def _(pe):
            pe.wait_ge(vec_in, 48)
            pe.wait_ge(ident_done, 1)
            pe.transpose(p_vec[:, 0:VR], vec[:], ident[0:VR, 0:VR]).then_inc(vec_turned, 1)
            pe.wait_ge(silu_done, 1)
            with pe.Fori(0, rounds) as r:
                for i in range(RING):
                    pe.wait_ge(w_in[i], 16 * r + 16)
                    for m in range(NB // P):
                        out = p_mod[:, bass.ds(r * (RING * NB // P) + (i * (NB // P) + m), 1)]
                        for k in range(KD):
                            mm = pe.matmul(out, w[:, i, k, m * P:(m + 1) * P], csilu[:, k:k + 1],
                                           start=k == 0, stop=k == KD - 1, skip_group_check=True)
                    mm.then_inc(w_used, 1)
            pe.wait_ge(plus_one, 1)
            pe.transpose(p_row[0:NJ, 0:P], mod[:], ident[:]).then_inc(row_turned, 1)

        @block.scalar
        def _(act):
            act.wait_ge(vec_turned, 1)
            act.activation(csilu[:], p_vec[:, NJ:NJ + KD], ACT.Silu).then_inc(silu_done, 1)

        @block.vector
        def _(dve):
            dve.wait_ge(silu_done, 1)
            dve.tensor_copy(cols[:], p_vec[:, 0:VR]).then_inc(cols_out, 1)
            dve.wait_ge(cols_out, 1)
            dve.tensor_copy(conv_cols[:], cols[:, NJ + KD:VR]).then_inc(cols_out, 1)
            dve.wait_ge(w_used, RING * rounds)
            dve.tensor_tensor(mod[:], p_mod[:, 0:NJ], cols[:, 0:NJ], ALU.add).then_inc(mod_done, 1)
            dve.wait_ge(mod_done, 1)
            dve.tensor_scalar(mod[:, SC1:SC1 + KD], mod[:, SC1:SC1 + KD], 1.0, None, ALU.add).then_inc(mod_done, 1)
            dve.wait_ge(mod_done, 2)
            dve.tensor_scalar(mod[:, SC2:SC2 + KD], mod[:, SC2:SC2 + KD], 1.0, None, ALU.add).then_inc(plus_one, 1)
            dve.wait_ge(row_turned, 1)
            dve.tensor_copy(mod_t[:], p_row[0:NJ, 0:P]).then_inc(row_out, 1)


def modulated_input(nc, keep, x, u_hi, u_lo):
    ident, mod = keep["ident"], keep["mod"]
    with ExitStack() as ctx:
        s = Scope(nc, ctx, "u")
        xr = s.sb("x", [P, 2, NB // P, D])
        uf = s.sb("uf", [P, 2, NB])
        p_t = s.ps("p_t", [P, 4, NB])
        x_in = [s.sem(f"x_in{i}") for i in range(2)]
        turned, affine, hi_done, lo_done = (s.sem(n) for n in ("turned", "affine", "hi_done", "lo_done"))
        block = ctx.enter_context(nc.Block())
        x_view = x.rearrange("b (g t p) d -> (b p) g t d", p=P, t=NB // P)

        @block.sync
        def _(sp):
            for g in range(TB):
                if g >= 2:
                    sp.wait_ge(turned, KD * (g - 1))
                sp.dma_start(xr[:, g % 2], x_view[:, g]).then_inc(x_in[g % 2], 16)

        @block.tensor
        def _(pe):
            for g in range(TB):
                pe.wait_ge(x_in[g % 2], 16 * (g // 2 + 1))
                for k in range(KD):
                    n = g * KD + k
                    if n >= 4:
                        pe.wait_ge(affine, n - 3)
                    for t in range(NB // P):
                        mm = pe.transpose(p_t[:, n % 4, t * P:(t + 1) * P], xr[:, g % 2, t, k * P:(k + 1) * P], ident[:])
                    mm.then_inc(turned, 1)

        @block.scalar
        def _(act):
            for n in range(TB * KD):
                k = n % KD
                act.wait_ge(turned, n + 1)
                if n >= 2:
                    act.wait_ge(lo_done, n - 1)
                act.activation(uf[:, n % 2], p_t[:, n % 4], ACT.Identity, bias=mod[:, SH1 + k:SH1 + k + 1],
                               scale=mod[:, SC1 + k:SC1 + k + 1]).then_inc(affine, 1)

        @block.vector
        def _(dve):
            for n in range(TB * KD):
                g, k = divmod(n, KD)
                dve.wait_ge(affine, n + 1)
                dve.tensor_copy(u_hi[:, k, g * NB:(g + 1) * NB], uf[:, n % 2]).then_inc(hi_done, 1)

        @block.gpsimd
        def _(pool):
            for n in range(TB * KD):
                g, k = divmod(n, KD)
                pool.wait_ge(hi_done, n + 1)
                pool.tensor_tensor(u_lo[:, k, g * NB:(g + 1) * NB], uf[:, n % 2],
                                   f32(u_hi[:, k, g * NB:(g + 1) * NB]), ALU.subtract).then_inc(lo_done, 1)


def input_projection(nc, keep, u_hi, u_lo, w_in, qkv_t, conv_t, gate_t):
    conv_cols = keep["conv_cols"]
    with ExitStack() as ctx:
        s = Scope(nc, ctx, "in")
        raw = s.sb("raw", [P, 2, KD, P])
        w_hi = s.sb("w_hi", [P, 2, KD, P], F32R)
        w_lo = s.sb("w_lo", [P, 2, KD, P], F32R)
        stage = s.sb("stage", [P, 2, S])
        cx = s.sb("cx", [P, S])
        gated = s.sb("gated", [P, S + 2])
        conv = s.sb("conv", [P, S])
        acc = s.ps("acc", [P, 2, TB, NB])
        raw_in = [s.sem(f"raw_in{i}") for i in range(2)]
        stored = [s.sem(f"stored{i}") for i in range(2)]
        hi_done, lo_done, pe_done = s.sem("hi_done"), s.sem("lo_done"), s.sem("pe_done")
        act_out, dve_out, conv_step, padded = (s.sem(n) for n in ("act_out", "dve_out", "conv_step", "padded"))
        block = ctx.enter_context(nc.Block())
        w_view = w_in.rearrange("l (k p) n -> (l p) k n", p=P)
        QKV, CONV, GATES = 3 * AW // P, 3 * KC, 2 * D // P
        TILES = QKV + CONV + GATES
        FIRST_G = QKV + CONV
        c_cb, c_cc, c_cx, c_q, c_ga = 0, CH, 2 * CH, 3 * CH, 3 * CH + 3 * AW

        def bank(t):
            return slice(t * NB, (t + 1) * NB)

        @block.sync
        def _(sp):
            def load(col, par, t, first=False):
                if not first:
                    sp.wait_ge(lo_done, t - 1)
                sp.dma_start(raw[:, par], w_view[:, :, bass.ds(col, P)]).then_inc(raw_in[par], 16)

            load(c_q, 0, 0, True)
            load(c_q + P, 1, 1, True)

            def store_qkv(t, par):
                sp.wait_ge(act_out, t + 1)
                sp.wait_ge(dve_out, t + 1)
                sp.dma_start(qkv_t[bass.ds(t * P, P), :], stage[:, par]).then_inc(stored[par], 16)

            with sp.Fori(0, QKV // 2 - 1) as i:
                for par in range(2):
                    t = 2 * i + par
                    load(c_q + (t + 2) * P, par, t + 2)
                    store_qkv(t, par)
            load(c_cx, 0, QKV)
            store_qkv(QKV - 2, 0)
            load(c_cc, 1, QKV + 1)
            store_qkv(QKV - 1, 1)

            def conv_round(j, half, last=False):
                t = QKV + 3 * j
                base = 3 * half
                load(c_cb + j * P, (base + 2) % 2, t + 2)
                nxt = (c_ga, c_ga + P) if last else (c_cx + (j + 1) * P, c_cc + (j + 1) * P)
                load(nxt[0], (base + 3) % 2, t + 3)
                load(nxt[1], (base + 4) % 2, t + 4)
                sp.wait_ge(dve_out, QKV + 2 * j + 2)
                sp.dma_start(conv_t[bass.ds(j * P, P), :], stage[:, half]).then_inc(stored[half], 16)

            with sp.Fori(0, KC // 2 - 1) as i:
                for half in range(2):
                    conv_round(2 * i + half, half)
            conv_round(KC - 2, 0)
            conv_round(KC - 1, 1, last=True)

            def store_gate(n, par):
                sp.wait_ge(act_out, QKV + KC + n + 1)
                sp.dma_start(gate_t[bass.ds(n * P, P), :], stage[:, par]).then_inc(stored[par], 16)

            with sp.Fori(0, GATES // 2 - 1) as i:
                for par in range(2):
                    n = 2 * i + par
                    load(c_ga + (n + 2) * P, par, FIRST_G + n + 2)
                    store_gate(n, par)
            for par in range(2):
                store_gate(GATES - 2 + par, par)
            for par in range(2):
                sp.wait_ge(stored[par], 16 * (QKV + KC + GATES) // 2)

        @block.tensor
        def _(pe):
            def tile(t, par):
                pe.wait_ge(lo_done, t + 1)
                for k in range(KD):
                    for w, us in ((w_hi, (u_hi, u_lo)), (w_lo, (u_hi,))):
                        for n, u in enumerate(us):
                            for tb in range(TB):
                                mm = pe.matmul(acc[:, par, tb], w[:, par, k], u[:, k, bank(tb)],
                                               start=k == 0 and w is w_hi and n == 0,
                                               stop=k == KD - 1 and w is w_lo, skip_group_check=True)
                mm.then_inc(pe_done, 1)

            tile(0, 0)
            tile(1, 1)
            with pe.Fori(1, QKV // 2) as i:
                for par in range(2):
                    pe.wait_ge(act_out, 2 * i + par - 1)
                    pe.wait_ge(dve_out, 2 * i + par - 1)
                    tile(2 * i + par, par)
            with pe.Fori(0, KC // 2) as i:
                for half in range(2):
                    j = 2 * i + half
                    t = QKV + 3 * j
                    pe.wait_ge(act_out, QKV - 1)
                    pe.wait_ge(dve_out, QKV - 1 + 2 * j)
                    tile(t, (3 * half) % 2)
                    pe.wait_ge(act_out, QKV)
                    pe.wait_ge(dve_out, QKV + 2 * j)
                    tile(t + 1, (3 * half + 1) % 2)
                    pe.wait_ge(act_out, QKV + j + 1)
                    tile(t + 2, (3 * half + 2) % 2)
            pe.wait_ge(dve_out, QKV + 2 * KC)
            with pe.Fori(0, GATES // 2) as i:
                for par in range(2):
                    n = 2 * i + par
                    pe.wait_ge(act_out, QKV + KC - 1 + n)
                    tile(FIRST_G + n, par)

        @block.scalar
        def _(act):
            def high(t, par, rnd, first=False):
                act.wait_ge(raw_in[par], 16 * rnd + 16)
                if not first:
                    act.wait_ge(pe_done, t - 1)
                act.activation(w_hi[:, par], raw[:, par], ACT.Copy).then_inc(hi_done, 1)

            def out_qkv(t, par, rnd, first=False):
                act.wait_ge(pe_done, t + 1)
                if not first:
                    act.wait_ge(stored[par], 16 * rnd)
                for tb in range(TB // 2):
                    ins = act.activation(stage[:, par, bank(tb)], acc[:, par, tb], ACT.Copy)
                ins.then_inc(act_out, 1)

            high(0, 0, 0, True)
            high(1, 1, 0, True)
            out_qkv(0, 0, 0, True)
            high(2, 0, 1)
            out_qkv(1, 1, 0, True)
            with act.Fori(1, QKV // 2) as i:
                high(2 * i + 1, 1, i)
                out_qkv(2 * i, 0, i)
                high(2 * i + 2, 0, i + 1)
                out_qkv(2 * i + 1, 1, i)
            with act.Fori(0, KC // 2) as i:
                for half in range(2):
                    j = 2 * i + half
                    t = QKV + 3 * j
                    b = 3 * half
                    rnd = QKV // 2 + 3 * i
                    high(t + 1, (b + 1) % 2, rnd + (b + 1) // 2)
                    act.wait_ge(pe_done, t + 1)
                    act.wait_ge(dve_out, QKV - 1 + 2 * j)
                    for tb in range(TB):
                        ins = act.activation(cx[:, bank(tb)], acc[:, b % 2, tb], ACT.Copy)
                    ins.then_inc(act_out, 1)
                    high(t + 2, (b + 2) % 2, rnd + (b + 2) // 2)
                    high(t + 3, (b + 3) % 2, rnd + (b + 3) // 2)

            def out_gate(n, par, rnd):
                act.wait_ge(pe_done, FIRST_G + n + 1)
                act.wait_ge(stored[par], 16 * (rnd + (QKV + KC) // 2))
                for tb in range(TB):
                    ins = act.activation(stage[:, par, bank(tb)], acc[:, par, tb], ACT.Sigmoid)
                ins.then_inc(act_out, 1)

            with act.Fori(0, GATES // 2 - 1) as i:
                for par in range(2):
                    n = 2 * i + par
                    high(FIRST_G + n + 1, 1 - par, FIRST_G // 2 + i + par)
                    out_gate(n, par, i)
            n = GATES - 2
            high(FIRST_G + n + 1, 1, FIRST_G // 2 + n // 2)
            out_gate(n, 0, n // 2)
            out_gate(n + 1, 1, n // 2)

        @block.vector
        def _(dve):
            dve.memset(gated[:, 0:2], 0.0).then_inc(padded, 1)

            def low(t, par):
                dve.wait_ge(hi_done, t + 1)
                dve.tensor_tensor(w_lo[:, par], raw[:, par], f32(w_hi[:, par]), ALU.subtract).then_inc(lo_done, 1)

            def out_qkv(t, par, rnd, first=False):
                dve.wait_ge(pe_done, t + 1)
                if not first:
                    dve.wait_ge(stored[par], 16 * rnd)
                for tb in range(TB // 2, TB):
                    ins = dve.tensor_copy(stage[:, par, bank(tb)], acc[:, par, tb])
                ins.then_inc(dve_out, 1)

            low(0, 0)
            low(1, 1)
            out_qkv(0, 0, 0, True)
            low(2, 0)
            out_qkv(1, 1, 0, True)
            with dve.Fori(1, QKV // 2) as i:
                low(2 * i + 1, 1)
                out_qkv(2 * i, 0, i)
                low(2 * i + 2, 0)
                out_qkv(2 * i + 1, 1, i)
            dve.wait_ge(padded, 1)
            with dve.Fori(0, KC // 2) as i:
                for half in range(2):
                    j = 2 * i + half
                    t = QKV + 3 * j
                    b = 3 * half
                    low(t + 1, (b + 1) % 2)
                    low(t + 2, (b + 2) % 2)
                    dve.wait_ge(pe_done, t + 2)
                    dve.wait_ge(act_out, QKV + j + 1)
                    for tb in range(TB):
                        ins = dve.tensor_tensor(gated[:, 2 + tb * NB:2 + (tb + 1) * NB], acc[:, (b + 1) % 2, tb],
                                                cx[:, bank(tb)], ALU.mult)
                    ins.then_inc(dve_out, 1)
                    dve.wait_ge(dve_out, QKV + 2 * j + 1)
                    dve.tensor_scalar(conv[:], gated[:, 2:S + 2], conv_cols[:, bass.ds(2 * KC + j, 1)], None,
                                      ALU.mult).then_inc(conv_step, 1)
                    for tap in (1, 0):
                        dve.wait_ge(conv_step, 3 * j + 2 - tap)
                        dve.scalar_tensor_tensor(out=conv[:], in0=gated[:, tap:S + tap],
                                                 scalar=conv_cols[:, bass.ds(tap * KC + j, 1)], in1=conv[:],
                                                 op0=ALU.mult, op1=ALU.add).then_inc(conv_step, 1)
                    low(t + 3, (b + 3) % 2)
                    dve.wait_ge(conv_step, 3 * j + 3)
                    dve.wait_ge(pe_done, t + 3)
                    dve.wait_ge(stored[half], 16 * (QKV // 2 + i))
                    for tb in range(TB):
                        ins = dve.tensor_tensor(stage[:, half, bank(tb)], acc[:, (b + 2) % 2, tb], conv[:, bank(tb)],
                                                ALU.mult)
                    ins.then_inc(dve_out, 1)
            with dve.Fori(0, GATES // 2 - 1) as i:
                for par in range(2):
                    low(FIRST_G + 2 * i + par + 1, 1 - par)
            low(TILES - 1, 1)


def attention(nc, keep, qkv_t, o_t):
    ident, marks = keep["ident"], keep["marks"]
    PAIR = 2 * P
    SCALE = HD ** -0.5
    CHUNKS = [-(-(t + 1) * P // NB) for t in range(NT)]
    CH_BEFORE = [sum(CHUNKS[:t]) for t in range(NT + 1)]
    GROUPS = [-(-(t + 1) // 4) for t in range(NT)]
    GR_BEFORE = [sum(GROUPS[:t]) for t in range(NT + 1)]
    NZ, NTB = CH_BEFORE[NT], GR_BEFORE[NT]
    ZB, TR = 4, 2
    with ExitStack() as ctx:
        s = Scope(nc, ctx, "att")
        q_raw, k_raw = s.sb("q_raw", [P, S]), s.sb("k_raw", [P, S])
        v_raw = s.sb("v_raw", [HD, S])
        q_parts = s.sb("q_parts", [P, S], F32R)
        k_hi, k_lo = s.sb("k_hi", [P, S], F32R), s.sb("k_lo", [P, S], F32R)
        v_parts = s.sb("v_parts", [P, NT, P], F32R)
        rest = s.sb("rest", [P, 2, S + 1])
        wt = s.sb("wt", [P, 2, S])
        wt_hi, wt_lo = s.sb("wt_hi", [P, 2, NT, PAIR], F32R), s.sb("wt_lo", [P, 2, NT, PAIR], F32R)
        mask = s.sb("mask", [P, P], F32R)
        ident_r = s.sb("ident_r", [P, P], F32R)
        mask_f = s.sb("mask_f", [P, P])
        zero = s.sb("zero", [P, 1])
        low_half = s.sb("low_half", [HD, PAIR])
        o_out = s.sb("o_out", [HD, 2, PAIR])
        p_z, p_t, p_o = s.ps("p_z", [P, ZB, NB]), s.ps("p_t", [P, TR, NB]), s.ps("p_o", [P, 2, NB])
        names = ("mask_step", "const_done", "k_hi_done", "k_done", "q_rounded", "q_done", "z_done", "z_used", "rest_done", "scan_done",
                 "weights_done", "wt_used", "turned", "hi_done", "lo_done", "o_done", "o_low", "o_used")
        m = {n: s.sem(n) for n in names}
        raw_in = s.sem("raw_in")
        o_stored = [s.sem(f"o_stored{i}") for i in range(2)]
        block = ctx.enter_context(nc.Block())
        VB = NT // 8
        NR = VB + GR_BEFORE[NT]
        NG = NT // 2

        @block.sync
        def _(sp):
            for i in range(2):
                sp.sem_inc(o_stored[i], 16)

            def load(h):
                for half in range(2):
                    rows = slice(half * HD, (half + 1) * HD)
                    sp.dma_start(q_raw[rows, :], qkv_t[bass.ds(h * HD, HD), :]).then_inc(raw_in, 16)
                    sp.dma_start(k_raw[rows, :], qkv_t[bass.ds(h * HD + AW, HD), :]).then_inc(raw_in, 16)
                sp.dma_start(v_raw[:], qkv_t[bass.ds(h * HD + 2 * AW, HD), :]).then_inc(raw_in, 16)

            def store(h):
                for g in range(NG):
                    sp.wait_ge(m["o_used"], h * NG + g + 3)
                    sp.dma_start(o_t[bass.ds(h * HD, HD), g * PAIR:(g + 1) * PAIR], o_out[:, g % 2]
                                 ).then_inc(o_stored[g % 2], 16)

            load(0)
            with sp.Fori(0, HEADS - 1) as h:
                sp.wait_ge(m["k_done"], h + 1)
                sp.wait_ge(m["q_done"], h + 1)
                sp.wait_ge(m["turned"], h * NR + VB)
                load(h + 1)
                store(h)
            store(HEADS - 1)
            for i in range(2):
                sp.wait_ge(o_stored[i], 16 * (HEADS * NG // 2 + 1))

        @block.gpsimd
        def _(pool):
            pool.memset(mask_f[:], 0.0).then_inc(m["mask_step"], 1)
            pool.wait_ge(m["mask_step"], 1)
            pool.affine_select(out=mask_f[:], in_=mask_f[:], compare_op=ALU.is_gt, fill=-BIG, base=0,
                               pattern=[[-1, P]], channel_multiplier=1).then_inc(m["mask_step"], 1)
            pool.wait_ge(m["mask_step"], 2)
            pool.tensor_copy(mask[:], mask_f[:]).then_inc(m["const_done"], 1)
            pool.tensor_copy(ident_r[:], ident[:]).then_inc(m["const_done"], 1)
            pool.memset(rest[:], 1.0).then_inc(m["const_done"], 1)
            with pool.Fori(0, HEADS) as h:
                pool.wait_ge(raw_in, 80 * h + 80)
                wait_apart(pool, marks["pool"], m["o_done"], h * NG + 2)
                pool.tensor_copy(k_hi[:], k_raw[:]).then_inc(m["k_hi_done"], 1)
                pool.wait_ge(m["k_hi_done"], h + 1)
                pool.tensor_tensor(k_lo[:], k_raw[:], f32(k_hi[:]), ALU.subtract).then_inc(m["k_done"], 1)
                for t in range(NT):
                    w = (t + 1) * P
                    pool.wait_ge(m["z_used"], h * NZ + CH_BEFORE[t + 1] + ZB)
                    pool.wait_ge(m["scan_done"], h * NT + t + 1)
                    pool.tensor_tensor(wt[:, t % 2, 0:w], wt[:, t % 2, 0:w], rest[:, t % 2, 1:w + 1], ALU.mult
                                       ).then_inc(m["weights_done"], 1)

        @block.tensor
        def _(pe):
            pe.sem_inc(m["wt_used"], 2)
            pe.sem_inc(m["o_done"], 2)
            pe.wait_ge(m["const_done"], 3)

            def scores(h, t):
                w = (t + 1) * P
                q = q_parts[:, t * P:(t + 1) * P]
                for c in range(CHUNKS[t]):
                    n = CH_BEFORE[t] + c
                    a, b = c * NB, min(w, (c + 1) * NB)
                    pe.wait_ge(m["z_used"], h * NZ + n + 1)
                    out = p_z[:, n % ZB, 0:b - a]
                    pe.matmul(out, q, k_hi[:, a:b], start=True, stop=False, skip_group_check=True)
                    mm = pe.matmul(out, q, k_lo[:, a:b], start=False, stop=b < w, skip_group_check=True)
                    if b == w:
                        mm = pe.matmul(p_z[:, n % ZB, b - a - P:b - a], ident_r[:], mask[:], start=False, stop=True,
                                       skip_group_check=True)
                    mm.then_inc(m["z_done"], 1)

            def turn_values(h):
                pe.wait_ge(raw_in, 80 * h + 80)
                for n in range(VB):
                    wait_apart(pe, marks["pe"], m["lo_done"], h * NR + n + 1)
                    for j in range(8):
                        mm = pe.transpose(p_t[:, n % TR, j * HD:(j + 1) * HD],
                                          v_raw[:, (8 * n + j) * P:(8 * n + j + 1) * P], ident[0:HD, 0:HD])
                    mm.then_inc(m["turned"], 1)

            def turn(h, t):
                pe.wait_ge(m["weights_done"], h * NT + t + 1)
                for r in range(GROUPS[t]):
                    n = VB + GR_BEFORE[t] + r
                    pe.wait_ge(m["lo_done"], h * NR + n + 1)
                    for j in range(4 * r, min(4 * r + 4, t + 1)):
                        mm = pe.transpose(p_t[:, n % TR, (j - 4 * r) * P:(j - 4 * r + 1) * P],
                                          wt[:, t % 2, j * P:(j + 1) * P], ident[:])
                    mm.then_inc(m["turned"], 1)

            def values(h, g):
                pe.wait_ge(m["lo_done"], h * NR + VB + GR_BEFORE[2 * g + 2] + TR)
                pe.wait_ge(m["o_used"], h * NG + g + 1)
                for j in range(2 * g + 2):
                    first = P if j == 2 * g + 1 else 0
                    for n, part in enumerate((wt_hi, wt_lo)):
                        mm = pe.matmul(p_o[:, g % 2, first:PAIR], v_parts[:, j], part[:, g % 2, j, first:PAIR],
                                       start=j == 0 and n == 0, stop=j == 2 * g + 1 and n == 1, skip_group_check=True)
                mm.then_inc(m["o_done"], 1)

            with pe.Fori(0, HEADS) as h:
                turn_values(h)
                pe.wait_ge(m["k_done"], h + 1)
                pe.wait_ge(m["q_done"], h + 1)
                scores(h, 0)
                scores(h, 1)
                for t in range(NT):
                    if t + 2 < NT:
                        scores(h, t + 2)
                    turn(h, t)
                    if t % 2 == 0 and t:
                        values(h, t // 2 - 1)
                values(h, NG - 1)

        @block.scalar
        def _(act):
            act.sem_inc(m["z_used"], ZB)
            act.wait_ge(m["const_done"], 3)

            def sigmoids(h, t):
                w = (t + 1) * P
                par = t % 2
                if t >= 2:
                    act.wait_ge(m["turned"], h * NR + VB + GR_BEFORE[t - 1])
                for c in range(CHUNKS[t]):
                    n = CH_BEFORE[t] + c
                    a, b = c * NB, min(w, (c + 1) * NB)
                    act.wait_ge(m["z_done"], h * NZ + n + 1)
                    ins = act.activation(rest[:, par, a:b], p_z[:, n % ZB, 0:b - a], ACT.Sigmoid, scale=-SCALE)
                ins.then_inc(m["rest_done"], 1)
                for c in range(CHUNKS[t]):
                    n = CH_BEFORE[t] + c
                    a, b = c * NB, min(w, (c + 1) * NB)
                    act.activation(wt[:, par, a:b], p_z[:, n % ZB, 0:b - a], ACT.Sigmoid, scale=SCALE
                                   ).then_inc(m["z_used"], 1)

            def high(h, t):
                act.wait_ge(m["o_done"], h * NG + t // 2 + 1)
                for r in range(GROUPS[t]):
                    n = VB + GR_BEFORE[t] + r
                    j, k = 4 * r, min(4 * r + 4, t + 1)
                    act.wait_ge(m["turned"], h * NR + n + 1)
                    act.activation(wt_hi[:, t // 2 % 2, j:k, t % 2 * P:(t % 2 + 1) * P],
                                   p_t[:, n % TR, 0:(k - j) * P].rearrange("p (j t) -> p j t", t=P), ACT.Copy
                                   ).then_inc(m["hi_done"], 1)

            with act.Fori(0, HEADS) as h:
                act.wait_ge(raw_in, 80 * h + 80)
                act.wait_ge(m["o_done"], h * NG + 2)
                act.activation(q_parts[:], q_raw[:], ACT.Copy).then_inc(m["q_rounded"], 1)
                for n in range(VB):
                    act.wait_ge(m["turned"], h * NR + n + 1)
                    act.activation(v_parts[:, 8 * n:8 * n + 8, 0:HD], p_t[:, n].rearrange("p (j d) -> p j d", d=HD),
                                   ACT.Copy).then_inc(m["hi_done"], 1)
                sigmoids(h, 0)
                sigmoids(h, 1)
                for t in range(NT):
                    high(h, t)
                    if t + 2 < NT:
                        sigmoids(h, t + 2)

        @block.vector
        def _(dve):
            dve.sem_inc(m["lo_done"], TR)
            dve.sem_inc(m["o_used"], 2)
            dve.memset(zero[:], 0.0).then_inc(m["o_low"], 1)
            dve.wait_ge(m["o_low"], 1)

            def scan(h, t):
                w = (t + 1) * P
                dve.wait_ge(m["rest_done"], h * NT + t + 1)
                r = rest[:, t % 2, 0:w]
                dve.tensor_tensor_scan(r[:, ::-1], r[:, ::-1], zero[:].to_broadcast([P, w]), 1.0, ALU.mult, ALU.max
                                       ).then_inc(m["scan_done"], 1)

            def low(h, t):
                for r in range(GROUPS[t]):
                    n = VB + GR_BEFORE[t] + r
                    j, k = 4 * r, min(4 * r + 4, t + 1)
                    cols = (slice(None), t // 2 % 2, slice(j, k), slice(t % 2 * P, (t % 2 + 1) * P))
                    dve.wait_ge(m["hi_done"], h * NR + n + 1)
                    dve.tensor_tensor(wt_lo[cols], p_t[:, n % TR, 0:(k - j) * P].rearrange("p (j t) -> p j t", t=P),
                                      f32(wt_hi[cols]), ALU.subtract).then_inc(m["lo_done"], 1)

            def output(h, g):
                dve.wait_ge(m["o_done"], h * NG + g + 3)
                dve.tensor_copy(low_half[:], p_o[HD:P, g % 2, 0:PAIR]).then_inc(m["o_low"], 1)
                dve.wait_ge(m["o_low"], h * NG + g + 2)
                dve.wait_ge(o_stored[g % 2], 16 * (h * (NG // 2) + g // 2 + 1))
                dve.tensor_tensor(o_out[:, g % 2], p_o[0:HD, g % 2, 0:PAIR], low_half[:], ALU.add
                                  ).then_inc(m["o_used"], 1)

            with dve.Fori(0, HEADS) as h:
                dve.wait_ge(m["q_rounded"], h + 1)
                dve.tensor_tensor(q_parts[HD:P, :], q_raw[HD:P, :], f32(q_parts[HD:P, :]), ALU.subtract
                                  ).then_inc(m["q_done"], 1)
                for n in range(VB):
                    dve.wait_ge(m["hi_done"], h * NR + n + 1)
                    dve.tensor_tensor(v_parts[:, 8 * n:8 * n + 8, HD:P], p_t[:, n].rearrange("p (j d) -> p j d", d=HD),
                                      f32(v_parts[:, 8 * n:8 * n + 8, 0:HD]), ALU.subtract).then_inc(m["lo_done"], 1)
                scan(h, 0)
                for t in range(NT):
                    if t + 1 < NT:
                        scan(h, t + 1)
                    low(h, t)
                    if t % 2 == 0 and t:
                        output(h, t // 2 - 1)
                output(h, NG - 1)


def branch_outputs(nc, keep, conv_t, o_t, gate_t, w_a, w_b, m_t):
    RB = 4
    with ExitStack() as ctx:
        s = Scope(nc, ctx, "br")
        w_raw = s.sb("w_raw", [P, 2, KC, D])
        w_hi, w_lo = s.sb("w_hi", [P, 2, KC, D], F32R), s.sb("w_lo", [P, 2, KC, D], F32R)
        b_raw = s.sb("b_raw", [P, 2, KC, NB])
        b_hi, b_lo = s.sb("b_hi", [P, 2, KC, NB], F32R), s.sb("b_lo", [P, 2, KC, NB], F32R)
        gates = s.sb("gates", [P, RB, 2, NB])
        prod = s.sb("prod", [P, RB, 2, NB])
        acc = s.ps("acc", [P, RB, 2, NB])
        names = ("w_in", "w_hi_done", "w_lo_done", "b_hi_done", "b_lo_done", "pe_done", "prod_done", "sum_done")
        m = {n: s.sem(n) for n in names}
        b_in = s.sem("b_in")
        g_in = [s.sem(f"g_in{i}") for i in range(RB)]
        stored = [s.sem(f"stored{i}") for i in range(RB)]
        block = ctx.enter_context(nc.Block())
        gate_v = gate_t.rearrange("(b r) t -> r b t", b=2)

        @block.sync
        def _(sp):
            for n, w in enumerate((w_a, w_b)):
                sp.dma_start(w_raw[:, n], w.rearrange("l (k p) n -> (l p) k n", p=P)).then_inc(m["w_in"], 16)
            with sp.Fori(0, TB) as tb:
                sp.wait_ge(m["b_lo_done"], 2 * tb + 2)
                for n, src in enumerate((conv_t, o_t)):
                    sp.dma_start(b_raw[:, n], src.rearrange("(k p) t -> p k t", p=P)[:, :, bass.ds(tb * NB, NB)]
                                 ).then_inc(b_in, 16)
                for d in range(KD):
                    sp.wait_ge(m["prod_done"], 2 * (tb * KD + d) + 2)
                    sp.dma_start(gates[:, d % RB], gate_v[d * P:(d + 1) * P, :, bass.ds(tb * NB, NB)]
                                 ).then_inc(g_in[d % RB], 16)

        @block.tensor
        def _(pe):
            with pe.Fori(0, TB) as tb:
                pe.wait_ge(m["w_lo_done"], 2)
                pe.wait_ge(m["b_lo_done"], 2 * tb + 4)
                for d in range(KD):
                    pe.wait_ge(m["prod_done"], 2 * (tb * KD + d) + 2)
                    for n in range(2):
                        for k in range(KC):
                            cols = slice(d * P, (d + 1) * P)
                            mm = product(pe, acc[:, d % RB, n],
                                         ((w_hi[:, n, k, cols], b_hi[:, n, k]), (w_hi[:, n, k, cols], b_lo[:, n, k]),
                                          (w_lo[:, n, k, cols], b_hi[:, n, k])), k == 0, k == KC - 1)
                    mm.then_inc(m["pe_done"], 1)

        @block.scalar
        def _(act):
            act.wait_ge(m["w_in"], 32)
            for n in range(2):
                act.activation(w_hi[:, n], w_raw[:, n], ACT.Copy).then_inc(m["w_hi_done"], 1)
            act.sem_inc(m["pe_done"], 1)
            with act.Fori(0, TB) as tb:
                act.wait_ge(b_in, 32 * tb + 32)
                act.wait_ge(m["pe_done"], tb * KD + 1)
                for n in range(2):
                    act.activation(b_hi[:, n], b_raw[:, n], ACT.Copy).then_inc(m["b_hi_done"], 1)
                for d in range(KD):
                    act.wait_ge(m["sum_done"], tb * KD + d + 1)
                    act.dma_start(m_t[d * P:(d + 1) * P, bass.ds(tb * NB, NB)], prod[:, d % RB, 0]
                                  ).then_inc(stored[d % RB], 16)
            for i in range(RB):
                act.wait_ge(stored[i], 16 * (TB * KD // RB + 1))

        @block.vector
        def _(dve):
            dve.sem_inc(m["prod_done"], 2 * RB)
            dve.sem_inc(m["b_lo_done"], 2)
            for n in range(2):
                dve.wait_ge(m["w_hi_done"], n + 1)
                dve.tensor_tensor(w_lo[:, n], w_raw[:, n], f32(w_hi[:, n]), ALU.subtract).then_inc(m["w_lo_done"], 1)
            with dve.Fori(0, TB) as tb:
                for n in range(2):
                    dve.wait_ge(m["b_hi_done"], 2 * tb + n + 1)
                    dve.tensor_tensor(b_lo[:, n], b_raw[:, n], f32(b_hi[:, n]), ALU.subtract
                                      ).then_inc(m["b_lo_done"], 1)
                for d in range(KD):
                    u = tb * KD + d
                    dve.wait_ge(m["pe_done"], u + 2)
                    dve.wait_ge(g_in[d % RB], 16 * (tb * (KD // RB) + d // RB + 1))
                    dve.wait_ge(stored[d % RB], 16 * (tb * (KD // RB) + d // RB + 1))
                    for n in range(2):
                        dve.tensor_tensor(prod[:, d % RB, n], acc[:, d % RB, n], gates[:, d % RB, n], ALU.mult
                                          ).then_inc(m["prod_done"], 1)

        @block.gpsimd
        def _(pool):
            for i in range(RB):
                pool.sem_inc(stored[i], 16)
            with pool.Fori(0, TB) as tb:
                for d in range(KD):
                    u = tb * KD + d
                    pool.wait_ge(m["prod_done"], 2 * u + 2 + 2 * RB)
                    pool.tensor_tensor(prod[:, d % RB, 0], prod[:, d % RB, 0], prod[:, d % RB, 1], ALU.add
                                       ).then_inc(m["sum_done"], 1)


class Tile:

    def __init__(self, i, o):
        self.n, self.half, self.quarter = 4 * i + o, 2 * i + o // 2, i + o // 4
        self.s2, self.s4 = o % 2, o % 4
        self.live = not isinstance(i, int) or 0 <= 4 * i + o < NT
        self.i, self.o = i, o

    def __add__(self, k):
        return Tile(self.i, self.o + k)


def pipeline(eng, step, lag):
    for o in range(4):
        step(Tile(0, o))
    with eng.Fori(1, NT // 4 - 1) as i:
        for o in range(4):
            step(Tile(i, o))
    for o in range(4 + lag):
        step(Tile(NT // 4 - 1, o))


class Chain:

    def __init__(self, eng, sem, base):
        self.eng, self.sem, self.base, self.n = eng, sem, base, 0

    def link(self, ins, mark=None):
        self.n += 1
        ins.then_inc(self.sem, 1)
        if mark is None:
            self.eng.wait_ge(self.sem, self.base + self.n)
        else:
            wait_apart(self.eng, mark, self.sem, self.base + self.n)


def mix_norm_route(nc, keep, m_t, w_o, x, mod_rows, ln1_g, ln1_b, w_router, b_router, x1, rows, results):
    ident, dest, gate_w, table, marks = (keep[n] for n in ("ident", "dest", "gate_w", "table", "marks"))
    A_OPS, C_OPS, R1_OPS, R2_OPS = 3, 2, 22, 3
    with ExitStack() as ctx:
        s = Scope(nc, ctx, "mix")
        w_raw = s.sb("w_raw", [P, KD // 2, D])
        w_hi, w_lo = s.sb("w_hi", [P, KD, D], F32R), s.sb("w_lo", [P, KD, D], F32R)
        a_raw = s.sb("a_raw", [P, 2, KD, P])
        a_hi, a_lo = s.sb("a_hi", [P, 2, KD, P], F32R), s.sb("a_lo", [P, 2, KD, P], F32R)
        xt, y, x1t = s.sb("xt", [P, 2, D]), s.sb("y", [P, D]), s.sb("x1t", [P, 2, D])
        u2, u2t = s.sb("u2", [P, 4, D]), s.sb("u2t", [P, KD, P])
        g1r, ln_g, ln_b, sc2r, sh2r = (s.sb(n, [P, D]) for n in ("g1r", "ln_g", "ln_b", "sc2r", "sh2r"))
        wr, br = s.sb("wr", [P, KD, E]), s.sb("br", [P, E])
        stats, mv = s.sb("stats", [P, 2, 6]), s.sb("mv", [P, 2])
        var, rstd, minus_half = s.sb("var", [P, 1]), s.sb("rstd", [P, 1]), s.sb("minus_half", [P, 1])
        tri, ones = s.sb("tri", [P, P]), s.sb("ones", [P, P])
        no_twin = s.sb("no_twin", [P, G, EG, EG])
        down_i, down = s.sb("down_i", [P, E], I32), s.sb("down", [P, E])
        base_i, base = s.sb("base_i", [P, E], I32), s.sb("base", [P, E])
        aff, sel, pairs = s.sb("aff", [P, E]), s.sb("sel", [P, E]), s.sb("pairs", [P, G, EG, EG])
        g_score, g_key, g_off = s.sb("g_score", [P, G]), s.sb("g_key", [P, G]), s.sb("g_off", [P, G])
        top, left, key = s.sb("top", [P, 1]), s.sb("left", [P, 2, E]), s.sb("key", [P, E])
        chosen = s.sb("chosen", [P, 2, 2, E])
        all_chosen = s.sb("all_chosen", [P, NT, 2, E])
        all_at = s.sb("all_at", [P, 2 * NT, E])
        moved = s.sb("moved", [P, 2 * NT])
        all_dest, shift = s.sb("all_dest", [P, 2 * NT]), s.sb("shift", [P, E])
        both, seen = s.sb("both", [P, 2, E]), s.sb("seen", [P, 2, E])
        picked, gates, g_sum = s.sb("picked", [P, 2, E]), s.sb("gates", [P, 2]), s.sb("g_sum", [P, 1])
        place, at, dest_f = s.sb("place", [P, E]), s.sb("at", [P, 2, E]), s.sb("dest_f", [P, 2])
        dest_now = s.sb("dest_now", [P, 2, 2], U32)
        zeros = s.sb("zeros", [P, D])
        n_rows, n_blk, tab_i, tab_f = (s.sb("n_rows", [P, E]), s.sb("n_blk", [P, E], I32), s.sb("tab_i", [P, E], I32),
                                       s.sb("tab_f", [P, E]))
        p_mix, p_t, p_r = s.ps("p_mix", [P, 2, 2, NB]), s.ps("p_t", [P, 2, NB]), s.ps("p_r", [P, 2, NB])
        names = ("const_in", "w_in", "w_hi_done", "w_lo_done", "a_hi_done", "a_lo_done", "mix_done", "mix_used",
                 "a_step", "c_step", "var_done", "var_step", "rstd_done", "x1_done", "u2_step", "u2_done", "turned",
                 "u2t_done", "logits_done", "aff_done", "r1_step", "recip_done", "both_done", "r1_done", "ranked", "rank_used", "r2_step",
                 "dest_done", "const_step", "const_done", "tail_step", "tail_done", "tails_written")
        m = {n: s.sem(n) for n in names}
        a_in = [s.sem(f"a_in{i}") for i in range(2)]
        x_in = [s.sem(f"x_in{i}") for i in range(2)]
        x1_stored = [s.sem(f"x1_stored{i}") for i in range(2)]
        scattered = [s.sem(f"scattered{i}") for i in range(4)]
        block = ctx.enter_context(nc.Block())

        def mod_row(j):
            return mod_rows[j * P:j * P + D].rearrange("(a d) -> a d", a=1).to_broadcast([P, D])


        @block.sync
        def _(sp):
            for i in range(2):
                sp.sem_inc(x1_stored[i], 16)
            w_view = w_o.rearrange("l (k p) n -> (l p) k n", p=P)
            sp.dma_start(w_raw[:], w_view[:, 0:KD // 2]).then_inc(m["w_in"], 16)

            def load_a(t):
                sp.dma_start(a_raw[:, t.s2], m_t.rearrange("(k p) t -> p k t", p=P)[:, :, bass.ds(t.n * P, P)]
                             ).then_inc(a_in[t.s2], 16)

            def load_x(t):
                sp.dma_start(xt[:, t.s2], x.rearrange("b t d -> (b t) d")[bass.ds(t.n * P, P), :]
                             ).then_inc(x_in[t.s2], 16)

            for o in range(2):
                load_a(Tile(0, o))
                load_x(Tile(0, o))
            for dst, src in ((g1r, mod_row(G1)), (sc2r, mod_row(SC2)), (sh2r, mod_row(SH2)),
                             (ln_g, ln1_g.to_broadcast([P, D])), (ln_b, ln1_b.to_broadcast([P, D])),
                             (wr, w_router.rearrange("(k p) e -> p k e", p=P)),
                             (br, b_router.rearrange("(a e) -> a e", a=1).to_broadcast([P, E]))):
                sp.dma_start(dst[:], src).then_inc(m["const_in"], 16)
            sp.wait_ge(m["w_lo_done"], 1)
            sp.dma_start(w_raw[:], w_view[:, KD // 2:KD]).then_inc(m["w_in"], 16)

            def step(t):
                if (t + 2).live:
                    sp.wait_ge(m["a_lo_done"], t.n + 1)
                    load_a(t + 2)
                sp.wait_ge(m["x1_done"], t.n + 1)
                sp.dma_start(x1[bass.ds(t.n * P, P), :], x1t[:, t.s2]).then_inc(x1_stored[t.s2], 16)
                if (t + 2).live:
                    load_x(t + 2)

            pipeline(sp, step, 0)
            for i in range(2):
                sp.wait_ge(x1_stored[i], 16 * (NT // 2 + 1))
            sp.wait_ge(m["tail_done"], 1)
            for e in range(E):
                at_row = sp.value_load(table[0:1, 2, e:e + 1], min_val=e * CAP, max_val=e * CAP + S)
                sp.dma_start(rows[bass.ds(at_row, P), :], zeros[:]).then_inc(m["tails_written"], 16)
            sp.dma_start(rows[E * CAP:E * CAP + P, :], zeros[:]).then_inc(m["tails_written"], 16)
            used = sp.value_load(table[0:1, 1, E - 1:E], min_val=2 * S // P, max_val=BLOCKS - 1)
            with sp.Fori(used, BLOCKS) as b:
                sp.dma_start(results[bass.ds(b * P, P), :], zeros[:]).then_inc(m["tails_written"], 16)
            with sp.Fori(0, used):
                sp.sem_inc(m["tails_written"], 16)
            sp.wait_ge(m["tails_written"], (BLOCKS + E + 1) * 16)

        @block.tensor
        def _(pe):
            pe.sem_inc(m["mix_done"], 2)
            pe.sem_inc(m["logits_done"], 1)
            pe.wait_ge(m["w_lo_done"], 2)
            pe.wait_ge(m["const_done"], 1)
            pe.wait_ge(m["const_in"], 16 * 7)

            def step(t):
                if t.live:
                    pe.wait_ge(m["a_lo_done"], t.n + 1)
                    pe.wait_ge(m["mix_used"], 2 * t.n + 2)
                    for k in range(KD):
                        for n in range(2):
                            w = slice(n * NB, (n + 1) * NB)
                            mm = product(pe, p_mix[:, t.s2, n], ((a_hi[:, t.s2, k], w_hi[:, k, w]),
                                                                 (a_hi[:, t.s2, k], w_lo[:, k, w]),
                                                                 (a_lo[:, t.s2, k], w_hi[:, k, w])), k == 0, k == KD - 1)
                    mm.then_inc(m["mix_done"], 1)
                b = t + -2
                if b.live:
                    pe.wait_ge(m["u2_done"], b.n + 3)
                    pe.wait_ge(m["u2t_done"], b.n + 1)
                    for k in range(KD):
                        mm = pe.transpose(p_t[:, k // 4, k % 4 * P:(k % 4 + 1) * P], u2[:, b.s4, k * P:(k + 1) * P], ident[:])
                    mm.then_inc(m["turned"], 1)
                c = t + -3
                if c.live:
                    pe.wait_ge(m["r1_done"], c.n + 2)
                    pe.wait_ge(m["rank_used"], c.n + 1)
                    pe.matmul(p_r[:, 1, 0:E], tri[:], both[:, c.s2], start=True, stop=False)
                    pe.matmul(p_r[:, 1, 0:E], ones[:], seen[:, c.s2], start=False, stop=True).then_inc(m["ranked"], 1)
                if b.live:
                    pe.wait_ge(m["u2t_done"], b.n + 2)
                    pe.wait_ge(m["aff_done"], b.n + 1)
                    for k in range(KD):
                        mm = pe.matmul(p_r[:, 0, 0:E], u2t[:, k], wr[:, k], start=k == 0, stop=k == KD - 1)
                    mm.then_inc(m["logits_done"], 1)

            pipeline(pe, step, 3)
            pe.wait_ge(m["rank_used"], NT + 1)
            pe.matmul(p_r[:, 1, 0:E], ones[:], seen[:, NT % 2], start=True, stop=True).then_inc(m["ranked"], 1)

        @block.scalar
        def _(act):
            act.sem_inc(m["u2t_done"], 1)
            act.sem_inc(m["aff_done"], 1)

            def high(t):
                act.wait_ge(a_in[t.s2], 16 * t.half + 16)
                act.wait_ge(m["mix_done"], t.n + 1)
                act.activation(a_hi[:, t.s2], a_raw[:, t.s2], ACT.Copy).then_inc(m["a_hi_done"], 1)

            for i in range(2):
                act.wait_ge(m["w_in"], 16 * i + 16)
                act.activation(w_hi[:, i * KD // 2:(i + 1) * KD // 2], w_raw[:], ACT.Copy).then_inc(m["w_hi_done"], 1)
            high(Tile(0, 0))

            def step(t):
                if (t + 1).live:
                    high(t + 1)
                b = t + -2
                if b.live:
                    act.wait_ge(m["turned"], b.n + 1)
                    act.wait_ge(m["logits_done"], b.n + 1)
                    for n in range(2):
                        ins = act.activation(u2t[:, 4 * n:4 * n + 4], p_t[:, n].rearrange("p (k t) -> p k t", t=P), ACT.Copy)
                    ins.then_inc(m["u2t_done"], 1)
                    act.wait_ge(m["logits_done"], b.n + 2)
                    act.wait_ge(m["r1_done"], b.n + 1)
                    act.activation(aff[:], p_r[:, 0, 0:E], ACT.Sigmoid).then_inc(m["aff_done"], 1)

            pipeline(act, step, 2)

        @block.gpsimd
        def _(pool):
            pool.sem_inc(m["u2_done"], 2)
            cs = Chain(pool, m["const_step"], 0)
            cs.link(pool.memset(tri[:], 1.0))
            cs.link(pool.affine_select(out=tri[:], in_=tri[:], compare_op=ALU.is_gt, fill=0.0, base=0,
                                       pattern=[[1, P]], channel_multiplier=-1))
            cs.link(pool.memset(ones[:], 1.0))
            cs.link(pool.memset(minus_half[:], -0.5))
            cs.link(pool.memset(no_twin[:], 0.0))
            cs.link(pool.affine_select(out=no_twin[:], in_=no_twin[:], compare_op=ALU.not_equal, fill=-BIG, base=0,
                                       pattern=[[0, G], [1, EG], [-1, EG]], channel_multiplier=0))
            cs.link(pool.iota(down_i[:], pattern=[[-1, E]], base=E, channel_multiplier=0))
            cs.link(pool.tensor_copy(down[:], down_i[:]))
            cs.link(pool.iota(base_i[:], pattern=[[CAP, E]], base=0, channel_multiplier=0))
            cs.link(pool.tensor_copy(base[:], base_i[:]))
            cs.link(pool.memset(zeros[:], 0.0))
            pool.memset(seen[:], 0.0).then_inc(m["const_done"], 1)

            def low(t):
                pool.wait_ge(m["a_hi_done"], t.n + 1)
                pool.tensor_tensor(a_lo[:, t.s2], a_raw[:, t.s2], f32(a_hi[:, t.s2]), ALU.subtract
                                   ).then_inc(m["a_lo_done"], 1)

            low(Tile(0, 0))

            def step(t):
                if (t + 1).live:
                    low(t + 1)
                if t.live:
                    wait_apart(pool, marks["pool"], m["var_done"], t.n + 1)
                    pool.tensor_scalar(var[:], mv[:, 1:2], EPS, None, ALU.add).then_inc(m["var_step"], 1)
                    pool.wait_ge(m["var_step"], t.n + 1)
                    pool.tensor_tensor(rstd[:], var[:], minus_half[:], ALU.pow).then_inc(m["rstd_done"], 1)
                c = t + -3
                if c.live:
                    wait_apart(pool, marks["pool"], m["dest_done"], c.n + 1)
                    for k in range(2):
                        pool.indirect_dma_start(out=rows, out_offset=bass.IndirectOffsetOnAxis(
                            ap=dest_now[:, c.s2, k:k + 1], axis=0), in_=u2[:, c.s4], in_offset=None
                        ).then_inc(scattered[c.s4], 16)
                if t.live:
                    pool.wait_ge(m["x1_done"], t.n + 1)
                    if (t + -4).live:
                        pool.wait_ge(scattered[t.s4], 32 * t.quarter)
                    pool.tensor_tensor(u2[:, t.s4], x1t[:, t.s2], sc2r[:], ALU.mult).then_inc(m["u2_step"], 1)
                    pool.wait_ge(m["u2_step"], t.n + 1)
                    pool.tensor_tensor(u2[:, t.s4], u2[:, t.s4], sh2r[:], ALU.add).then_inc(m["u2_done"], 1)

            pool.wait_ge(m["const_in"], 16 * 7)
            pipeline(pool, step, 3)
            for i in range(4):
                pool.wait_ge(scattered[i], 32 * (NT // 4))

        @block.vector
        def _(dve):
            dve.sem_inc(m["mix_used"], 4)
            dve.sem_inc(m["r1_done"], 1)
            dve.sem_inc(m["rank_used"], 1)
            for i in range(2):
                dve.wait_ge(m["w_hi_done"], i + 1)
                part = (slice(None), slice(i * KD // 2, (i + 1) * KD // 2))
                dve.tensor_tensor(w_lo[part], w_raw[:], f32(w_hi[part]), ALU.subtract).then_inc(m["w_lo_done"], 1)
            dve.wait_ge(m["const_in"], 16 * 7)
            dve.wait_ge(m["const_done"], 1)

            def norm(t):
                ch = Chain(dve, m["a_step"], A_OPS * t.n)
                dve.wait_ge(m["mix_done"], t.n + 3)
                for n in range(2):
                    w = slice(n * NB, (n + 1) * NB)
                    dve.tensor_tensor(y[:, w], p_mix[:, t.s2, n], g1r[:, w], ALU.mult).then_inc(m["mix_used"], 1)
                dve.wait_ge(m["mix_used"], 2 * t.n + 6)
                dve.wait_ge(x_in[t.s2], 16 * t.half + 16)
                ch.link(dve.scalar_tensor_tensor(out=y[:], in0=xt[:, t.s2], scalar=ALPHA, in1=y[:], op0=ALU.mult, op1=ALU.add))
                for n in range(2):
                    ch.link(dve.bn_stats(stats[:, n], y[:, n * NB:(n + 1) * NB]), mark=marks["dve"] if n == 1 else None)
                dve.bn_aggr(mv[:], stats[:].rearrange("p a b -> p (a b)")).then_inc(m["var_done"], 1)

            def affine(t):
                ch = Chain(dve, m["c_step"], C_OPS * t.n)
                dve.wait_ge(m["rstd_done"], t.n + 1)
                dve.wait_ge(m["var_done"], t.n + 1)
                dve.wait_ge(x1_stored[t.s2], 16 * t.half + 16)
                dve.wait_ge(m["u2_done"], t.n + 1)
                ch.link(dve.tensor_scalar(x1t[:, t.s2], y[:], mv[:, 0:1], rstd[:], ALU.subtract, ALU.mult))
                ch.link(dve.tensor_tensor(x1t[:, t.s2], x1t[:, t.s2], ln_g[:], ALU.mult))
                dve.tensor_tensor(x1t[:, t.s2], x1t[:, t.s2], ln_b[:], ALU.add).then_inc(m["x1_done"], 1)

            def choose(t):
                ch = Chain(dve, m["r1_step"], R1_OPS * t.n)
                dve.wait_ge(m["aff_done"], t.n + 2)
                ch.link(dve.tensor_tensor(sel[:], aff[:], br[:], ALU.add))
                by_group = sel[:].rearrange("p (g e) -> p g e", g=G)
                ch.link(dve.tensor_tensor(pairs[:], by_group.unsqueeze(3).to_broadcast([P, G, EG, EG]),
                                          by_group.unsqueeze(2).to_broadcast([P, G, EG, EG]), ALU.add))
                ch.link(dve.tensor_tensor(pairs[:], pairs[:], no_twin[:], ALU.add))
                ch.link(dve.tensor_reduce(g_score[:], pairs[:].rearrange("p g a b -> p g (a b)"), AX.X, ALU.max))
                ch.link(dve.tensor_reduce(top[:], g_score[:], AX.X, ALU.max))
                ch.link(dve.scalar_tensor_tensor(out=g_key[:], in0=g_score[:], scalar=top[:], in1=down[:, 0:G],
                                                 op0=ALU.is_ge, op1=ALU.mult))
                ch.link(dve.tensor_reduce(top[:], g_key[:], AX.X, ALU.max))
                ch.link(dve.tensor_scalar(g_off[:], g_key[:], top[:], -BIG, ALU.not_equal, ALU.mult))
                ch.link(dve.tensor_tensor(left[:, 0].rearrange("p (g e) -> p g e", g=G), by_group,
                                          g_off[:].unsqueeze(2).to_broadcast([P, G, EG]), ALU.add))
                for n in range(2):
                    hot = chosen[:, t.s2, n]
                    ch.link(dve.tensor_reduce(top[:], left[:, n], AX.X, ALU.max))
                    ch.link(dve.scalar_tensor_tensor(out=key[:], in0=left[:, n], scalar=top[:], in1=down[:],
                                                     op0=ALU.is_ge, op1=ALU.mult))
                    ch.link(dve.tensor_reduce(top[:], key[:], AX.X, ALU.max))
                    ch.link(dve.tensor_scalar(hot, key[:], top[:], None, ALU.is_equal))
                    if n == 0:
                        ch.link(dve.scalar_tensor_tensor(out=left[:, 1], in0=hot, scalar=-2 * BIG, in1=left[:, 0],
                                                         op0=ALU.mult, op1=ALU.add))
                hots = chosen[:, t.s2]
                ch.link(dve.tensor_tensor(picked[:], hots, aff[:].unsqueeze(1).to_broadcast([P, 2, E]), ALU.mult))
                ch.link(dve.tensor_reduce(gates[:], picked[:], AX.X, ALU.add))
                ch.link(dve.tensor_reduce(g_sum[:], gates[:], AX.X, ALU.add))
                ch.link(dve.tensor_copy(all_chosen[:, bass.ds(t.n, 1)].rearrange("p a n e -> p (a n) e"), hots))
                assert ch.n == R1_OPS, ch.n
                dve.reciprocal(g_sum[:], g_sum[:]).then_inc(m["recip_done"], 1)
                dve.wait_ge(m["recip_done"], t.n + 1)
                dve.tensor_scalar(gate_w[:, bass.ds(2 * t.n, 2)], gates[:], g_sum[:], None, ALU.mult)
                dve.tensor_tensor(both[:, t.s2], hots[:, 0], hots[:, 1], ALU.add).then_inc(m["both_done"], 1)
                dve.wait_ge(m["both_done"], t.n + 1)
                dve.tensor_tensor(seen[:, 1 - t.s2], seen[:, t.s2], both[:, t.s2], ALU.add).then_inc(m["r1_done"], 1)

            def put(t):
                ch = Chain(dve, m["r2_step"], R2_OPS * t.n)
                dve.wait_ge(m["ranked"], t.n + 1)
                dve.tensor_tensor(place[:], p_r[:, 1, 0:E], base[:], ALU.add).then_inc(m["rank_used"], 1)
                dve.wait_ge(m["rank_used"], t.n + 2)
                ch.link(dve.tensor_tensor(at[:], chosen[:, t.s2], place[:].unsqueeze(1).to_broadcast([P, 2, E]), ALU.mult))
                ch.link(dve.tensor_reduce(dest_f[:], at[:], AX.X, ALU.add))
                if (t + -2).live:
                    dve.wait_ge(scattered[(t + -2).s4], 32 * (t + -2).quarter + 32)
                ch.link(dve.tensor_copy(all_dest[:, bass.ds(2 * t.n, 2)], dest_f[:]))
                dve.tensor_copy(dest_now[:, t.s2], dest_f[:]).then_inc(m["dest_done"], 1)

            def step(t):
                if t.live:
                    norm(t)
                if (t + -2).live:
                    choose(t + -2)
                if (t + -3).live:
                    put(t + -3)
                if t.live:
                    affine(t)

            pipeline(dve, step, 3)
            ch = Chain(dve, m["tail_step"], 0)
            dve.wait_ge(m["ranked"], NT + 1)
            ch.link(dve.tensor_copy(n_rows[:], p_r[:, 1, 0:E]))
            ch.link(dve.tensor_tensor(tab_f[:], n_rows[:], base[:], ALU.add))
            ch.link(dve.tensor_copy(table[:, 2], tab_f[:]))
            ch.link(dve.tensor_scalar(tab_f[:], n_rows[:], float(P - 1), None, ALU.add))
            ch.link(dve.tensor_copy(tab_i[:], tab_f[:]))
            ch.link(dve.tensor_scalar(n_blk[:], tab_i[:], 7, None, ALU.logical_shift_right))
            ch.link(dve.tensor_copy(n_rows[:], n_blk[:]))
            ch.link(dve.tensor_tensor_scan(tab_f[:], ones[:, 0:E], n_rows[:], 0.0, ALU.mult, ALU.add))
            ch.link(dve.tensor_copy(table[:, 1], tab_f[:]))
            ch.link(dve.tensor_tensor(n_rows[:], tab_f[:], n_rows[:], ALU.subtract))
            ch.link(dve.tensor_copy(table[:, 0], n_rows[:]))
            ch.link(dve.scalar_tensor_tensor(out=shift[:], in0=n_rows[:], scalar=float(P), in1=base[:], op0=ALU.mult,
                                             op1=ALU.subtract))
            ch.link(dve.tensor_tensor(all_at[:], all_chosen[:].rearrange("p t n e -> p (t n) e"),
                                      shift[:].unsqueeze(1).to_broadcast([P, 2 * NT, E]), ALU.mult))
            ch.link(dve.tensor_reduce(moved[:], all_at[:], AX.X, ALU.add))
            dve.tensor_tensor(dest[:], all_dest[:], moved[:], ALU.add).then_inc(m["tail_done"], 1)


def experts(nc, keep, w_gate, w_up, w_down, rows, results):
    ident, table, marks = keep["ident"], keep["table"], keep["marks"]
    PIECES = ((0, KD // 2), (KD // 2, KD))
    CHUNKS = KD + KF
    with ExitStack() as ctx:
        s = Scope(nc, ctx, "moe")
        gu_raw, dn_raw = s.sb("gu_raw", [P, KD, 2, FF]), s.sb("dn_raw", [P, KF, D])
        gu_hi, gu_lo = s.sb("gu_hi", [P, KD, 2, FF], F32R), s.sb("gu_lo", [P, KD, 2, FF], F32R)
        dn_hi, dn_lo = s.sb("dn_hi", [P, KF, D], F32R), s.sb("dn_lo", [P, KF, D], F32R)
        x_raw = s.sb("x_raw", [P, D])
        x_hi, x_lo = s.sb("x_hi", [P, KD, P], F32R), s.sb("x_lo", [P, KD, P], F32R)
        act_g, h = s.sb("act_g", [P, FF]), s.sb("h", [P, FF])
        h_hi, h_lo = s.sb("h_hi", [P, KF, P], F32R), s.sb("h_lo", [P, KF, P], F32R)
        y = s.sb("y", [P, D])
        p_gu, p_y = s.ps("p_gu", [P, 2, FF]), s.ps("p_y", [P, 2, NB])
        p_x, p_h = s.ps("p_x", [P, 2, NB]), s.ps("p_h", [P, 2, NB])
        names = ("hi_done", "lo_done", "x_in", "x_turned", "x_hi_done", "x_lo_done", "gu_used", "dn_used", "gu_done",
                 "silu_done", "h_done", "h_turned", "h_hi_done", "h_lo_done", "y_done", "y_out", "y_stored")
        m = {n: s.sem(n) for n in names}
        piece_in = [s.sem(f"piece_in{i}") for i in range(3)]
        block = ctx.enter_context(nc.Block())

        def span(eng, e):
            first = eng.value_load(table[0:1, 0, bass.ds(e, 1)], min_val=0, max_val=BLOCKS)
            end = eng.value_load(table[0:1, 1, bass.ds(e, 1)], min_val=0, max_val=BLOCKS)
            return first, end

        def chunk(c):
            if c < KD:
                return tuple(w[:, c].rearrange("p g f -> p (g f)") for w in (gu_raw, gu_hi, gu_lo))
            return tuple(w[:, c - KD] for w in (dn_raw, dn_hi, dn_lo))

        def row_of(shifted):
            return nc.s_assert_within(shifted - BLOCKS * P, 0, E * CAP, skip_runtime_bounds_check_because=
                                      "a block of an expert lies in the expert's region")

        def split_free(eng, first, c):
            if c < KD:
                wait_apart(eng, marks["pool"], m["gu_used"], first * KD + (c + 1))
            else:
                wait_apart(eng, marks["pool"], m["dn_used"], first * KF + (c - KD + 1))

        @block.sync
        def _(sp):
            def load_weights(e, first=False):
                for i, (a, b) in enumerate(PIECES):
                    if not first:
                        sp.wait_ge(m["lo_done"], (e - 1) * CHUNKS + b)
                    for g, w in enumerate((w_gate, w_up)):
                        sp.dma_start(gu_raw[:, a:b, g], w.rearrange("l e (k p) f -> (l e) p k f", p=P)[
                            bass.ds(e, 1), :, a:b].rearrange("e p k f -> p (e k) f")).then_inc(piece_in[i], 16)
                if not first:
                    sp.wait_ge(m["lo_done"], e * CHUNKS)
                sp.dma_start(dn_raw[:], w_down.rearrange("l e (k p) d -> (l e) p k d", p=P)[
                    bass.ds(e, 1)].rearrange("e p k d -> p (e k) d")).then_inc(piece_in[2], 16)

            def load_x(b, row):
                wait_apart(sp, marks["sp"], m["x_turned"], b + 1)
                sp.dma_start(x_raw[:], rows[bass.ds(row, P), :]).then_inc(m["x_in"], 16)

            def load_blocks(e, last=False):
                first, end = span(sp, e)
                shift = sp.snap(e * CAP - first * P + BLOCKS * P)
                

                def row(b):
                    return row_of(sp.snap(b * P + shift))

                with sp.If(end > first):
                    load_x(first, row(first))
                with sp.If(end > first + 1):
                    load_x(first + 1, row(first + 1))
                if not last:
                    load_weights(e + 1)
                with sp.If(end > first + 2):
                    with sp.Fori(first + 2, end) as b:
                        load_x(b, row(b))
                return end

            load_weights(0, True)
            with sp.Fori(0, E - 1) as e:
                load_blocks(e)
            end = load_blocks(E - 1, last=True)
            load_x(end, E * CAP)

        @block.tensor
        def _(pe):
            pe.sem_inc(m["gu_used"], KD)
            pe.sem_inc(m["dn_used"], KF)
            pe.sem_inc(m["x_turned"], 1)

            def turn_x(b):
                pe.wait_ge(m["x_in"], 16 * b + 16)
                for k in range(KD):
                    mm = pe.transpose(p_x[:, k // 4, k % 4 * P:(k % 4 + 1) * P], x_raw[:, k * P:(k + 1) * P], ident[:])
                mm.then_inc(m["x_turned"], 1)

            turn_x(0)
            with pe.Fori(0, E) as e:
                first, end = span(pe, e)
                with pe.If(end > first):
                    with pe.Fori(first, end) as b:
                        pe.wait_ge(m["x_lo_done"], b + 1)
                        for k in range(KD):
                            pe.wait_ge(m["lo_done"], e * CHUNKS + (k + 1))
                            for g in range(2):
                                mm = product(pe, p_gu[:, g], ((x_hi[:, k], gu_hi[:, k, g]), (x_hi[:, k], gu_lo[:, k, g]),
                                                              (x_lo[:, k], gu_hi[:, k, g])), k == 0, k == KD - 1)
                            mm.then_inc(m["gu_used"], 1)
                        turn_x(b + 1)
                        for i in range(2):
                            pe.wait_ge(m["h_done"], 2 * b + (i + 1))
                            for j in range(2):
                                f = 2 * i + j
                                mm = pe.transpose(p_h[:, i, j * P:(j + 1) * P], h[:, f * P:(f + 1) * P], ident[:])
                            mm.then_inc(m["h_turned"], 1)
                        pe.wait_ge(m["y_out"], 2 * b + 2)
                        for k in range(KF):
                            pe.wait_ge(m["h_lo_done"], 2 * b + (k // 2 + 1))
                            pe.wait_ge(m["lo_done"], e * CHUNKS + (KD + k + 1))
                            for n in range(2):
                                w = slice(n * NB, (n + 1) * NB)
                                mm = product(pe, p_y[:, n], ((h_hi[:, k], dn_hi[:, k, w]), (h_hi[:, k], dn_lo[:, k, w]),
                                                             (h_lo[:, k], dn_hi[:, k, w])), k == 0, k == KF - 1)
                            mm.then_inc(m["dn_used"], 1)

        @block.scalar
        def _(act):
            act.sem_inc(m["y_out"], 2)
            act.sem_inc(m["y_stored"], 16)

            def high_x(b):
                act.wait_ge(m["x_turned"], b + 2)
                for n in range(2):
                    act.activation(x_hi[:, 4 * n:4 * n + 4], p_x[:, n].rearrange("p (k t) -> p k t", t=P), ACT.Copy
                                   ).then_inc(m["x_hi_done"], 1)

            high_x(0)
            with act.Fori(0, E) as e:
                first, end = span(act, e)
                with act.If(end > first):
                    with act.Fori(first, end) as b:
                        act.wait_ge(m["gu_used"], b * KD + 2 * KD)
                        for i in range(2):
                            act.activation(act_g[:, i * 256:(i + 1) * 256], p_gu[:, 0, i * 256:(i + 1) * 256], ACT.Silu
                                           ).then_inc(m["silu_done"], 1)
                        for i in range(2):
                            act.wait_ge(m["h_turned"], 2 * b + (i + 1))
                            act.activation(h_hi[:, 2 * i:2 * i + 2], p_h[:, i, 0:2 * P].rearrange("p (k t) -> p k t", t=P),
                                           ACT.Copy).then_inc(m["h_hi_done"], 1)
                        high_x(b + 1)
                        act.wait_ge(m["dn_used"], b * KF + 2 * KF)
                        act.wait_ge(m["y_stored"], 16 * b + 16)
                        for n in range(2):
                            act.activation(y[:, n * NB:(n + 1) * NB], p_y[:, n], ACT.Copy).then_inc(m["y_out"], 1)
                        act.wait_ge(m["y_out"], 2 * b + 4)
                        act.dma_start(results[bass.ds(b * P, P), :], y[:]).then_inc(m["y_stored"], 16)
            total = act.value_load(table[0:1, 1, E - 1:E], min_val=0, max_val=BLOCKS)
            wait_apart(act, marks["act"], m["y_stored"], total * 16 + 16)

        @block.gpsimd
        def _(pool):
            with pool.Fori(0, E) as e:
                first, end = span(pool, e)
                for c in range(CHUNKS):
                    raw, hi, lo = chunk(c)
                    if c in (0, KD // 2):
                        pool.wait_ge(piece_in[c // (KD // 2)], 32 * e + 32)
                    if c == KD:
                        pool.wait_ge(piece_in[2], 16 * e + 16)
                    split_free(pool, first, c)
                    pool.tensor_copy(hi, raw).then_inc(m["hi_done"], 1)

        @block.vector
        def _(dve):
            def low_x(b):
                for n in range(2):
                    dve.wait_ge(m["x_hi_done"], 2 * b + (n + 1))
                    part = (slice(None), slice(4 * n, 4 * n + 4))
                    ins = dve.tensor_tensor(x_lo[part], p_x[:, n].rearrange("p (k t) -> p k t", t=P), f32(x_hi[part]),
                                            ALU.subtract)
                ins.then_inc(m["x_lo_done"], 1)

            low_x(0)
            with dve.Fori(0, E) as e:
                first, end = span(dve, e)
                for c in range(CHUNKS):
                    raw, hi, lo = chunk(c)
                    dve.wait_ge(m["hi_done"], e * CHUNKS + (c + 1))
                    dve.tensor_tensor(lo, raw, f32(hi), ALU.subtract).then_inc(m["lo_done"], 1)
                with dve.If(end > first):
                    with dve.Fori(first, end) as b:
                        for i in range(2):
                            w = slice(i * 256, (i + 1) * 256)
                            dve.wait_ge(m["silu_done"], 2 * b + (i + 1))
                            dve.tensor_tensor(h[:, w], p_gu[:, 1, w], act_g[:, w], ALU.mult).then_inc(m["h_done"], 1)
                        for i in range(2):
                            part = (slice(None), slice(2 * i, 2 * i + 2))
                            dve.wait_ge(m["h_hi_done"], 2 * b + (i + 1))
                            dve.tensor_tensor(h_lo[part], p_h[:, i, 0:2 * P].rearrange("p (k t) -> p k t", t=P),
                                              f32(h_hi[part]), ALU.subtract).then_inc(m["h_lo_done"], 1)
                        low_x(b + 1)


def combine_norm(nc, keep, results, x1, mod_rows, ln2_g, ln2_b, out):
    dest, gate_w, marks = keep["dest"], keep["gate_w"], keep["marks"]
    A_OPS = 5
    with ExitStack() as ctx:
        s = Scope(nc, ctx, "fin")
        g2r, ln_g, ln_b = (s.sb(n, [P, D]) for n in ("g2r", "ln_g", "ln_b"))
        idx = s.sb("idx", [P, 2, 2], U32)
        yy, xt = s.sb("yy", [P, 2, 2, D]), s.sb("xt", [P, 2, D])
        first, y, res = s.sb("first", [P, 2, D]), s.sb("y", [P, 2, D]), s.sb("res", [P, 2, D])
        stats, mv, var, rstd = s.sb("stats", [P, 2, 6]), s.sb("mv", [P, 2]), s.sb("var", [P, 1]), s.sb("rstd", [P, 1])
        minus_half = s.sb("minus_half", [P, 1])
        names = ("const_in", "half_set", "idx_done", "first_done", "a_step", "var_done", "var_step", "rstd_done",
                 "normed", "scaled", "res_done")
        m = {n: s.sem(n) for n in names}
        y_in, x_in, stored = ([s.sem(f"{n}{i}") for i in range(2)] for n in ("y_in", "x_in", "stored"))
        block = ctx.enter_context(nc.Block())

        @block.sync
        def _(sp):
            for dst, src in ((g2r, mod_rows[G2 * P:G2 * P + D].rearrange("(a d) -> a d", a=1).to_broadcast([P, D])),
                             (ln_g, ln2_g.to_broadcast([P, D])), (ln_b, ln2_b.to_broadcast([P, D]))):
                sp.dma_start(dst[:], src).then_inc(m["const_in"], 16)

            with sp.Fori(0, NT // 2) as i:
                for par in range(2):
                    t = 2 * i + par
                    sp.wait_ge(m["normed"], t + 1)
                    sp.dma_start(xt[:, par], x1[bass.ds(t * P, P), :]).then_inc(x_in[par], 16)

        @block.gpsimd
        def _(pool):
            pool.memset(minus_half[:], -0.5).then_inc(m["half_set"], 1)
            pool.wait_ge(m["const_in"], 48)
            pool.wait_ge(m["half_set"], 1)

            def gather(t, par):
                wait_apart(pool, marks["pool"], m["normed"], t + 1)
                pool.tensor_copy(idx[:, par], dest[:, bass.ds(2 * t, 2)]).then_inc(m["idx_done"], 1)
                wait_apart(pool, marks["pool"], m["idx_done"], t + 1)
                for k in range(2):
                    pool.indirect_dma_start(out=yy[:, par, k], out_offset=None, in_=results, in_offset=bass.IndirectOffsetOnAxis(
                        ap=idx[:, par, k:k + 1], axis=0)).then_inc(y_in[par], 16)

            def finish(t, par):
                wait_apart(pool, marks["pool"], m["var_done"], t + 1)
                pool.tensor_scalar(var[:], mv[:, 1:2], EPS, None, ALU.add).then_inc(m["var_step"], 1)
                pool.wait_ge(m["var_step"], t + 1)
                pool.tensor_tensor(rstd[:], var[:], minus_half[:], ALU.pow).then_inc(m["rstd_done"], 1)
                pool.wait_ge(m["normed"], t + 3)
                pool.tensor_tensor(res[:, par], y[:, par], ln_g[:], ALU.mult).then_inc(m["scaled"], 1)
                pool.wait_ge(m["scaled"], t + 1)
                pool.tensor_tensor(res[:, par], res[:, par], ln_b[:], ALU.add).then_inc(m["res_done"], 1)

            gather(0, 0)
            gather(1, 1)
            with pool.Fori(0, NT // 2 - 1) as i:
                for par in range(2):
                    finish(2 * i + par, par)
                    gather(2 * i + par + 2, par)
            for par in range(2):
                finish(NT - 2 + par, par)

        @block.scalar
        def _(act):
            for i in range(2):
                act.sem_inc(stored[i], 16)

            def weigh(t, par, i):
                act.wait_ge(y_in[par], 32 * i + 32)
                act.wait_ge(m["normed"], t + 1)
                act.activation(first[:, par], yy[:, par, 0], ACT.Copy, scale=gate_w[:, bass.ds(2 * t, 1)]
                               ).then_inc(m["first_done"], 1)

            def store(t, par):
                act.wait_ge(m["res_done"], t + 1)
                act.dma_start(out.rearrange("b t d -> (b t) d")[bass.ds(t * P, P), :], res[:, par]
                              ).then_inc(stored[par], 16)

            weigh(0, 0, 0)
            with act.Fori(0, NT // 2 - 1) as i:
                weigh(2 * i + 1, 1, i)
                store(2 * i, 0)
                weigh(2 * i + 2, 0, i + 1)
                store(2 * i + 1, 1)
            weigh(NT - 1, 1, NT // 2 - 1)
            store(NT - 2, 0)
            store(NT - 1, 1)
            for i in range(2):
                act.wait_ge(stored[i], 16 * (NT // 2 + 1))

        @block.vector
        def _(dve):
            dve.sem_inc(m["normed"], 2)
            dve.wait_ge(m["const_in"], 48)
            with dve.Fori(0, NT // 2) as i:
                for par in range(2):
                    t = 2 * i + par
                    ch = Chain(dve, m["a_step"], A_OPS * t)
                    dve.wait_ge(m["first_done"], t + 1)
                    dve.wait_ge(x_in[par], 16 * i + 16)
                    dve.wait_ge(stored[par], 16 * i + 16)
                    ch.link(dve.scalar_tensor_tensor(out=y[:, par], in0=yy[:, par, 1], scalar=gate_w[:, bass.ds(2 * t + 1, 1)],
                                                     in1=first[:, par], op0=ALU.mult, op1=ALU.add))
                    ch.link(dve.tensor_tensor(y[:, par], y[:, par], g2r[:], ALU.mult))
                    ch.link(dve.scalar_tensor_tensor(out=y[:, par], in0=xt[:, par], scalar=ALPHA, in1=y[:, par],
                                                     op0=ALU.mult, op1=ALU.add))
                    for n in range(2):
                        ch.link(dve.bn_stats(stats[:, n], y[:, par, n * NB:(n + 1) * NB]), mark=marks["dve"] if n == 1 else None)
                    dve.bn_aggr(mv[:], stats[:].rearrange("p a b -> p (a b)")).then_inc(m["var_done"], 1)
                    dve.wait_ge(m["var_done"], t + 1)
                    dve.wait_ge(m["rstd_done"], t + 1)
                    dve.tensor_scalar(y[:, par], y[:, par], mv[:, 0:1], rstd[:], ALU.subtract, ALU.mult
                                      ).then_inc(m["normed"], 1)


def hybrid_layer(nc, x, c, w_ada, b_ada, w_in, w_conv, w_a, w_b, w_o, ln1_g, ln1_b, w_router, b_router, w_gate, w_up,
                 w_down, ln2_g, ln2_b, out):
    def scratch(name, shape):
        return nc.dram_tensor(name, shape, F32, kind="Internal").ap()

    mod_rows = scratch("mod_rows", [6 * D])
    qkv_t, conv_t, gate_t = scratch("qkv_t", [3 * AW, S]), scratch("conv_t", [CH, S]), scratch("gate_t", [2 * D, S])
    o_t, m_t, x1 = scratch("o_t", [AW, S]), scratch("m_t", [D, S]), scratch("x1", [S, D])
    rows, results = scratch("rows", [E * CAP + P, D]), scratch("results", [BLOCKS * P, D])
    with ExitStack() as ctx:
        s = Scope(nc, ctx, "keep")
        keep = {
            "ident": s.sb("ident", [P, P]), "mod": s.sb("mod", [P, 6 * KD]), "conv_cols": s.sb("conv_cols", [P, 3 * KC]),
            "dest": s.sb("dest", [P, 2 * NT], U32), "gate_w": s.sb("gate_w", [P, 2 * NT]),
            "table": s.sb("table", [P, 3, E], I32),
            "marks": {n: s.sem(f"mark_{n}") for n in ("sp", "act", "pool", "pe", "dve")},
        }
        modulation(nc, keep, c, w_ada, b_ada, w_conv, mod_rows)
        with ExitStack() as uctx:
            us = Scope(nc, uctx, "u")
            u_hi, u_lo = us.sb("hi", [P, KD, S], F32R), us.sb("lo", [P, KD, S], F32R)
            modulated_input(nc, keep, x, u_hi, u_lo)
            input_projection(nc, keep, u_hi, u_lo, w_in, qkv_t, conv_t, gate_t)
        attention(nc, keep, qkv_t, o_t)
        branch_outputs(nc, keep, conv_t, o_t, gate_t, w_a, w_b, m_t)
        mix_norm_route(nc, keep, m_t, w_o, x, mod_rows, ln1_g, ln1_b, w_router, b_router, x1, rows, results)
        experts(nc, keep, w_gate, w_up, w_down, rows, results)
        combine_norm(nc, keep, results, x1, mod_rows, ln2_g, ln2_b, out)


_INS = ["x", "c", "w_ada", "b_ada", "w_in", "w_conv", "w_a", "w_b", "w_o", "ln1_g", "ln1_b", "w_router", "b_router",
        "w_gate", "w_up", "w_down", "ln2_g", "ln2_b"]


def kernel(**inputs):
    import numpy as np
    import concourse.bacc as bacc
    from concourse.bass_utils import run_bass_kernel_spmd

    nc = bacc.Bacc("TRN2", target_bir_lowering=False, num_devices=1)
    arrays, args = {}, []
    for name in _INS:
        a = np.ascontiguousarray(inputs[name])
        arrays[f"in_{name}"] = a
        args.append(nc.dram_tensor(f"in_{name}", a.shape, mybir.dt.from_np(a.dtype), kind="ExternalInput").ap())
    out = nc.dram_tensor("out", (1, S, D), F32, kind="ExternalOutput").ap()
    hybrid_layer(nc, *args, out)
    r = run_bass_kernel_spmd(nc, [arrays], core_ids=[0])
    return r.results[0]["out"]
```

```python
from contextlib import ExitStack

import concourse.bass as bass
from concourse import mybir

F32 = mybir.dt.float32
F32R = mybir.dt.float32r
I32 = mybir.dt.int32
U32 = mybir.dt.uint32
ALU = mybir.AluOpType
ACT = mybir.ActivationFunctionType
AX = mybir.AxisListType

P = 128
NB = 512
D = 1024
S = 2048
KD = D // P
NT = S // P
TB = S // NB
CH = 512
HEADS = 8
HD = 64
AW = HEADS * HD
KC = CH // P
E = 16
G = 4
EG = E // G
FF = 512
KF = FF // P
CAP = S + P
BLOCKS = 2 * S // P + E
EPS = 1e-5
ALPHA = 2.0 ** 0.25
BIG = 1e30

FIRST_MOD = 2 * D // NB

SH1, SC1, G1, SH2, SC2, G2 = (KD * i for i in range(6))


class Scope:

    def __init__(self, nc, ctx, tag, used):
        self.nc, self.ctx, self.tag = nc, ctx, tag
        self.used = used

    def sb(self, name, shape, dt=F32):
        return self.ctx.enter_context(self.nc.sbuf_tensor(f"{self.tag}_{name}", shape, dt))

    def ps(self, name, shape, dt=F32):
        return self.ctx.enter_context(self.nc.psum_tensor(f"{self.tag}_{name}", shape, dt))

    def sem(self, name):
        sem = self.nc.alloc_semaphore(f"{self.tag}_{name}")
        self.used.append(sem)
        return sem


def clear_semaphores(nc, used):
    nc.clear_and_free_semaphores(used)
    used.clear()
    nc.all_engine_barrier()


def f32(ap):
    return ap.bitcast(F32)


def mod_products(pe, out, column, w, csilu):
    for m in range(NB // P):
        for k in range(KD):
            mm = pe.matmul(out[:, column + m:column + m + 1], w[:, k, m * P:(m + 1) * P], csilu[:, k:k + 1],
                           start=k == 0, stop=k == KD - 1, skip_group_check=True)
    return mm


def wait_apart(eng, mark, sem, value):
    eng.wait_ge(sem, value)
    eng.sem_inc(mark, 1)


def product(pe, out, pairs, first, last):
    for n, (a, b) in enumerate(pairs):
        mm = pe.matmul(out, a, b, start=first and n == 0, stop=last and n == len(pairs) - 1,
                       skip_group_check=True)
    return mm


def modulation(nc, used, keep, c, w_ada, b_ada, w_conv):
    ident, mod, conv_cols, csilu = keep["ident"], keep["mod"], keep["conv_cols"], keep["csilu"]
    NJ = 6 * KD
    VR = NJ + KD + 3 * KC
    with ExitStack() as ctx:
        s = Scope(nc, ctx, "ada", used)
        vec = s.sb("vec", [VR, P])
        w = s.sb("w", [P, FIRST_MOD, KD, NB])
        p_vec = s.ps("p_vec", [P, NB])
        p_mod = s.ps("p_mod", [P, NB])
        vec_in, vec_turned, cols_out = s.sem("vec_in"), s.sem("vec_turned"), s.sem("cols_out")
        ident_zero, ident_done = s.sem("ident_zero"), s.sem("ident_done")
        silu_done, mod_summed, mod_done = s.sem("silu_done"), s.sem("mod_summed"), s.sem("mod_done")
        w_in = [s.sem(f"w_in{i}") for i in range(FIRST_MOD)]
        block = ctx.enter_context(nc.Block())
        w_view = w_ada.rearrange("l (k p) (b n) -> (l p) b k n", p=P, n=NB)

        @block.gpsimd
        def _(pool):
            pool.memset(ident[:], 0.0).then_inc(ident_zero, 1)
            pool.wait_ge(ident_zero, 1)
            pool.affine_select(out=ident[:], in_=ident[:], compare_op=ALU.not_equal, fill=1.0, base=0,
                               pattern=[[-1, P]], channel_multiplier=1).then_inc(ident_done, 1)

        @block.sync
        def _(sp):
            sp.dma_start(vec[0:NJ, :], b_ada.rearrange("l (r p) -> (l r) p", p=P)).then_inc(vec_in, 16)
            sp.dma_start(vec[NJ:NJ + KD, :], c.rearrange("b (r p) -> (b r) p", p=P)).then_inc(vec_in, 16)
            sp.dma_start(vec[NJ + KD:VR, :], w_conv.rearrange("l t (r p) -> (l t r) p", p=P)).then_inc(vec_in, 16)
            for i in range(FIRST_MOD):
                sp.dma_start(w[:, i], w_view[:, i]).then_inc(w_in[i], 16)

        @block.tensor
        def _(pe):
            pe.wait_ge(vec_in, 48)
            pe.wait_ge(ident_done, 1)
            pe.transpose(p_vec[:, 0:VR], vec[:], ident[0:VR, 0:VR]).then_inc(vec_turned, 1)
            pe.wait_ge(silu_done, 1)
            for i in range(FIRST_MOD):
                pe.wait_ge(w_in[i], 16)
                mm = mod_products(pe, p_mod, i * NB // P, w[:, i], csilu)
            mm.then_inc(mod_summed, 1)

        @block.scalar
        def _(act):
            act.wait_ge(vec_turned, 1)
            act.activation(csilu[:], p_vec[:, NJ:NJ + KD], ACT.Silu).then_inc(silu_done, 1)

        @block.vector
        def _(dve):
            dve.wait_ge(silu_done, 1)
            dve.tensor_copy(mod[:], p_vec[:, 0:NJ]).then_inc(cols_out, 1)
            dve.tensor_copy(conv_cols[:], p_vec[:, NJ + KD:VR]).then_inc(cols_out, 1)
            dve.wait_ge(cols_out, 2)
            dve.wait_ge(mod_summed, 1)
            n = FIRST_MOD * NB // P
            dve.tensor_tensor(mod[:, 0:n], mod[:, 0:n], p_mod[:, 0:n], ALU.add).then_inc(mod_done, 1)
            dve.wait_ge(mod_done, 1)
            dve.tensor_scalar(mod[:, SC1:SC1 + KD], mod[:, SC1:SC1 + KD], 1.0, None, ALU.add)


def modulated_input(nc, used, keep, x, u_hi, u_lo):
    ident, mod = keep["ident"], keep["mod"]
    with ExitStack() as ctx:
        s = Scope(nc, ctx, "u", used)
        xr = s.sb("x", [P, 2, NB // P, D])
        uf = s.sb("uf", [P, 2, NB])
        p_t = s.ps("p_t", [P, 4, NB])
        x_in = [s.sem(f"x_in{i}") for i in range(2)]
        turned, affine, hi_done, lo_done = (s.sem(n) for n in ("turned", "affine", "hi_done", "lo_done"))
        block = ctx.enter_context(nc.Block())
        x_view = x.rearrange("b (g t p) d -> (b p) g t d", p=P, t=NB // P)

        @block.sync
        def _(sp):
            for g in range(TB):
                if g >= 2:
                    sp.wait_ge(turned, KD * (g - 1))
                sp.dma_start(xr[:, g % 2], x_view[:, g]).then_inc(x_in[g % 2], 16)

        @block.tensor
        def _(pe):
            for g in range(TB):
                pe.wait_ge(x_in[g % 2], 16 * (g // 2 + 1))
                for k in range(KD):
                    n = g * KD + k
                    if n >= 4:
                        pe.wait_ge(affine, n - 3)
                    for t in range(NB // P):
                        mm = pe.transpose(p_t[:, n % 4, t * P:(t + 1) * P], xr[:, g % 2, t, k * P:(k + 1) * P], ident[:])
                    mm.then_inc(turned, 1)

        @block.scalar
        def _(act):
            for n in range(TB * KD):
                k = n % KD
                act.wait_ge(turned, n + 1)
                if n >= 2:
                    act.wait_ge(lo_done, n - 1)
                act.activation(uf[:, n % 2], p_t[:, n % 4], ACT.Identity, bias=mod[:, SH1 + k:SH1 + k + 1],
                               scale=mod[:, SC1 + k:SC1 + k + 1]).then_inc(affine, 1)

        @block.vector
        def _(dve):
            for n in range(TB * KD):
                g, k = divmod(n, KD)
                dve.wait_ge(affine, n + 1)
                dve.tensor_copy(u_hi[:, k, g * NB:(g + 1) * NB], uf[:, n % 2]).then_inc(hi_done, 1)

        @block.gpsimd
        def _(pool):
            for n in range(TB * KD):
                g, k = divmod(n, KD)
                pool.wait_ge(hi_done, n + 1)
                pool.tensor_tensor(u_lo[:, k, g * NB:(g + 1) * NB], uf[:, n % 2],
                                   f32(u_hi[:, k, g * NB:(g + 1) * NB]), ALU.subtract).then_inc(lo_done, 1)


def input_projection(nc, used, keep, u_hi, u_lo, w_in, qkv_hi, qkv_lo, conv_t, gate_t):
    conv_cols = keep["conv_cols"]
    with ExitStack() as ctx:
        s = Scope(nc, ctx, "in", used)
        raw = s.sb("raw", [P, 2, KD, P])
        w_hi = s.sb("w_hi", [P, 2, KD, P], F32R)
        w_lo = s.sb("w_lo", [P, 2, KD, P], F32R)
        stage = s.sb("stage", [P, 2, S])
        cx = s.sb("cx", [P, S])
        gated = s.sb("gated", [P, S + 2])
        conv = s.sb("conv", [P, S])
        acc = s.ps("acc", [P, 2, TB, NB])
        raw_in = [s.sem(f"raw_in{i}") for i in range(2)]
        stored = [s.sem(f"stored{i}") for i in range(2)]
        hi_done, lo_done, pe_done = s.sem("hi_done"), s.sem("lo_done"), s.sem("pe_done")
        act_out, dve_out, conv_step, padded = (s.sem(n) for n in ("act_out", "dve_out", "conv_step", "padded"))
        block = ctx.enter_context(nc.Block())
        w_view = w_in.rearrange("l (k p) n -> (l p) k n", p=P)
        QKV, CONV, GATES = 3 * AW // P, 3 * KC, 2 * D // P
        TILES = QKV + CONV + GATES
        FIRST_G = QKV + CONV
        c_cb, c_cc, c_cx, c_q, c_ga = 0, CH, 2 * CH, 3 * CH, 3 * CH + 3 * AW

        def bank(t):
            return slice(t * NB, (t + 1) * NB)

        @block.sync
        def _(sp):
            def load(col, par, t, first=False):
                if not first:
                    sp.wait_ge(lo_done, t - 1)
                sp.dma_start(raw[:, par], w_view[:, :, bass.ds(col, P)]).then_inc(raw_in[par], 16)

            load(c_q, 0, 0, True)
            load(c_q + P, 1, 1, True)

            def store_qkv(t):
                sp.wait_ge(act_out, t + 1)
                sp.dma_start(qkv_hi[bass.ds(t * P, P), :], stage[:, 0]).then_inc(stored[0], 16)
                sp.wait_ge(dve_out, t + 1)
                sp.dma_start(qkv_lo[bass.ds(t * P, P), :], stage[:, 1]).then_inc(stored[1], 16)

            with sp.Fori(0, QKV // 2 - 1) as i:
                for par in range(2):
                    t = 2 * i + par
                    load(c_q + (t + 2) * P, par, t + 2)
                    store_qkv(t)
            load(c_cx, 0, QKV)
            store_qkv(QKV - 2)
            load(c_cc, 1, QKV + 1)
            store_qkv(QKV - 1)

            def conv_round(j, half, last=False):
                t = QKV + 3 * j
                base = 3 * half
                load(c_cb + j * P, (base + 2) % 2, t + 2)
                nxt = (c_ga, c_ga + P) if last else (c_cx + (j + 1) * P, c_cc + (j + 1) * P)
                load(nxt[0], (base + 3) % 2, t + 3)
                load(nxt[1], (base + 4) % 2, t + 4)
                sp.wait_ge(dve_out, QKV + 2 * j + 2)
                sp.dma_start(conv_t[bass.ds(j * P, P), :], stage[:, half]).then_inc(stored[half], 16)

            with sp.Fori(0, KC // 2 - 1) as i:
                for half in range(2):
                    conv_round(2 * i + half, half)
            conv_round(KC - 2, 0)
            conv_round(KC - 1, 1, last=True)

            def store_gate(n, par):
                sp.wait_ge(act_out, QKV + KC + n + 1)
                sp.dma_start(gate_t[bass.ds(n * P, P), :], stage[:, par]).then_inc(stored[par], 16)

            with sp.Fori(0, GATES // 2 - 1) as i:
                for par in range(2):
                    n = 2 * i + par
                    load(c_ga + (n + 2) * P, par, FIRST_G + n + 2)
                    store_gate(n, par)
            for par in range(2):
                store_gate(GATES - 2 + par, par)
            for par in range(2):
                sp.wait_ge(stored[par], 16 * (QKV + (KC + GATES) // 2))

        @block.tensor
        def _(pe):
            def tile(t, par):
                pe.wait_ge(lo_done, t + 1)
                for k in range(KD):
                    for w, us in ((w_hi, (u_hi, u_lo)), (w_lo, (u_hi,))):
                        for n, u in enumerate(us):
                            for tb in range(TB):
                                mm = pe.matmul(acc[:, par, tb], w[:, par, k], u[:, k, bank(tb)],
                                               start=k == 0 and w is w_hi and n == 0,
                                               stop=k == KD - 1 and w is w_lo, skip_group_check=True)
                mm.then_inc(pe_done, 1)

            tile(0, 0)
            tile(1, 1)
            with pe.Fori(1, QKV // 2) as i:
                for par in range(2):
                    pe.wait_ge(act_out, 2 * i + par - 1)
                    pe.wait_ge(dve_out, 2 * i + par - 1)
                    tile(2 * i + par, par)
            with pe.Fori(0, KC // 2) as i:
                for half in range(2):
                    j = 2 * i + half
                    t = QKV + 3 * j
                    pe.wait_ge(act_out, QKV - 1)
                    pe.wait_ge(dve_out, QKV - 1 + 2 * j)
                    tile(t, (3 * half) % 2)
                    pe.wait_ge(act_out, QKV)
                    pe.wait_ge(dve_out, QKV + 2 * j)
                    tile(t + 1, (3 * half + 1) % 2)
                    pe.wait_ge(act_out, QKV + j + 1)
                    tile(t + 2, (3 * half + 2) % 2)
            pe.wait_ge(dve_out, QKV + 2 * KC)
            with pe.Fori(0, GATES // 2) as i:
                for par in range(2):
                    n = 2 * i + par
                    pe.wait_ge(act_out, QKV + KC - 1 + n)
                    tile(FIRST_G + n, par)

        @block.scalar
        def _(act):
            def high(t, par, rnd, first=False):
                act.wait_ge(raw_in[par], 16 * rnd + 16)
                if not first:
                    act.wait_ge(pe_done, t - 1)
                act.activation(w_hi[:, par], raw[:, par], ACT.Copy).then_inc(hi_done, 1)

            def out_qkv(t, par, first=False):
                act.wait_ge(pe_done, t + 1)
                if not first:
                    act.wait_ge(stored[0], 16 * t)
                    act.wait_ge(stored[1], 16 * t)
                for tb in range(TB):
                    ins = act.activation(stage[:, 0, bank(tb)].bitcast(F32R), acc[:, par, tb], ACT.Copy)
                ins.then_inc(act_out, 1)

            high(0, 0, 0, True)
            high(1, 1, 0, True)
            out_qkv(0, 0, True)
            high(2, 0, 1)
            out_qkv(1, 1)
            with act.Fori(1, QKV // 2) as i:
                high(2 * i + 1, 1, i)
                out_qkv(2 * i, 0)
                high(2 * i + 2, 0, i + 1)
                out_qkv(2 * i + 1, 1)
            with act.Fori(0, KC // 2) as i:
                for half in range(2):
                    j = 2 * i + half
                    t = QKV + 3 * j
                    b = 3 * half
                    rnd = QKV // 2 + 3 * i
                    high(t + 1, (b + 1) % 2, rnd + (b + 1) // 2)
                    act.wait_ge(pe_done, t + 1)
                    act.wait_ge(dve_out, QKV - 1 + 2 * j)
                    for tb in range(TB):
                        ins = act.activation(cx[:, bank(tb)], acc[:, b % 2, tb], ACT.Copy)
                    ins.then_inc(act_out, 1)
                    high(t + 2, (b + 2) % 2, rnd + (b + 2) // 2)
                    high(t + 3, (b + 3) % 2, rnd + (b + 3) // 2)

            def out_gate(n, par, rnd):
                act.wait_ge(pe_done, FIRST_G + n + 1)
                act.wait_ge(stored[par], 16 * (rnd + QKV + KC // 2))
                for tb in range(TB):
                    ins = act.activation(stage[:, par, bank(tb)], acc[:, par, tb], ACT.Sigmoid)
                ins.then_inc(act_out, 1)

            with act.Fori(0, GATES // 2 - 1) as i:
                for par in range(2):
                    n = 2 * i + par
                    high(FIRST_G + n + 1, 1 - par, FIRST_G // 2 + i + par)
                    out_gate(n, par, i)
            n = GATES - 2
            high(FIRST_G + n + 1, 1, FIRST_G // 2 + n // 2)
            out_gate(n, 0, n // 2)
            out_gate(n + 1, 1, n // 2)

        @block.vector
        def _(dve):
            dve.memset(gated[:, 0:2], 0.0).then_inc(padded, 1)

            def low(t, par):
                dve.wait_ge(hi_done, t + 1)
                dve.tensor_tensor(w_lo[:, par], raw[:, par], f32(w_hi[:, par]), ALU.subtract).then_inc(lo_done, 1)

            def out_qkv(t, par):
                dve.wait_ge(act_out, t + 1)
                for tb in range(TB):
                    ins = dve.tensor_tensor(stage[:, 1, bank(tb)], acc[:, par, tb], stage[:, 0, bank(tb)],
                                            ALU.subtract)
                ins.then_inc(dve_out, 1)

            low(0, 0)
            low(1, 1)
            out_qkv(0, 0)
            low(2, 0)
            out_qkv(1, 1)
            with dve.Fori(1, QKV // 2) as i:
                low(2 * i + 1, 1)
                out_qkv(2 * i, 0)
                low(2 * i + 2, 0)
                out_qkv(2 * i + 1, 1)
            dve.wait_ge(padded, 1)
            with dve.Fori(0, KC // 2) as i:
                for half in range(2):
                    j = 2 * i + half
                    t = QKV + 3 * j
                    b = 3 * half
                    low(t + 1, (b + 1) % 2)
                    low(t + 2, (b + 2) % 2)
                    dve.wait_ge(pe_done, t + 2)
                    dve.wait_ge(act_out, QKV + j + 1)
                    for tb in range(TB):
                        ins = dve.tensor_tensor(gated[:, 2 + tb * NB:2 + (tb + 1) * NB], acc[:, (b + 1) % 2, tb],
                                                cx[:, bank(tb)], ALU.mult)
                    ins.then_inc(dve_out, 1)
                    dve.wait_ge(dve_out, QKV + 2 * j + 1)
                    dve.tensor_scalar(conv[:], gated[:, 2:S + 2], conv_cols[:, bass.ds(2 * KC + j, 1)], None,
                                      ALU.mult).then_inc(conv_step, 1)
                    for tap in (1, 0):
                        dve.wait_ge(conv_step, 3 * j + 2 - tap)
                        dve.scalar_tensor_tensor(out=conv[:], in0=gated[:, tap:S + tap],
                                                 scalar=conv_cols[:, bass.ds(tap * KC + j, 1)], in1=conv[:],
                                                 op0=ALU.mult, op1=ALU.add).then_inc(conv_step, 1)
                    low(t + 3, (b + 3) % 2)
                    dve.wait_ge(conv_step, 3 * j + 3)
                    dve.wait_ge(pe_done, t + 3)
                    dve.wait_ge(stored[half], 16 * (QKV + i))
                    for tb in range(TB):
                        ins = dve.tensor_tensor(stage[:, half, bank(tb)], acc[:, (b + 2) % 2, tb], conv[:, bank(tb)],
                                                ALU.mult)
                    ins.then_inc(dve_out, 1)
            with dve.Fori(0, GATES // 2 - 1) as i:
                for par in range(2):
                    low(FIRST_G + 2 * i + par + 1, 1 - par)
            low(TILES - 1, 1)


def attention(nc, used, keep, qkv_hi, qkv_lo, w_ada, o_t, mod_rows):
    ident, mod, csilu, marks = keep["ident"], keep["mod"], keep["csilu"], keep["marks"]
    PAIR = 2 * P
    SCALE = HD ** -0.5
    ZW = 2 * NB
    UNITS = [-(-(t + 1) * P // ZW) for t in range(NT)]
    UN_BEFORE = [sum(UNITS[:t]) for t in range(NT + 1)]
    GROUPS = [-(-(t + 1) // 4) for t in range(NT)]
    GR_BEFORE = [sum(GROUPS[:t]) for t in range(NT + 1)]
    NZ = UN_BEFORE[NT]
    ZB, TR = 2, 2
    AHEAD = 3
    SIZES = [(t + 1) * P + 1 for t in range(AHEAD)] + [S + 1 - P * ((NT - 1 - n) % AHEAD) for n in range(AHEAD)]
    PLACE = [sum(SIZES[:t if t < AHEAD else AHEAD + t % AHEAD]) for t in range(NT)]
    MOD_W = NB // 2
    MOD_AT = (NT // 2 - 2, NT - 2)
    NJ = 6 * KD
    with ExitStack() as ctx:
        s = Scope(nc, ctx, "att", used)
        q_parts = s.sb("q_parts", [P, 2, S], F32R)
        k_hi, k_lo = s.sb("k_hi", [P, 2, S], F32R), s.sb("k_lo", [P, 2, S], F32R)
        v_stack = s.sb("v_stack", [P, S])
        v_parts = s.sb("v_parts", [P, 2, NT, P], F32R)
        rest = s.sb("rest", [P, sum(SIZES)])
        wt = s.sb("wt", [P, sum(SIZES)])
        wt_hi, wt_lo = s.sb("wt_hi", [P, 2, NT, PAIR], F32R), s.sb("wt_lo", [P, 2, NT, PAIR], F32R)
        mask = s.sb("mask", [P, P], F32R)
        ident_r = s.sb("ident_r", [P, P], F32R)
        mask_f = s.sb("mask_f", [P, P])
        zero = s.sb("zero", [P, 1])
        low_half = s.sb("low_half", [HD, PAIR])
        o_out = s.sb("o_out", [HD, 2, PAIR])
        w_mod = s.sb("w_mod", [P, KD, MOD_W])
        mod_t = s.sb("mod_t", [NJ, P])
        p_z, p_t, p_o = s.ps("p_z", [P, ZB, ZW]), s.ps("p_t", [P, TR, NB]), s.ps("p_o", [P, 2, NB])
        names = ("mask_step", "const_done", "z_done", "z_used", "rest_done", "scan_done", "weights_done",
                 "turned", "hi_done", "lo_done", "o_done", "o_low", "o_used", "v_in", "mod_in",
                 "mod_done", "mod_step", "row_turned", "row_out", "row_stored")
        m = {n: s.sem(n) for n in names}
        qk_in = [s.sem(f"qk_in{i}") for i in range(2)]
        o_stored = [s.sem(f"o_stored{i}") for i in range(2)]
        block = ctx.enter_context(nc.Block())
        VB = NT // 4
        NR = VB + GR_BEFORE[NT]
        NG = NT // 2
        mod_view = w_ada.rearrange("l (k p) (b n) -> (l p) b k n", p=P, n=MOD_W)
        MOD_0 = FIRST_MOD * NB // MOD_W

        def heads(eng, run_head):
            with eng.Fori(0, HEADS // 2 - 1) as i:
                for sl in range(2):
                    run_head(i, sl, True)
            for sl in range(2):
                run_head(HEADS // 2 - 1, sl, sl == 0)

        @block.sync
        def _(sp):
            for i in range(2):
                sp.sem_inc(o_stored[i], 16)

            def load_qk(h, sl):
                for half in range(2):
                    rows = slice(half * HD, (half + 1) * HD)
                    src = (qkv_hi, qkv_lo)[half]
                    sp.dma_start(f32(q_parts[rows, sl]), src[bass.ds(h * HD, HD), :]).then_inc(qk_in[sl], 16)
                    sp.dma_start(f32(k_hi[rows, sl]), qkv_hi[bass.ds(h * HD + AW, HD), :]).then_inc(qk_in[sl], 16)
                    sp.dma_start(f32(k_lo[rows, sl]), qkv_lo[bass.ds(h * HD + AW, HD), :]).then_inc(qk_in[sl], 16)

            def load_v(h):
                for half, src in enumerate((qkv_hi, qkv_lo)):
                    sp.dma_start(v_stack[half * HD:(half + 1) * HD, :], src[bass.ds(h * HD + 2 * AW, HD), :]
                                 ).then_inc(m["v_in"], 16)

            load_qk(0, 0)
            load_v(0)
            sp.dma_start(w_mod[:], mod_view[:, MOD_0]).then_inc(m["mod_in"], 16)

            def run_head(i, sl, more):
                h = 2 * i + sl
                if more:
                    sp.wait_ge(m["o_done"], h * NG + 2)
                    load_qk(h + 1, 1 - sl)
                    sp.wait_ge(m["turned"], h * NR + VB)
                    load_v(h + 1)
                for g in range(NG):
                    for n, t in enumerate(MOD_AT):
                        if g == t // 2 and (more or n == 0):
                            sp.wait_ge(m["mod_done"], 2 * h + (n + 1))
                            sp.dma_start(w_mod[:], mod_view[:, bass.ds(2 * h + (MOD_0 + n + 1), 1)].rearrange(
                                "p b k n -> p (b k) n")).then_inc(m["mod_in"], 16)
                    sp.wait_ge(m["o_used"], h * NG + g + 3)
                    sp.dma_start(o_t[bass.ds(h * HD, HD), g * PAIR:(g + 1) * PAIR], o_out[:, g % 2]
                                 ).then_inc(o_stored[g % 2], 16)

            heads(sp, run_head)
            sp.wait_ge(m["row_out"], 1)
            sp.dma_start(mod_rows.rearrange("(r p) -> r p", p=P), mod_t[:]).then_inc(m["row_stored"], 16)
            sp.wait_ge(m["row_stored"], 16)
            for i in range(2):
                sp.wait_ge(o_stored[i], 16 * (HEADS * NG // 2 + 1))

        @block.gpsimd
        def _(pool):
            pool.memset(mask_f[:], 0.0).then_inc(m["mask_step"], 1)
            pool.wait_ge(m["mask_step"], 1)
            pool.affine_select(out=mask_f[:], in_=mask_f[:], compare_op=ALU.is_gt, fill=-BIG, base=0,
                               pattern=[[-1, P]], channel_multiplier=1).then_inc(m["mask_step"], 1)
            pool.wait_ge(m["mask_step"], 2)
            pool.tensor_copy(mask[:], mask_f[:]).then_inc(m["const_done"], 1)
            pool.tensor_copy(ident_r[:], ident[:]).then_inc(m["const_done"], 1)
            pool.memset(rest[:], 1.0).then_inc(m["const_done"], 1)
            with pool.Fori(0, HEADS) as h:
                for t in range(NT):
                    w = (t + 1) * P
                    pool.wait_ge(m["z_used"], h * NZ + UN_BEFORE[t + 1] + ZB)
                    pool.wait_ge(m["scan_done"], h * NT + t + 1)
                    o = PLACE[t]
                    pool.tensor_tensor(wt[:, o:o + w], wt[:, o:o + w], rest[:, o + 1:o + w + 1], ALU.mult
                                       ).then_inc(m["weights_done"], 1)

        @block.tensor
        def _(pe):
            pe.sem_inc(m["o_done"], 2)
            pe.wait_ge(m["const_done"], 3)

            def scores(h, sl, t, banks):
                w = (t + 1) * P
                q = q_parts[:, sl, t * P:(t + 1) * P]
                for c in banks:
                    u, a, b = c * NB // ZW, c * NB, min(w, (c + 1) * NB)
                    n = UN_BEFORE[t] + u
                    if a == u * ZW:
                        pe.wait_ge(m["z_used"], h * NZ + n + 1)
                    out = p_z[:, n % ZB, a - u * ZW:b - u * ZW]
                    pe.matmul(out, q, k_hi[:, sl, a:b], start=True, stop=False, skip_group_check=True)
                    mm = pe.matmul(out, q, k_lo[:, sl, a:b], start=False, stop=b < w, skip_group_check=True)
                    if b == w:
                        mm = pe.matmul(p_z[:, n % ZB, b - u * ZW - P:b - u * ZW], ident_r[:], mask[:],
                                       start=False, stop=True, skip_group_check=True)
                    if b == min(w, (u + 1) * ZW):
                        mm.then_inc(m["z_done"], 1)

            def turn_values(h):
                pe.wait_ge(m["v_in"], 32 * h + 32)
                for n in range(VB):
                    pe.wait_ge(m["lo_done"], h * NR + n + 1)
                    for j in range(4):
                        mm = pe.transpose(p_t[:, n % TR, j * P:(j + 1) * P],
                                          v_stack[:, (4 * n + j) * P:(4 * n + j + 1) * P], ident[:])
                    mm.then_inc(m["turned"], 1)

            def turn(h, t, r):
                if r == 0:
                    pe.wait_ge(m["weights_done"], h * NT + t + 1)
                n = VB + GR_BEFORE[t] + r
                pe.wait_ge(m["lo_done"], h * NR + n + 1)
                for j in range(4 * r, min(4 * r + 4, t + 1)):
                    mm = pe.transpose(p_t[:, n % TR, (j - 4 * r) * P:(j - 4 * r + 1) * P],
                                      wt[:, PLACE[t] + j * P:PLACE[t] + (j + 1) * P], ident[:])
                mm.then_inc(m["turned"], 1)

            def values(h, sl, g, blocks):
                for j in blocks:
                    if j == 0:
                        pe.wait_ge(m["lo_done"], h * NR + VB + GR_BEFORE[2 * g + 2] + TR)
                        pe.wait_ge(m["o_used"], h * NG + g + 1)
                    first = P if j == 2 * g + 1 else 0
                    for n, part in enumerate((wt_hi, wt_lo)):
                        mm = pe.matmul(p_o[:, g % 2, first:PAIR], v_parts[:, sl, j], part[:, g % 2, j, first:PAIR],
                                       start=j == 0 and n == 0, stop=j == 2 * g + 1 and n == 1, skip_group_check=True)
                    if j == 2 * g + 1:
                        mm.then_inc(m["o_done"], 1)

            def share(count, r, parts):
                return range(count * r // parts, count * (r + 1) // parts)

            pe.wait_ge(qk_in[0], 96)
            for t in range(AHEAD):
                scores(0, 0, t, range(GROUPS[t]))
            turn_values(0)

            def run_head(i, sl, more):
                h = 2 * i + sl
                for t in range(NT):
                    ahead = (t + AHEAD) % NT
                    g = t // 2 - 1
                    if t + AHEAD == NT and more:
                        pe.wait_ge(qk_in[1 - sl], 96 * (i + sl) + 96)
                    for r in range(GROUPS[t]):
                        turn(h, t, r)
                        if t + AHEAD < NT:
                            scores(h, sl, ahead, share(GROUPS[ahead], r, GROUPS[t]))
                        elif more:
                            scores(h + 1, 1 - sl, ahead, share(GROUPS[ahead], r, GROUPS[t]))
                        if g >= 0:
                            values(h, sl, g, [t % 2 * (g + 1) + j for j in share(g + 1, r, GROUPS[t])])
                    if t in MOD_AT:
                        n = MOD_AT.index(t)
                        pe.wait_ge(m["mod_in"], 32 * h + (16 * n + 16))
                        for c in range(MOD_W // P):
                            out = p_o[:, 0, bass.ds((2 * h + n) * (MOD_W // P) + (PAIR + c), 1)]
                            for k in range(KD):
                                mm = pe.matmul(out, w_mod[:, k, c * P:(c + 1) * P], csilu[:, k:k + 1],
                                               start=k == 0, stop=k == KD - 1, skip_group_check=True)
                        mm.then_inc(m["mod_done"], 1)
                if more:
                    turn_values(h + 1)
                values(h, sl, NG - 1, range(NT))

            heads(pe, run_head)
            pe.wait_ge(m["mod_step"], 2)
            pe.wait_ge(m["lo_done"], HEADS * NR + TR)
            pe.transpose(p_t[0:NJ, 0, 0:P], mod[:], ident[:]).then_inc(m["row_turned"], 1)

        @block.scalar
        def _(act):
            act.sem_inc(m["z_used"], ZB)
            act.wait_ge(m["const_done"], 3)

            def sigmoids(h, t):
                w, o = (t + 1) * P, PLACE[t]
                spans = [(n, u * ZW, min(w, (u + 1) * ZW)) for u, n in enumerate(range(UN_BEFORE[t], UN_BEFORE[t + 1]))]
                for n, a, b in spans:
                    act.wait_ge(m["z_done"], h * NZ + n + 1)
                    ins = act.activation(rest[:, o + a:o + b], p_z[:, n % ZB, 0:b - a], ACT.Sigmoid, scale=-SCALE)
                ins.then_inc(m["rest_done"], 1)
                for n, a, b in spans:
                    act.activation(wt[:, o + a:o + b], p_z[:, n % ZB, 0:b - a], ACT.Sigmoid, scale=SCALE
                                   ).then_inc(m["z_used"], 1)

            def high(h, t):
                act.wait_ge(m["o_done"], h * NG + t // 2 + 1)
                for r in range(GROUPS[t]):
                    n = VB + GR_BEFORE[t] + r
                    j, k = 4 * r, min(4 * r + 4, t + 1)
                    act.wait_ge(m["turned"], h * NR + n + 1)
                    act.activation(wt_hi[:, t // 2 % 2, j:k, t % 2 * P:(t % 2 + 1) * P],
                                   p_t[:, n % TR, 0:(k - j) * P].rearrange("p (j t) -> p j t", t=P), ACT.Copy
                                   ).then_inc(m["hi_done"], 1)

            def copy_values(h, sl):
                for n in range(VB):
                    act.wait_ge(m["turned"], h * NR + n + 1)
                    act.activation(v_parts[:, sl, 4 * n:4 * n + 2], p_t[:, n % TR, 0:2 * P].rearrange(
                        "p (j d) -> p j d", d=P), ACT.Copy).then_inc(m["hi_done"], 1)

            for t in range(AHEAD):
                sigmoids(0, t)
            copy_values(0, 0)

            def run_head(i, sl, more):
                h = 2 * i + sl
                for t in range(NT):
                    high(h, t)
                    if t + AHEAD < NT or more:
                        sigmoids(h if t + AHEAD < NT else h + 1, (t + AHEAD) % NT)
                if more:
                    copy_values(h + 1, 1 - sl)

            heads(act, run_head)

        @block.vector
        def _(dve):
            dve.sem_inc(m["lo_done"], TR)
            dve.sem_inc(m["o_used"], 2)
            dve.memset(zero[:], 0.0).then_inc(m["o_low"], 1)
            dve.wait_ge(m["o_low"], 1)

            def scan(h, t):
                w = (t + 1) * P
                dve.wait_ge(m["rest_done"], h * NT + t + 1)
                r = rest[:, PLACE[t]:PLACE[t] + w]
                dve.tensor_tensor_scan(r[:, ::-1], r[:, ::-1], zero[:].to_broadcast([P, w]), 1.0, ALU.mult, ALU.max
                                       ).then_inc(m["scan_done"], 1)

            def low(h, t):
                for r in range(GROUPS[t]):
                    n = VB + GR_BEFORE[t] + r
                    j, k = 4 * r, min(4 * r + 4, t + 1)
                    cols = (slice(None), t // 2 % 2, slice(j, k), slice(t % 2 * P, (t % 2 + 1) * P))
                    dve.wait_ge(m["hi_done"], h * NR + n + 1)
                    dve.tensor_tensor(wt_lo[cols], p_t[:, n % TR, 0:(k - j) * P].rearrange("p (j t) -> p j t", t=P),
                                      f32(wt_hi[cols]), ALU.subtract).then_inc(m["lo_done"], 1)

            def output(h, g):
                dve.wait_ge(m["o_done"], h * NG + g + 3)
                dve.wait_ge(m["o_used"], h * NG + g + 2)
                dve.tensor_copy(low_half[:], p_o[HD:P, g % 2, 0:PAIR]).then_inc(m["o_low"], 1)
                dve.wait_ge(m["o_low"], h * NG + g + 2)
                dve.wait_ge(o_stored[g % 2], 16 * (h * (NG // 2) + g // 2 + 1))
                dve.tensor_tensor(o_out[:, g % 2], p_o[0:HD, g % 2, 0:PAIR], low_half[:], ALU.add
                                  ).then_inc(m["o_used"], 1)

            def copy_values(h, sl):
                for n in range(VB):
                    dve.wait_ge(m["hi_done"], h * NR + n + 1)
                    dve.tensor_copy(v_parts[:, sl, 4 * n + 2:4 * n + 4], p_t[:, n % TR, 2 * P:4 * P].rearrange(
                        "p (j d) -> p j d", d=P)).then_inc(m["lo_done"], 1)

            for t in range(AHEAD - 1):
                scan(0, t)
            copy_values(0, 0)

            def run_head(i, sl, more):
                h = 2 * i + sl
                for t in range(NT):
                    ahead = t + AHEAD - 1
                    low(h, t)
                    if ahead < NT:
                        scan(h, ahead)
                    elif more:
                        scan(h + 1, ahead - NT)
                    if t % 2 == 1 and t > 1:
                        output(h, t // 2 - 1)
                if more:
                    copy_values(h + 1, 1 - sl)
                output(h, NG - 1)

            heads(dve, run_head)
            n = FIRST_MOD * NB // P
            dve.wait_ge(m["mod_done"], 2 * HEADS)
            dve.tensor_tensor(mod[:, n:NJ], mod[:, n:NJ], p_o[:, 0, PAIR:PAIR + NJ - n], ALU.add
                              ).then_inc(m["mod_step"], 1)
            dve.wait_ge(m["mod_step"], 1)
            dve.tensor_scalar(mod[:, SC2:SC2 + KD], mod[:, SC2:SC2 + KD], 1.0, None, ALU.add
                              ).then_inc(m["mod_step"], 1)
            dve.wait_ge(m["row_turned"], 1)
            dve.tensor_copy(mod_t[:], p_t[0:NJ, 0, 0:P]).then_inc(m["row_out"], 1)


def branch_outputs(nc, used, keep, conv_t, o_t, gate_t, w_a, w_b, m_t):
    RB = 4
    with ExitStack() as ctx:
        s = Scope(nc, ctx, "br", used)
        w_raw = s.sb("w_raw", [P, 2, KC, D])
        w_hi, w_lo = s.sb("w_hi", [P, 2, KC, D], F32R), s.sb("w_lo", [P, 2, KC, D], F32R)
        b_raw = s.sb("b_raw", [P, 2, KC, NB])
        b_hi, b_lo = s.sb("b_hi", [P, 2, KC, NB], F32R), s.sb("b_lo", [P, 2, KC, NB], F32R)
        gates = s.sb("gates", [P, RB, 2, NB])
        prod = s.sb("prod", [P, RB, 2, NB])
        acc = s.ps("acc", [P, RB, 2, NB])
        names = ("w_in", "w_hi_done", "w_lo_done", "b_hi_done", "b_lo_done", "pe_done", "prod_done", "sum_done")
        m = {n: s.sem(n) for n in names}
        b_in = s.sem("b_in")
        g_in = [s.sem(f"g_in{i}") for i in range(RB)]
        stored = [s.sem(f"stored{i}") for i in range(RB)]
        block = ctx.enter_context(nc.Block())
        gate_v = gate_t.rearrange("(b r) t -> r b t", b=2)

        @block.sync
        def _(sp):
            for n, w in enumerate((w_a, w_b)):
                sp.dma_start(w_raw[:, n], w.rearrange("l (k p) n -> (l p) k n", p=P)).then_inc(m["w_in"], 16)
            with sp.Fori(0, TB) as tb:
                sp.wait_ge(m["b_lo_done"], 2 * tb + 2)
                for n, src in enumerate((conv_t, o_t)):
                    sp.dma_start(b_raw[:, n], src.rearrange("(k p) t -> p k t", p=P)[:, :, bass.ds(tb * NB, NB)]
                                 ).then_inc(b_in, 16)
                for d in range(KD):
                    sp.wait_ge(m["prod_done"], 2 * (tb * KD + d) + 2)
                    sp.dma_start(gates[:, d % RB], gate_v[d * P:(d + 1) * P, :, bass.ds(tb * NB, NB)]
                                 ).then_inc(g_in[d % RB], 16)

        @block.tensor
        def _(pe):
            with pe.Fori(0, TB) as tb:
                pe.wait_ge(m["w_lo_done"], 2)
                pe.wait_ge(m["b_lo_done"], 2 * tb + 4)
                for d in range(KD):
                    pe.wait_ge(m["prod_done"], 2 * (tb * KD + d) + 2)
                    for n in range(2):
                        for k in range(KC):
                            cols = slice(d * P, (d + 1) * P)
                            mm = product(pe, acc[:, d % RB, n],
                                         ((w_hi[:, n, k, cols], b_hi[:, n, k]), (w_hi[:, n, k, cols], b_lo[:, n, k]),
                                          (w_lo[:, n, k, cols], b_hi[:, n, k])), k == 0, k == KC - 1)
                    mm.then_inc(m["pe_done"], 1)

        @block.scalar
        def _(act):
            act.wait_ge(m["w_in"], 32)
            for n in range(2):
                act.activation(w_hi[:, n], w_raw[:, n], ACT.Copy).then_inc(m["w_hi_done"], 1)
            act.sem_inc(m["pe_done"], 1)
            with act.Fori(0, TB) as tb:
                act.wait_ge(b_in, 32 * tb + 32)
                act.wait_ge(m["pe_done"], tb * KD + 1)
                for n in range(2):
                    act.activation(b_hi[:, n], b_raw[:, n], ACT.Copy).then_inc(m["b_hi_done"], 1)
                for d in range(KD):
                    act.wait_ge(m["sum_done"], tb * KD + d + 1)
                    act.dma_start(m_t[d * P:(d + 1) * P, bass.ds(tb * NB, NB)], prod[:, d % RB, 0]
                                  ).then_inc(stored[d % RB], 16)
            for i in range(RB):
                act.wait_ge(stored[i], 16 * (TB * KD // RB + 1))

        @block.vector
        def _(dve):
            dve.sem_inc(m["prod_done"], 2 * RB)
            dve.sem_inc(m["b_lo_done"], 2)
            for n in range(2):
                dve.wait_ge(m["w_hi_done"], n + 1)
                dve.tensor_tensor(w_lo[:, n], w_raw[:, n], f32(w_hi[:, n]), ALU.subtract).then_inc(m["w_lo_done"], 1)
            with dve.Fori(0, TB) as tb:
                for n in range(2):
                    dve.wait_ge(m["b_hi_done"], 2 * tb + n + 1)
                    dve.tensor_tensor(b_lo[:, n], b_raw[:, n], f32(b_hi[:, n]), ALU.subtract
                                      ).then_inc(m["b_lo_done"], 1)
                for d in range(KD):
                    u = tb * KD + d
                    dve.wait_ge(m["pe_done"], u + 2)
                    dve.wait_ge(g_in[d % RB], 16 * (tb * (KD // RB) + d // RB + 1))
                    dve.wait_ge(stored[d % RB], 16 * (tb * (KD // RB) + d // RB + 1))
                    for n in range(2):
                        dve.tensor_tensor(prod[:, d % RB, n], acc[:, d % RB, n], gates[:, d % RB, n], ALU.mult
                                          ).then_inc(m["prod_done"], 1)

        @block.gpsimd
        def _(pool):
            for i in range(RB):
                pool.sem_inc(stored[i], 16)
            with pool.Fori(0, TB) as tb:
                for d in range(KD):
                    u = tb * KD + d
                    pool.wait_ge(m["prod_done"], 2 * u + 2 + 2 * RB)
                    pool.tensor_tensor(prod[:, d % RB, 0], prod[:, d % RB, 0], prod[:, d % RB, 1], ALU.add
                                       ).then_inc(m["sum_done"], 1)


class Tile:

    def __init__(self, i, o):
        self.n, self.half, self.quarter = 4 * i + o, 2 * i + o // 2, i + o // 4
        self.s2, self.s4 = o % 2, o % 4
        self.live = not isinstance(i, int) or 0 <= 4 * i + o < NT
        self.i, self.o = i, o

    def __add__(self, k):
        return Tile(self.i, self.o + k)


def pipeline(eng, step, lag):
    for o in range(4):
        step(Tile(0, o))
    with eng.Fori(1, NT // 4 - 1) as i:
        for o in range(4):
            step(Tile(i, o))
    for o in range(4 + lag):
        step(Tile(NT // 4 - 1, o))


class Chain:

    def __init__(self, eng, sem, base):
        self.eng, self.sem, self.base, self.n = eng, sem, base, 0

    def link(self, ins, mark=None):
        self.n += 1
        ins.then_inc(self.sem, 1)
        if mark is None:
            self.eng.wait_ge(self.sem, self.base + self.n)
        else:
            wait_apart(self.eng, mark, self.sem, self.base + self.n)


def mix_norm_route(nc, used, keep, m_t, w_o, x, mod_rows, ln1_g, ln1_b, w_router, b_router, x1, rows, results):
    ident, dest, gate_w, table, marks = (keep[n] for n in ("ident", "dest", "gate_w", "table", "marks"))
    A_OPS, C_OPS, R1_OPS, R2_OPS = 3, 2, 22, 3
    with ExitStack() as ctx:
        s = Scope(nc, ctx, "mix", used)
        w_raw = s.sb("w_raw", [P, KD // 2, D])
        w_hi, w_lo = s.sb("w_hi", [P, KD, D], F32R), s.sb("w_lo", [P, KD, D], F32R)
        a_raw = s.sb("a_raw", [P, 2, KD, P])
        a_hi, a_lo = s.sb("a_hi", [P, 2, KD, P], F32R), s.sb("a_lo", [P, 2, KD, P], F32R)
        xt, y, x1t = s.sb("xt", [P, 2, D]), s.sb("y", [P, D]), s.sb("x1t", [P, 2, D])
        u2, u2t = s.sb("u2", [P, 4, D]), s.sb("u2t", [P, KD, P])
        g1r, ln_g, ln_b, sc2r, sh2r = (s.sb(n, [P, D]) for n in ("g1r", "ln_g", "ln_b", "sc2r", "sh2r"))
        wr, br = s.sb("wr", [P, KD, E]), s.sb("br", [P, E])
        stats, mv = s.sb("stats", [P, 2, 6]), s.sb("mv", [P, 2])
        var, rstd, minus_half = s.sb("var", [P, 1]), s.sb("rstd", [P, 1]), s.sb("minus_half", [P, 1])
        tri, ones = s.sb("tri", [P, P]), s.sb("ones", [P, P])
        no_twin = s.sb("no_twin", [P, G, EG, EG])
        down_i, down = s.sb("down_i", [P, E], I32), s.sb("down", [P, E])
        base_i, base = s.sb("base_i", [P, E], I32), s.sb("base", [P, E])
        aff, sel, pairs = s.sb("aff", [P, E]), s.sb("sel", [P, E]), s.sb("pairs", [P, G, EG, EG])
        g_score, g_key, g_off = s.sb("g_score", [P, G]), s.sb("g_key", [P, G]), s.sb("g_off", [P, G])
        top, left, key = s.sb("top", [P, 1]), s.sb("left", [P, 2, E]), s.sb("key", [P, E])
        chosen = s.sb("chosen", [P, 2, 2, E])
        all_chosen = s.sb("all_chosen", [P, NT, 2, E])
        all_at = s.sb("all_at", [P, 2 * NT, E])
        moved = s.sb("moved", [P, 2 * NT])
        all_dest, shift = s.sb("all_dest", [P, 2 * NT]), s.sb("shift", [P, E])
        both, seen = s.sb("both", [P, 2, E]), s.sb("seen", [P, 2, E])
        picked, gates, g_sum = s.sb("picked", [P, 2, E]), s.sb("gates", [P, 2]), s.sb("g_sum", [P, 1])
        place, at, dest_f = s.sb("place", [P, E]), s.sb("at", [P, 2, E]), s.sb("dest_f", [P, 2])
        dest_now = s.sb("dest_now", [P, 2, 2], U32)
        n_rows, n_blk, tab_i, tab_f = (s.sb("n_rows", [P, E]), s.sb("n_blk", [P, E], I32), s.sb("tab_i", [P, E], I32),
                                       s.sb("tab_f", [P, E]))
        tab_l = s.sb("tab_l", [P, E])
        p_mix, p_t, p_r = s.ps("p_mix", [P, 2, 2, NB]), s.ps("p_t", [P, 2, NB]), s.ps("p_r", [P, 2, NB])
        names = ("const_in", "w_in", "w_hi_done", "w_lo_done", "a_hi_done", "a_lo_done", "mix_done", "mix_used",
                 "a_step", "c_step", "var_done", "var_step", "rstd_done", "x1_done", "u2_step", "u2_done", "turned",
                 "u2t_done", "logits_done", "aff_done", "r1_step", "recip_done", "both_done", "r1_done", "ranked", "rank_used", "r2_step",
                 "dest_done", "const_step", "const_done", "tail_step")
        m = {n: s.sem(n) for n in names}
        a_in = [s.sem(f"a_in{i}") for i in range(2)]
        x_in = [s.sem(f"x_in{i}") for i in range(2)]
        x1_stored = [s.sem(f"x1_stored{i}") for i in range(2)]
        scattered = [s.sem(f"scattered{i}") for i in range(4)]
        block = ctx.enter_context(nc.Block())

        def mod_row(j):
            return mod_rows[j * P:j * P + D].rearrange("(a d) -> a d", a=1).to_broadcast([P, D])


        @block.sync
        def _(sp):
            for i in range(2):
                sp.sem_inc(x1_stored[i], 16)
            w_view = w_o.rearrange("l (k p) n -> (l p) k n", p=P)
            sp.dma_start(w_raw[:], w_view[:, 0:KD // 2]).then_inc(m["w_in"], 16)

            def load_a(t):
                sp.dma_start(a_raw[:, t.s2], m_t.rearrange("(k p) t -> p k t", p=P)[:, :, bass.ds(t.n * P, P)]
                             ).then_inc(a_in[t.s2], 16)

            def load_x(t):
                sp.dma_start(xt[:, t.s2], x.rearrange("b t d -> (b t) d")[bass.ds(t.n * P, P), :]
                             ).then_inc(x_in[t.s2], 16)

            for o in range(2):
                load_a(Tile(0, o))
                load_x(Tile(0, o))
            for dst, src in ((g1r, mod_row(G1)), (sc2r, mod_row(SC2)), (sh2r, mod_row(SH2)),
                             (ln_g, ln1_g.to_broadcast([P, D])), (ln_b, ln1_b.to_broadcast([P, D])),
                             (wr, w_router.rearrange("(k p) e -> p k e", p=P)),
                             (br, b_router.rearrange("(a e) -> a e", a=1).to_broadcast([P, E]))):
                sp.dma_start(dst[:], src).then_inc(m["const_in"], 16)
            sp.wait_ge(m["w_lo_done"], 1)
            sp.dma_start(w_raw[:], w_view[:, KD // 2:KD]).then_inc(m["w_in"], 16)

            def step(t):
                if (t + 2).live:
                    sp.wait_ge(m["a_lo_done"], t.n + 1)
                    load_a(t + 2)
                sp.wait_ge(m["x1_done"], t.n + 1)
                sp.dma_start(x1[bass.ds(t.n * P, P), :], x1t[:, t.s2]).then_inc(x1_stored[t.s2], 16)
                if (t + 2).live:
                    load_x(t + 2)

            pipeline(sp, step, 0)
            for i in range(2):
                sp.wait_ge(x1_stored[i], 16 * (NT // 2 + 1))

        @block.tensor
        def _(pe):
            pe.sem_inc(m["mix_done"], 2)
            pe.sem_inc(m["logits_done"], 1)
            pe.wait_ge(m["w_lo_done"], 2)
            pe.wait_ge(m["const_done"], 1)
            pe.wait_ge(m["const_in"], 16 * 7)

            def step(t):
                if t.live:
                    pe.wait_ge(m["a_lo_done"], t.n + 1)
                    pe.wait_ge(m["mix_used"], 2 * t.n + 2)
                    for k in range(KD):
                        for n in range(2):
                            w = slice(n * NB, (n + 1) * NB)
                            mm = product(pe, p_mix[:, t.s2, n], ((a_hi[:, t.s2, k], w_hi[:, k, w]),
                                                                 (a_hi[:, t.s2, k], w_lo[:, k, w]),
                                                                 (a_lo[:, t.s2, k], w_hi[:, k, w])), k == 0, k == KD - 1)
                    mm.then_inc(m["mix_done"], 1)
                b = t + -2
                if b.live:
                    pe.wait_ge(m["u2_done"], b.n + 3)
                    pe.wait_ge(m["u2t_done"], b.n + 1)
                    for k in range(KD):
                        mm = pe.transpose(p_t[:, k // 4, k % 4 * P:(k % 4 + 1) * P], u2[:, b.s4, k * P:(k + 1) * P], ident[:])
                    mm.then_inc(m["turned"], 1)
                c = t + -3
                if c.live:
                    pe.wait_ge(m["r1_done"], c.n + 2)
                    pe.wait_ge(m["rank_used"], c.n + 1)
                    pe.matmul(p_r[:, 1, 0:E], tri[:], both[:, c.s2], start=True, stop=False)
                    pe.matmul(p_r[:, 1, 0:E], ones[:], seen[:, c.s2], start=False, stop=True).then_inc(m["ranked"], 1)
                if b.live:
                    pe.wait_ge(m["u2t_done"], b.n + 2)
                    pe.wait_ge(m["aff_done"], b.n + 1)
                    for k in range(KD):
                        mm = pe.matmul(p_r[:, 0, 0:E], u2t[:, k], wr[:, k], start=k == 0, stop=k == KD - 1)
                    mm.then_inc(m["logits_done"], 1)

            pipeline(pe, step, 3)
            pe.wait_ge(m["rank_used"], NT + 1)
            pe.matmul(p_r[:, 1, 0:E], ones[:], seen[:, NT % 2], start=True, stop=True).then_inc(m["ranked"], 1)

        @block.scalar
        def _(act):
            act.sem_inc(m["u2t_done"], 1)
            act.sem_inc(m["aff_done"], 1)

            def high(t):
                act.wait_ge(a_in[t.s2], 16 * t.half + 16)
                act.wait_ge(m["mix_done"], t.n + 1)
                act.activation(a_hi[:, t.s2], a_raw[:, t.s2], ACT.Copy).then_inc(m["a_hi_done"], 1)

            for i in range(2):
                act.wait_ge(m["w_in"], 16 * i + 16)
                act.activation(w_hi[:, i * KD // 2:(i + 1) * KD // 2], w_raw[:], ACT.Copy).then_inc(m["w_hi_done"], 1)
            high(Tile(0, 0))

            def step(t):
                if (t + 1).live:
                    high(t + 1)
                b = t + -2
                if b.live:
                    act.wait_ge(m["turned"], b.n + 1)
                    act.wait_ge(m["logits_done"], b.n + 1)
                    for n in range(2):
                        ins = act.activation(u2t[:, 4 * n:4 * n + 4], p_t[:, n].rearrange("p (k t) -> p k t", t=P), ACT.Copy)
                    ins.then_inc(m["u2t_done"], 1)
                    act.wait_ge(m["logits_done"], b.n + 2)
                    act.wait_ge(m["r1_done"], b.n + 1)
                    act.activation(aff[:], p_r[:, 0, 0:E], ACT.Sigmoid).then_inc(m["aff_done"], 1)

            pipeline(act, step, 2)

        @block.gpsimd
        def _(pool):
            pool.sem_inc(m["u2_done"], 2)
            cs = Chain(pool, m["const_step"], 0)
            cs.link(pool.memset(tri[:], 1.0))
            cs.link(pool.affine_select(out=tri[:], in_=tri[:], compare_op=ALU.is_gt, fill=0.0, base=0,
                                       pattern=[[1, P]], channel_multiplier=-1))
            cs.link(pool.memset(ones[:], 1.0))
            cs.link(pool.memset(minus_half[:], -0.5))
            cs.link(pool.memset(no_twin[:], 0.0))
            cs.link(pool.affine_select(out=no_twin[:], in_=no_twin[:], compare_op=ALU.not_equal, fill=-BIG, base=0,
                                       pattern=[[0, G], [1, EG], [-1, EG]], channel_multiplier=0))
            cs.link(pool.iota(down_i[:], pattern=[[-1, E]], base=E, channel_multiplier=0))
            cs.link(pool.tensor_copy(down[:], down_i[:]))
            cs.link(pool.iota(base_i[:], pattern=[[CAP, E]], base=0, channel_multiplier=0))
            cs.link(pool.tensor_copy(base[:], base_i[:]))
            pool.memset(seen[:], 0.0).then_inc(m["const_done"], 1)

            def low(t):
                pool.wait_ge(m["a_hi_done"], t.n + 1)
                pool.tensor_tensor(a_lo[:, t.s2], a_raw[:, t.s2], f32(a_hi[:, t.s2]), ALU.subtract
                                   ).then_inc(m["a_lo_done"], 1)

            low(Tile(0, 0))

            def step(t):
                if (t + 1).live:
                    low(t + 1)
                if t.live:
                    wait_apart(pool, marks["pool"], m["var_done"], t.n + 1)
                    pool.tensor_scalar(var[:], mv[:, 1:2], EPS, None, ALU.add).then_inc(m["var_step"], 1)
                    pool.wait_ge(m["var_step"], t.n + 1)
                    pool.tensor_tensor(rstd[:], var[:], minus_half[:], ALU.pow).then_inc(m["rstd_done"], 1)
                c = t + -3
                if c.live:
                    wait_apart(pool, marks["pool"], m["dest_done"], c.n + 1)
                    for k in range(2):
                        pool.indirect_dma_start(out=rows, out_offset=bass.IndirectOffsetOnAxis(
                            ap=dest_now[:, c.s2, k:k + 1], axis=0), in_=u2[:, c.s4], in_offset=None
                        ).then_inc(scattered[c.s4], 16)
                if t.live:
                    pool.wait_ge(m["x1_done"], t.n + 1)
                    if (t + -4).live:
                        pool.wait_ge(scattered[t.s4], 32 * t.quarter)
                    pool.tensor_tensor(u2[:, t.s4], x1t[:, t.s2], sc2r[:], ALU.mult).then_inc(m["u2_step"], 1)
                    pool.wait_ge(m["u2_step"], t.n + 1)
                    pool.tensor_tensor(u2[:, t.s4], u2[:, t.s4], sh2r[:], ALU.add).then_inc(m["u2_done"], 1)

            pool.wait_ge(m["const_in"], 16 * 7)
            pipeline(pool, step, 3)
            for i in range(4):
                pool.wait_ge(scattered[i], 32 * (NT // 4))

        @block.vector
        def _(dve):
            dve.sem_inc(m["mix_used"], 4)
            dve.sem_inc(m["r1_done"], 1)
            dve.sem_inc(m["rank_used"], 1)
            for i in range(2):
                dve.wait_ge(m["w_hi_done"], i + 1)
                part = (slice(None), slice(i * KD // 2, (i + 1) * KD // 2))
                dve.tensor_tensor(w_lo[part], w_raw[:], f32(w_hi[part]), ALU.subtract).then_inc(m["w_lo_done"], 1)
            dve.wait_ge(m["const_in"], 16 * 7)
            dve.wait_ge(m["const_done"], 1)

            def norm(t):
                ch = Chain(dve, m["a_step"], A_OPS * t.n)
                dve.wait_ge(m["mix_done"], t.n + 3)
                for n in range(2):
                    w = slice(n * NB, (n + 1) * NB)
                    dve.tensor_tensor(y[:, w], p_mix[:, t.s2, n], g1r[:, w], ALU.mult).then_inc(m["mix_used"], 1)
                dve.wait_ge(m["mix_used"], 2 * t.n + 6)
                dve.wait_ge(x_in[t.s2], 16 * t.half + 16)
                ch.link(dve.scalar_tensor_tensor(out=y[:], in0=xt[:, t.s2], scalar=ALPHA, in1=y[:], op0=ALU.mult, op1=ALU.add))
                for n in range(2):
                    ch.link(dve.bn_stats(stats[:, n], y[:, n * NB:(n + 1) * NB]), mark=marks["dve"] if n == 1 else None)
                dve.bn_aggr(mv[:], stats[:].rearrange("p a b -> p (a b)")).then_inc(m["var_done"], 1)

            def affine(t):
                ch = Chain(dve, m["c_step"], C_OPS * t.n)
                dve.wait_ge(m["rstd_done"], t.n + 1)
                dve.wait_ge(m["var_done"], t.n + 1)
                dve.wait_ge(x1_stored[t.s2], 16 * t.half + 16)
                dve.wait_ge(m["u2_done"], t.n + 1)
                ch.link(dve.tensor_scalar(x1t[:, t.s2], y[:], mv[:, 0:1], rstd[:], ALU.subtract, ALU.mult))
                ch.link(dve.tensor_tensor(x1t[:, t.s2], x1t[:, t.s2], ln_g[:], ALU.mult))
                dve.tensor_tensor(x1t[:, t.s2], x1t[:, t.s2], ln_b[:], ALU.add).then_inc(m["x1_done"], 1)

            def choose(t):
                ch = Chain(dve, m["r1_step"], R1_OPS * t.n)
                dve.wait_ge(m["aff_done"], t.n + 2)
                ch.link(dve.tensor_tensor(sel[:], aff[:], br[:], ALU.add))
                by_group = sel[:].rearrange("p (g e) -> p g e", g=G)
                ch.link(dve.tensor_tensor(pairs[:], by_group.unsqueeze(3).to_broadcast([P, G, EG, EG]),
                                          by_group.unsqueeze(2).to_broadcast([P, G, EG, EG]), ALU.add))
                ch.link(dve.tensor_tensor(pairs[:], pairs[:], no_twin[:], ALU.add))
                ch.link(dve.tensor_reduce(g_score[:], pairs[:].rearrange("p g a b -> p g (a b)"), AX.X, ALU.max))
                ch.link(dve.tensor_reduce(top[:], g_score[:], AX.X, ALU.max))
                ch.link(dve.scalar_tensor_tensor(out=g_key[:], in0=g_score[:], scalar=top[:], in1=down[:, 0:G],
                                                 op0=ALU.is_ge, op1=ALU.mult))
                ch.link(dve.tensor_reduce(top[:], g_key[:], AX.X, ALU.max))
                ch.link(dve.tensor_scalar(g_off[:], g_key[:], top[:], -BIG, ALU.not_equal, ALU.mult))
                ch.link(dve.tensor_tensor(left[:, 0].rearrange("p (g e) -> p g e", g=G), by_group,
                                          g_off[:].unsqueeze(2).to_broadcast([P, G, EG]), ALU.add))
                for n in range(2):
                    hot = chosen[:, t.s2, n]
                    ch.link(dve.tensor_reduce(top[:], left[:, n], AX.X, ALU.max))
                    ch.link(dve.scalar_tensor_tensor(out=key[:], in0=left[:, n], scalar=top[:], in1=down[:],
                                                     op0=ALU.is_ge, op1=ALU.mult))
                    ch.link(dve.tensor_reduce(top[:], key[:], AX.X, ALU.max))
                    ch.link(dve.tensor_scalar(hot, key[:], top[:], None, ALU.is_equal))
                    if n == 0:
                        ch.link(dve.scalar_tensor_tensor(out=left[:, 1], in0=hot, scalar=-2 * BIG, in1=left[:, 0],
                                                         op0=ALU.mult, op1=ALU.add))
                hots = chosen[:, t.s2]
                ch.link(dve.tensor_tensor(picked[:], hots, aff[:].unsqueeze(1).to_broadcast([P, 2, E]), ALU.mult))
                ch.link(dve.tensor_reduce(gates[:], picked[:], AX.X, ALU.add))
                ch.link(dve.tensor_reduce(g_sum[:], gates[:], AX.X, ALU.add))
                ch.link(dve.tensor_copy(all_chosen[:, bass.ds(t.n, 1)].rearrange("p a n e -> p (a n) e"), hots))
                assert ch.n == R1_OPS, ch.n
                dve.reciprocal(g_sum[:], g_sum[:]).then_inc(m["recip_done"], 1)
                dve.wait_ge(m["recip_done"], t.n + 1)
                dve.tensor_scalar(gate_w[:, bass.ds(2 * t.n, 2)], gates[:], g_sum[:], None, ALU.mult)
                dve.tensor_tensor(both[:, t.s2], hots[:, 0], hots[:, 1], ALU.add).then_inc(m["both_done"], 1)
                dve.wait_ge(m["both_done"], t.n + 1)
                dve.tensor_tensor(seen[:, 1 - t.s2], seen[:, t.s2], both[:, t.s2], ALU.add).then_inc(m["r1_done"], 1)

            def put(t):
                ch = Chain(dve, m["r2_step"], R2_OPS * t.n)
                dve.wait_ge(m["ranked"], t.n + 1)
                dve.tensor_tensor(place[:], p_r[:, 1, 0:E], base[:], ALU.add).then_inc(m["rank_used"], 1)
                dve.wait_ge(m["rank_used"], t.n + 2)
                ch.link(dve.tensor_tensor(at[:], chosen[:, t.s2], place[:].unsqueeze(1).to_broadcast([P, 2, E]), ALU.mult))
                ch.link(dve.tensor_reduce(dest_f[:], at[:], AX.X, ALU.add))
                if (t + -2).live:
                    dve.wait_ge(scattered[(t + -2).s4], 32 * (t + -2).quarter + 32)
                ch.link(dve.tensor_copy(all_dest[:, bass.ds(2 * t.n, 2)], dest_f[:]))
                dve.tensor_copy(dest_now[:, t.s2], dest_f[:]).then_inc(m["dest_done"], 1)

            def step(t):
                if t.live:
                    norm(t)
                if (t + -2).live:
                    choose(t + -2)
                if (t + -3).live:
                    put(t + -3)
                if t.live:
                    affine(t)

            pipeline(dve, step, 3)
            ch = Chain(dve, m["tail_step"], 0)
            dve.wait_ge(m["ranked"], NT + 1)
            ch.link(dve.tensor_copy(n_rows[:], p_r[:, 1, 0:E]))
            ch.link(dve.tensor_tensor(tab_f[:], n_rows[:], base[:], ALU.add))
            ch.link(dve.tensor_copy(table[:, 2], tab_f[:]))
            ch.link(dve.tensor_scalar(tab_f[:], n_rows[:], float(P - 1), None, ALU.add))
            ch.link(dve.tensor_copy(tab_i[:], tab_f[:]))
            ch.link(dve.tensor_scalar(n_blk[:], tab_i[:], 7, None, ALU.logical_shift_right))
            ch.link(dve.tensor_copy(n_rows[:], n_blk[:]))
            ch.link(dve.tensor_tensor_scan(tab_f[:], ones[:, 0:E], n_rows[:], 0.0, ALU.mult, ALU.add))
            ch.link(dve.tensor_copy(table[:, 1], tab_f[:]))
            ch.link(dve.tensor_scalar(tab_l[:], tab_f[:], -1.0, 0.0, ALU.add, ALU.max))
            ch.link(dve.tensor_copy(table[:, 3], tab_l[:]))
            ch.link(dve.tensor_tensor(n_rows[:], tab_f[:], n_rows[:], ALU.subtract))
            ch.link(dve.tensor_copy(table[:, 0], n_rows[:]))
            ch.link(dve.scalar_tensor_tensor(out=shift[:], in0=n_rows[:], scalar=float(P), in1=base[:], op0=ALU.mult,
                                             op1=ALU.subtract))
            ch.link(dve.tensor_tensor(all_at[:], all_chosen[:].rearrange("p t n e -> p (t n) e"),
                                      shift[:].unsqueeze(1).to_broadcast([P, 2 * NT, E]), ALU.mult))
            ch.link(dve.tensor_reduce(moved[:], all_at[:], AX.X, ALU.add))
            dve.tensor_tensor(dest[:], all_dest[:], moved[:], ALU.add)


def experts(nc, used, keep, w_gate, w_up, w_down, rows, results):
    ident, table, marks = keep["ident"], keep["table"], keep["marks"]
    CHUNKS = KD + KF
    PIECE = 2
    PIECES = CHUNKS // PIECE
    with ExitStack() as ctx:
        s = Scope(nc, ctx, "moe", used)
        gu_raw, dn_raw = s.sb("gu_raw", [P, KD, 2, FF]), s.sb("dn_raw", [P, KF, D])
        gu_hi, gu_lo = s.sb("gu_hi", [P, KD, 2, FF], F32R), s.sb("gu_lo", [P, KD, 2, FF], F32R)
        dn_hi, dn_lo = s.sb("dn_hi", [P, KF, D], F32R), s.sb("dn_lo", [P, KF, D], F32R)
        x_raw = s.sb("x_raw", [P, D])
        x_hi, x_lo = s.sb("x_hi", [P, KD, P], F32R), s.sb("x_lo", [P, KD, P], F32R)
        act_g, h = s.sb("act_g", [P, FF]), s.sb("h", [P, FF])
        h_hi, h_lo = s.sb("h_hi", [P, KF, P], F32R), s.sb("h_lo", [P, KF, P], F32R)
        y = s.sb("y", [P, D])
        zeros = s.sb("zeros", [P, D])
        p_gu, p_y = s.ps("p_gu", [P, 2, FF]), s.ps("p_y", [P, 2, NB])
        p_x, p_h = s.ps("p_x", [P, 2, NB]), s.ps("p_h", [P, 2, NB])
        names = ("hi_done", "lo_done", "x_in", "x_turned", "x_hi_done", "x_lo_done", "gu_used", "dn_used",
                 "silu_done", "h_done", "h_turned", "h_hi_done", "h_lo_done", "y_out", "y_stored", "zeros_set",
                 "tails_written", "unused_filled")
        m = {n: s.sem(n) for n in names}
        piece_in = [s.sem(f"piece_in{i}") for i in range(PIECES)]
        block = ctx.enter_context(nc.Block())

        def span(eng, e):
            first = eng.value_load(table[0:1, 0, bass.ds(e, 1)], min_val=0, max_val=BLOCKS)
            end = eng.value_load(table[0:1, 1, bass.ds(e, 1)], min_val=0, max_val=BLOCKS)
            return first, end

        def chunk(c):
            if c < KD:
                return tuple(w[:, c].rearrange("p g f -> p (g f)") for w in (gu_raw, gu_hi, gu_lo))
            return tuple(w[:, c - KD] for w in (dn_raw, dn_hi, dn_lo))

        def row_of(shifted):
            return nc.s_assert_within(shifted - BLOCKS * P, 0, E * CAP, skip_runtime_bounds_check_because=
                                      "a block of an expert lies in the expert's region")

        def expert_blocks(eng, e, run_block, split, last):
            first, end = span(eng, e)
            with eng.If(end > first + 1):
                with eng.Fori(first, end - 1) as b:
                    run_block(b, None)
            with eng.If(end > first):
                run_block(eng.value_load(table[0:1, 3, bass.ds(e, 1)], min_val=0, max_val=BLOCKS - 1),
                          None if last else e + 1)
            if not last:
                with eng.If(end == first):
                    split(e + 1, end, range(CHUNKS))

        @block.sync
        def _(sp):
            def load_weights(e, first=False):
                for i in range(PIECES):
                    a, b = i * PIECE, (i + 1) * PIECE
                    if not first:
                        sp.wait_ge(m["lo_done"], (e - 1) * CHUNKS + b)
                    if a < KD:
                        for g, w in enumerate((w_gate, w_up)):
                            sp.dma_start(gu_raw[:, a:b, g], w.rearrange("l e (k p) f -> (l e) p k f", p=P)[
                                bass.ds(e, 1), :, a:b].rearrange("e p k f -> p (e k) f")).then_inc(piece_in[i], 16)
                    else:
                        sp.dma_start(dn_raw[:, a - KD:b - KD], w_down.rearrange("l e (k p) d -> (l e) p k d", p=P)[
                            bass.ds(e, 1), :, a - KD:b - KD].rearrange("e p k d -> p (e k) d")
                                     ).then_inc(piece_in[i], 16)

            def load_x(b, row):
                wait_apart(sp, marks["sp"], m["x_turned"], b + 1)
                sp.dma_start(x_raw[:], rows[bass.ds(row, P), :]).then_inc(m["x_in"], 16)

            def load_blocks(e, at_first=False, last=False):
                first, end = span(sp, e)
                shift = sp.snap(e * CAP - first * P + BLOCKS * P)
                

                def row(b):
                    return row_of(sp.snap(b * P + shift))

                wait_apart(sp, marks["sp"], m["tails_written"], e * 16 + 16)
                with sp.If(end > first):
                    load_x(first, row(first))
                if at_first:
                    load_weights(e, True)
                with sp.If(end > first + 1):
                    load_x(first + 1, row(first + 1))
                if not last:
                    load_weights(e + 1)
                with sp.If(end > first + 2):
                    with sp.Fori(first + 2, end) as b:
                        load_x(b, row(b))
                return end

            load_blocks(0, at_first=True)
            with sp.Fori(1, E - 1) as e:
                load_blocks(e)
            end = load_blocks(E - 1, last=True)
            sp.wait_ge(m["tails_written"], 16 * E + 16)
            load_x(end, E * CAP)
            with sp.Fori(end, BLOCKS) as b:
                sp.dma_start(results[bass.ds(b * P, P), :], zeros[:]).then_inc(m["unused_filled"], 16)
            with sp.Fori(0, end):
                sp.sem_inc(m["unused_filled"], 16)
            sp.wait_ge(m["unused_filled"], BLOCKS * 16)

        @block.gpsimd
        def _(pool):
            pool.memset(zeros[:], 0.0).then_inc(m["zeros_set"], 1)
            pool.wait_ge(m["zeros_set"], 1)
            with pool.Fori(0, E) as e:
                at_row = pool.value_load(table[0:1, 2, bass.ds(e, 1)], min_val=0, max_val=E * CAP)
                pool.dma_start(rows[bass.ds(at_row, P), :], zeros[:]).then_inc(m["tails_written"], 16)
                pool.wait_ge(m["tails_written"], 16 * e + 16)
            pool.dma_start(rows[E * CAP:E * CAP + P, :], zeros[:]).then_inc(m["tails_written"], 16)

        @block.tensor
        def _(pe):
            pe.sem_inc(m["gu_used"], KD)
            pe.sem_inc(m["dn_used"], KF)
            pe.sem_inc(m["x_turned"], 1)

            def turn_x(b):
                pe.wait_ge(m["x_in"], 16 * b + 16)
                for k in range(KD):
                    mm = pe.transpose(p_x[:, k // 4, k % 4 * P:(k % 4 + 1) * P], x_raw[:, k * P:(k + 1) * P], ident[:])
                mm.then_inc(m["x_turned"], 1)

            turn_x(0)
            with pe.Fori(0, E) as e:
                first, end = span(pe, e)
                with pe.If(end > first):
                    with pe.Fori(first, end) as b:
                        pe.wait_ge(m["x_lo_done"], b + 1)
                        for k in range(KD):
                            pe.wait_ge(m["lo_done"], e * CHUNKS + (k + 1))
                            for g in range(2):
                                mm = product(pe, p_gu[:, g], ((x_hi[:, k], gu_hi[:, k, g]), (x_hi[:, k], gu_lo[:, k, g]),
                                                              (x_lo[:, k], gu_hi[:, k, g])), k == 0, k == KD - 1)
                            mm.then_inc(m["gu_used"], 1)
                        turn_x(b + 1)
                        for i in range(2):
                            pe.wait_ge(m["h_done"], 2 * b + (i + 1))
                            for j in range(2):
                                f = 2 * i + j
                                mm = pe.transpose(p_h[:, i, j * P:(j + 1) * P], h[:, f * P:(f + 1) * P], ident[:])
                            mm.then_inc(m["h_turned"], 1)
                        pe.wait_ge(m["y_out"], 2 * b + 2)
                        for k in range(KF):
                            pe.wait_ge(m["h_lo_done"], 2 * b + (k // 2 + 1))
                            pe.wait_ge(m["lo_done"], e * CHUNKS + (KD + k + 1))
                            for n in range(2):
                                w = slice(n * NB, (n + 1) * NB)
                                mm = product(pe, p_y[:, n], ((h_hi[:, k], dn_hi[:, k, w]), (h_hi[:, k], dn_lo[:, k, w]),
                                                             (h_lo[:, k], dn_hi[:, k, w])), k == 0, k == KF - 1)
                            mm.then_inc(m["dn_used"], 1)

        @block.scalar
        def _(act):
            act.sem_inc(m["y_out"], 2)
            act.sem_inc(m["y_stored"], 16)

            def split(e, first, chunks):
                for c in chunks:
                    raw, hi, lo = chunk(c)
                    if c % PIECE == 0:
                        dmas = 32 if c < KD else 16
                        act.wait_ge(piece_in[c // PIECE], dmas * e + dmas)
                    if first is not None:
                        if c < KD:
                            act.wait_ge(m["gu_used"], first * KD + (c + 1))
                        else:
                            act.wait_ge(m["dn_used"], first * KF + (c - KD + 1))
                    act.activation(hi, raw, ACT.Copy).then_inc(m["hi_done"], 1)

            def high_x(b):
                act.wait_ge(m["x_turned"], b + 2)
                for n in range(2):
                    act.activation(x_hi[:, 4 * n:4 * n + 4], p_x[:, n].rearrange("p (k t) -> p k t", t=P), ACT.Copy
                                   ).then_inc(m["x_hi_done"], 1)

            def run_block(b, e_next):
                act.wait_ge(m["gu_used"], b * KD + 2 * KD)
                for i in range(2):
                    act.activation(act_g[:, i * 256:(i + 1) * 256], p_gu[:, 0, i * 256:(i + 1) * 256], ACT.Silu
                                   ).then_inc(m["silu_done"], 1)
                for i in range(2):
                    act.wait_ge(m["h_turned"], 2 * b + (i + 1))
                    act.activation(h_hi[:, 2 * i:2 * i + 2], p_h[:, i, 0:2 * P].rearrange("p (k t) -> p k t", t=P),
                                   ACT.Copy).then_inc(m["h_hi_done"], 1)
                high_x(b + 1)
                if e_next is not None:
                    split(e_next, b + 1, range(KD))
                act.wait_ge(m["dn_used"], b * KF + 2 * KF)
                act.wait_ge(m["y_stored"], 16 * b + 16)
                for n in range(2):
                    act.activation(y[:, n * NB:(n + 1) * NB], p_y[:, n], ACT.Copy).then_inc(m["y_out"], 1)
                act.wait_ge(m["y_out"], 2 * b + 4)
                act.dma_start(results[bass.ds(b * P, P), :], y[:]).then_inc(m["y_stored"], 16)
                if e_next is not None:
                    split(e_next, b + 1, range(KD, CHUNKS))

            high_x(0)
            split(0, None, range(CHUNKS))
            with act.Fori(0, E - 1) as e:
                expert_blocks(act, e, run_block, split, False)
            expert_blocks(act, E - 1, run_block, split, True)
            total = act.value_load(table[0:1, 1, E - 1:E], min_val=0, max_val=BLOCKS)
            wait_apart(act, marks["act"], m["y_stored"], total * 16 + 16)

        @block.vector
        def _(dve):
            def split(e, first, chunks):
                for c in chunks:
                    raw, hi, lo = chunk(c)
                    dve.wait_ge(m["hi_done"], e * CHUNKS + (c + 1))
                    dve.tensor_tensor(lo, raw, f32(hi), ALU.subtract).then_inc(m["lo_done"], 1)

            def low_x(b):
                for n in range(2):
                    dve.wait_ge(m["x_hi_done"], 2 * b + (n + 1))
                    part = (slice(None), slice(4 * n, 4 * n + 4))
                    ins = dve.tensor_tensor(x_lo[part], p_x[:, n].rearrange("p (k t) -> p k t", t=P), f32(x_hi[part]),
                                            ALU.subtract)
                ins.then_inc(m["x_lo_done"], 1)

            def run_block(b, e_next):
                for i in range(2):
                    w = slice(i * 256, (i + 1) * 256)
                    dve.wait_ge(m["silu_done"], 2 * b + (i + 1))
                    dve.tensor_tensor(h[:, w], p_gu[:, 1, w], act_g[:, w], ALU.mult).then_inc(m["h_done"], 1)
                for i in range(2):
                    part = (slice(None), slice(2 * i, 2 * i + 2))
                    dve.wait_ge(m["h_hi_done"], 2 * b + (i + 1))
                    dve.tensor_tensor(h_lo[part], p_h[:, i, 0:2 * P].rearrange("p (k t) -> p k t", t=P),
                                      f32(h_hi[part]), ALU.subtract).then_inc(m["h_lo_done"], 1)
                low_x(b + 1)
                if e_next is not None:
                    split(e_next, None, range(CHUNKS))

            low_x(0)
            split(0, None, range(CHUNKS))
            with dve.Fori(0, E - 1) as e:
                expert_blocks(dve, e, run_block, split, False)
            expert_blocks(dve, E - 1, run_block, split, True)


def combine_norm(nc, used, keep, results, x1, mod_rows, ln2_g, ln2_b, out):
    dest, gate_w, marks = keep["dest"], keep["gate_w"], keep["marks"]
    A_OPS = 5
    with ExitStack() as ctx:
        s = Scope(nc, ctx, "fin", used)
        g2r, ln_g, ln_b = (s.sb(n, [P, D]) for n in ("g2r", "ln_g", "ln_b"))
        idx = s.sb("idx", [P, 2, 2], U32)
        yy, xt = s.sb("yy", [P, 2, 2, D]), s.sb("xt", [P, 2, D])
        first, y, res = s.sb("first", [P, 2, D]), s.sb("y", [P, 2, D]), s.sb("res", [P, 2, D])
        stats, mv, var, rstd = s.sb("stats", [P, 2, 6]), s.sb("mv", [P, 2]), s.sb("var", [P, 1]), s.sb("rstd", [P, 1])
        minus_half = s.sb("minus_half", [P, 1])
        names = ("const_in", "half_set", "idx_done", "first_done", "a_step", "var_done", "var_step", "rstd_done",
                 "normed", "scaled", "res_done")
        m = {n: s.sem(n) for n in names}
        y_in, x_in, stored = ([s.sem(f"{n}{i}") for i in range(2)] for n in ("y_in", "x_in", "stored"))
        block = ctx.enter_context(nc.Block())

        @block.sync
        def _(sp):
            for dst, src in ((g2r, mod_rows[G2 * P:G2 * P + D].rearrange("(a d) -> a d", a=1).to_broadcast([P, D])),
                             (ln_g, ln2_g.to_broadcast([P, D])), (ln_b, ln2_b.to_broadcast([P, D]))):
                sp.dma_start(dst[:], src).then_inc(m["const_in"], 16)

            with sp.Fori(0, NT // 2) as i:
                for par in range(2):
                    t = 2 * i + par
                    sp.wait_ge(m["normed"], t + 1)
                    sp.dma_start(xt[:, par], x1[bass.ds(t * P, P), :]).then_inc(x_in[par], 16)

        @block.gpsimd
        def _(pool):
            pool.memset(minus_half[:], -0.5).then_inc(m["half_set"], 1)
            pool.wait_ge(m["const_in"], 48)
            pool.wait_ge(m["half_set"], 1)

            def gather(t, par):
                wait_apart(pool, marks["pool"], m["normed"], t + 1)
                pool.tensor_copy(idx[:, par], dest[:, bass.ds(2 * t, 2)]).then_inc(m["idx_done"], 1)
                wait_apart(pool, marks["pool"], m["idx_done"], t + 1)
                for k in range(2):
                    pool.indirect_dma_start(out=yy[:, par, k], out_offset=None, in_=results, in_offset=bass.IndirectOffsetOnAxis(
                        ap=idx[:, par, k:k + 1], axis=0)).then_inc(y_in[par], 16)

            def finish(t, par):
                wait_apart(pool, marks["pool"], m["var_done"], t + 1)
                pool.tensor_scalar(var[:], mv[:, 1:2], EPS, None, ALU.add).then_inc(m["var_step"], 1)
                pool.wait_ge(m["var_step"], t + 1)
                pool.tensor_tensor(rstd[:], var[:], minus_half[:], ALU.pow).then_inc(m["rstd_done"], 1)
                pool.wait_ge(m["normed"], t + 3)
                pool.tensor_tensor(res[:, par], y[:, par], ln_g[:], ALU.mult).then_inc(m["scaled"], 1)
                pool.wait_ge(m["scaled"], t + 1)
                pool.tensor_tensor(res[:, par], res[:, par], ln_b[:], ALU.add).then_inc(m["res_done"], 1)

            gather(0, 0)
            gather(1, 1)
            with pool.Fori(0, NT // 2 - 1) as i:
                for par in range(2):
                    finish(2 * i + par, par)
                    gather(2 * i + par + 2, par)
            for par in range(2):
                finish(NT - 2 + par, par)

        @block.scalar
        def _(act):
            for i in range(2):
                act.sem_inc(stored[i], 16)

            def weigh(t, par, i):
                act.wait_ge(y_in[par], 32 * i + 32)
                act.wait_ge(m["normed"], t + 1)
                act.activation(first[:, par], yy[:, par, 0], ACT.Copy, scale=gate_w[:, bass.ds(2 * t, 1)]
                               ).then_inc(m["first_done"], 1)

            def store(t, par):
                act.wait_ge(m["res_done"], t + 1)
                act.dma_start(out.rearrange("b t d -> (b t) d")[bass.ds(t * P, P), :], res[:, par]
                              ).then_inc(stored[par], 16)

            weigh(0, 0, 0)
            with act.Fori(0, NT // 2 - 1) as i:
                weigh(2 * i + 1, 1, i)
                store(2 * i, 0)
                weigh(2 * i + 2, 0, i + 1)
                store(2 * i + 1, 1)
            weigh(NT - 1, 1, NT // 2 - 1)
            store(NT - 2, 0)
            store(NT - 1, 1)
            for i in range(2):
                act.wait_ge(stored[i], 16 * (NT // 2 + 1))

        @block.vector
        def _(dve):
            dve.sem_inc(m["normed"], 2)
            dve.wait_ge(m["const_in"], 48)
            with dve.Fori(0, NT // 2) as i:
                for par in range(2):
                    t = 2 * i + par
                    ch = Chain(dve, m["a_step"], A_OPS * t)
                    dve.wait_ge(m["first_done"], t + 1)
                    dve.wait_ge(x_in[par], 16 * i + 16)
                    dve.wait_ge(stored[par], 16 * i + 16)
                    ch.link(dve.scalar_tensor_tensor(out=y[:, par], in0=yy[:, par, 1], scalar=gate_w[:, bass.ds(2 * t + 1, 1)],
                                                     in1=first[:, par], op0=ALU.mult, op1=ALU.add))
                    ch.link(dve.tensor_tensor(y[:, par], y[:, par], g2r[:], ALU.mult))
                    ch.link(dve.scalar_tensor_tensor(out=y[:, par], in0=xt[:, par], scalar=ALPHA, in1=y[:, par],
                                                     op0=ALU.mult, op1=ALU.add))
                    for n in range(2):
                        ch.link(dve.bn_stats(stats[:, n], y[:, par, n * NB:(n + 1) * NB]), mark=marks["dve"] if n == 1 else None)
                    dve.bn_aggr(mv[:], stats[:].rearrange("p a b -> p (a b)")).then_inc(m["var_done"], 1)
                    dve.wait_ge(m["var_done"], t + 1)
                    dve.wait_ge(m["rstd_done"], t + 1)
                    dve.tensor_scalar(y[:, par], y[:, par], mv[:, 0:1], rstd[:], ALU.subtract, ALU.mult
                                      ).then_inc(m["normed"], 1)


def hybrid_layer(nc, x, c, w_ada, b_ada, w_in, w_conv, w_a, w_b, w_o, ln1_g, ln1_b, w_router, b_router, w_gate, w_up,
                 w_down, ln2_g, ln2_b, out):
    def scratch(name, shape):
        return nc.dram_tensor(name, shape, F32, kind="Internal").ap()

    mod_rows = scratch("mod_rows", [6 * D])
    qkv_hi, qkv_lo = scratch("qkv_hi", [3 * AW, S]), scratch("qkv_lo", [3 * AW, S])
    conv_t, gate_t = scratch("conv_t", [CH, S]), scratch("gate_t", [2 * D, S])
    o_t, m_t, x1 = scratch("o_t", [AW, S]), scratch("m_t", [D, S]), scratch("x1", [S, D])
    rows, results = scratch("rows", [E * CAP + P, D]), scratch("results", [BLOCKS * P, D])
    used = []
    with ExitStack() as ctx:
        s = Scope(nc, ctx, "keep", [])
        keep = {
            "ident": s.sb("ident", [P, P]), "mod": s.sb("mod", [P, 6 * KD]), "conv_cols": s.sb("conv_cols", [P, 3 * KC]),
            "dest": s.sb("dest", [P, 2 * NT], U32), "gate_w": s.sb("gate_w", [P, 2 * NT]),
            "table": s.sb("table", [P, 4, E], I32),
            "csilu": s.sb("csilu", [P, KD]),
            "marks": {n: s.sem(f"mark_{n}") for n in ("sp", "act", "pool", "pe", "dve")},
        }
        modulation(nc, used, keep, c, w_ada, b_ada, w_conv)
        with ExitStack() as uctx:
            us = Scope(nc, uctx, "u", [])
            u_hi, u_lo = us.sb("hi", [P, KD, S], F32R), us.sb("lo", [P, KD, S], F32R)
            modulated_input(nc, used, keep, x, u_hi, u_lo)
            input_projection(nc, used, keep, u_hi, u_lo, w_in, qkv_hi, qkv_lo, conv_t, gate_t)
        attention(nc, used, keep, qkv_hi, qkv_lo, w_ada, o_t, mod_rows)
        clear_semaphores(nc, used)
        branch_outputs(nc, used, keep, conv_t, o_t, gate_t, w_a, w_b, m_t)
        mix_norm_route(nc, used, keep, m_t, w_o, x, mod_rows, ln1_g, ln1_b, w_router, b_router, x1, rows, results)
        experts(nc, used, keep, w_gate, w_up, w_down, rows, results)
        combine_norm(nc, used, keep, results, x1, mod_rows, ln2_g, ln2_b, out)


_INS = ["x", "c", "w_ada", "b_ada", "w_in", "w_conv", "w_a", "w_b", "w_o", "ln1_g", "ln1_b", "w_router", "b_router",
        "w_gate", "w_up", "w_down", "ln2_g", "ln2_b"]


def kernel(**inputs):
    import numpy as np
    import concourse.bacc as bacc
    from concourse.bass_utils import run_bass_kernel_spmd

    nc = bacc.Bacc("TRN2", target_bir_lowering=False, num_devices=1)
    arrays, args = {}, []
    for name in _INS:
        a = np.ascontiguousarray(inputs[name])
        arrays[f"in_{name}"] = a
        args.append(nc.dram_tensor(f"in_{name}", a.shape, mybir.dt.from_np(a.dtype), kind="ExternalInput").ap())
    out = nc.dram_tensor("out", (1, S, D), F32, kind="ExternalOutput").ap()
    hybrid_layer(nc, *args, out)
    r = run_bass_kernel_spmd(nc, [arrays], core_ids=[0])
    return r.results[0]["out"]
```

```python
from contextlib import ExitStack

import concourse.bass as bass
from concourse import mybir

F32 = mybir.dt.float32
F32R = mybir.dt.float32r
I32 = mybir.dt.int32
U32 = mybir.dt.uint32
ALU = mybir.AluOpType
ACT = mybir.ActivationFunctionType
AX = mybir.AxisListType

P = 128
NB = 512
D = 1024
S = 2048
KD = D // P
NT = S // P
TB = S // NB
CH = 512
HEADS = 8
HD = 64
AW = HEADS * HD
KC = CH // P
E = 16
G = 4
EG = E // G
FF = 512
KF = FF // P
CAP = S + P
BLOCKS = 2 * S // P + E
EPS = 1e-5
ALPHA = 2.0 ** 0.25
BIG = 1e30

FIRST_MOD = 2 * D // NB

SH1, SC1, G1, SH2, SC2, G2 = (KD * i for i in range(6))


class Scope:

    def __init__(self, nc, ctx, tag, used):
        self.nc, self.ctx, self.tag = nc, ctx, tag
        self.used = used

    def sb(self, name, shape, dt=F32):
        return self.ctx.enter_context(self.nc.sbuf_tensor(f"{self.tag}_{name}", shape, dt))

    def ps(self, name, shape, dt=F32):
        return self.ctx.enter_context(self.nc.psum_tensor(f"{self.tag}_{name}", shape, dt))

    def sem(self, name):
        sem = self.nc.alloc_semaphore(f"{self.tag}_{name}")
        self.used.append(sem)
        return sem


def clear_semaphores(nc, used):
    nc.clear_and_free_semaphores(used)
    used.clear()
    nc.all_engine_barrier()


def f32(ap):
    return ap.bitcast(F32)


def mod_products(pe, out, column, w, csilu):
    for m in range(NB // P):
        for k in range(KD):
            mm = pe.matmul(out[:, column + m:column + m + 1], w[:, k, m * P:(m + 1) * P], csilu[:, k:k + 1],
                           start=k == 0, stop=k == KD - 1, skip_group_check=True)
    return mm


def wait_apart(eng, mark, sem, value):
    eng.wait_ge(sem, value)
    eng.sem_inc(mark, 1)


def product(pe, out, pairs, first, last):
    for n, (a, b) in enumerate(pairs):
        mm = pe.matmul(out, a, b, start=first and n == 0, stop=last and n == len(pairs) - 1,
                       skip_group_check=True)
    return mm


def modulation(nc, used, keep, c, w_ada, b_ada, w_conv):
    ident, mod, conv_cols, csilu = keep["ident"], keep["mod"], keep["conv_cols"], keep["csilu"]
    NJ = 6 * KD
    VR = NJ + KD + 3 * KC
    with ExitStack() as ctx:
        s = Scope(nc, ctx, "ada", used)
        vec = s.sb("vec", [VR, P])
        w = s.sb("w", [P, FIRST_MOD, KD, NB])
        p_vec = s.ps("p_vec", [P, NB])
        p_mod = s.ps("p_mod", [P, NB])
        vec_in, vec_turned, cols_out = s.sem("vec_in"), s.sem("vec_turned"), s.sem("cols_out")
        ident_zero, ident_done = s.sem("ident_zero"), s.sem("ident_done")
        silu_done, mod_summed, mod_done = s.sem("silu_done"), s.sem("mod_summed"), s.sem("mod_done")
        w_in = [s.sem(f"w_in{i}") for i in range(FIRST_MOD)]
        block = ctx.enter_context(nc.Block())
        w_view = w_ada.rearrange("l (k p) (b n) -> (l p) b k n", p=P, n=NB)

        @block.gpsimd
        def _(pool):
            pool.memset(ident[:], 0.0).then_inc(ident_zero, 1)
            pool.wait_ge(ident_zero, 1)
            pool.affine_select(out=ident[:], in_=ident[:], compare_op=ALU.not_equal, fill=1.0, base=0,
                               pattern=[[-1, P]], channel_multiplier=1).then_inc(ident_done, 1)

        @block.sync
        def _(sp):
            sp.dma_start(vec[0:NJ, :], b_ada.rearrange("l (r p) -> (l r) p", p=P)).then_inc(vec_in, 16)
            sp.dma_start(vec[NJ:NJ + KD, :], c.rearrange("b (r p) -> (b r) p", p=P)).then_inc(vec_in, 16)
            sp.dma_start(vec[NJ + KD:VR, :], w_conv.rearrange("l t (r p) -> (l t r) p", p=P)).then_inc(vec_in, 16)
            for i in range(FIRST_MOD):
                sp.dma_start(w[:, i], w_view[:, i]).then_inc(w_in[i], 16)

        @block.tensor
        def _(pe):
            pe.wait_ge(vec_in, 48)
            pe.wait_ge(ident_done, 1)
            pe.transpose(p_vec[:, 0:VR], vec[:], ident[0:VR, 0:VR]).then_inc(vec_turned, 1)
            pe.wait_ge(silu_done, 1)
            for i in range(FIRST_MOD):
                pe.wait_ge(w_in[i], 16)
                mm = mod_products(pe, p_mod, i * NB // P, w[:, i], csilu)
            mm.then_inc(mod_summed, 1)

        @block.scalar
        def _(act):
            act.wait_ge(vec_turned, 1)
            act.activation(csilu[:], p_vec[:, NJ:NJ + KD], ACT.Silu).then_inc(silu_done, 1)

        @block.vector
        def _(dve):
            dve.wait_ge(silu_done, 1)
            dve.tensor_copy(mod[:], p_vec[:, 0:NJ]).then_inc(cols_out, 1)
            dve.tensor_copy(conv_cols[:], p_vec[:, NJ + KD:VR]).then_inc(cols_out, 1)
            dve.wait_ge(cols_out, 2)
            dve.wait_ge(mod_summed, 1)
            n = FIRST_MOD * NB // P
            dve.tensor_tensor(mod[:, 0:n], mod[:, 0:n], p_mod[:, 0:n], ALU.add).then_inc(mod_done, 1)
            dve.wait_ge(mod_done, 1)
            dve.tensor_scalar(mod[:, SC1:SC1 + KD], mod[:, SC1:SC1 + KD], 1.0, None, ALU.add)


def modulated_input(nc, used, keep, x, u_hi, u_lo):
    ident, mod = keep["ident"], keep["mod"]
    with ExitStack() as ctx:
        s = Scope(nc, ctx, "u", used)
        xr = s.sb("x", [P, 2, NB // P, D])
        uf = s.sb("uf", [P, 2, NB])
        p_t = s.ps("p_t", [P, 4, NB])
        x_in = [s.sem(f"x_in{i}") for i in range(2)]
        turned, affine, hi_done, lo_done = (s.sem(n) for n in ("turned", "affine", "hi_done", "lo_done"))
        block = ctx.enter_context(nc.Block())
        x_view = x.rearrange("b (g t p) d -> (b p) g t d", p=P, t=NB // P)

        @block.sync
        def _(sp):
            for g in range(TB):
                if g >= 2:
                    sp.wait_ge(turned, KD * (g - 1))
                sp.dma_start(xr[:, g % 2], x_view[:, g]).then_inc(x_in[g % 2], 16)

        @block.tensor
        def _(pe):
            for g in range(TB):
                pe.wait_ge(x_in[g % 2], 16 * (g // 2 + 1))
                for k in range(KD):
                    n = g * KD + k
                    if n >= 4:
                        pe.wait_ge(affine, n - 3)
                    for t in range(NB // P):
                        mm = pe.transpose(p_t[:, n % 4, t * P:(t + 1) * P], xr[:, g % 2, t, k * P:(k + 1) * P], ident[:])
                    mm.then_inc(turned, 1)

        @block.scalar
        def _(act):
            for n in range(TB * KD):
                k = n % KD
                act.wait_ge(turned, n + 1)
                if n >= 2:
                    act.wait_ge(lo_done, n - 1)
                act.activation(uf[:, n % 2], p_t[:, n % 4], ACT.Identity, bias=mod[:, SH1 + k:SH1 + k + 1],
                               scale=mod[:, SC1 + k:SC1 + k + 1]).then_inc(affine, 1)

        @block.vector
        def _(dve):
            for n in range(TB * KD):
                g, k = divmod(n, KD)
                dve.wait_ge(affine, n + 1)
                dve.tensor_copy(u_hi[:, k, g * NB:(g + 1) * NB], uf[:, n % 2]).then_inc(hi_done, 1)

        @block.gpsimd
        def _(pool):
            for n in range(TB * KD):
                g, k = divmod(n, KD)
                pool.wait_ge(hi_done, n + 1)
                pool.tensor_tensor(u_lo[:, k, g * NB:(g + 1) * NB], uf[:, n % 2],
                                   f32(u_hi[:, k, g * NB:(g + 1) * NB]), ALU.subtract).then_inc(lo_done, 1)


def input_projection(nc, used, keep, u_hi, u_lo, w_in, qkv_hi, qkv_lo, conv_t, gate_t):
    conv_cols = keep["conv_cols"]
    with ExitStack() as ctx:
        s = Scope(nc, ctx, "in", used)
        raw = s.sb("raw", [P, 2, KD, P])
        w_hi = s.sb("w_hi", [P, 2, KD, P], F32R)
        w_lo = s.sb("w_lo", [P, 2, KD, P], F32R)
        stage = s.sb("stage", [P, 2, S])
        cx = s.sb("cx", [P, S])
        gated = s.sb("gated", [P, S + 2])
        conv = s.sb("conv", [P, S])
        acc = s.ps("acc", [P, 2, TB, NB])
        raw_in = [s.sem(f"raw_in{i}") for i in range(2)]
        stored = [s.sem(f"stored{i}") for i in range(2)]
        hi_done, lo_done, pe_done = s.sem("hi_done"), s.sem("lo_done"), s.sem("pe_done")
        act_out, dve_out, conv_step, padded = (s.sem(n) for n in ("act_out", "dve_out", "conv_step", "padded"))
        block = ctx.enter_context(nc.Block())
        w_view = w_in.rearrange("l (k p) n -> (l p) k n", p=P)
        QKV, CONV, GATES = 3 * AW // P, 3 * KC, 2 * D // P
        TILES = QKV + CONV + GATES
        FIRST_G = QKV + CONV
        c_cb, c_cc, c_cx, c_q, c_ga = 0, CH, 2 * CH, 3 * CH, 3 * CH + 3 * AW

        def bank(t):
            return slice(t * NB, (t + 1) * NB)

        @block.sync
        def _(sp):
            def load(col, par, t, first=False):
                if not first:
                    sp.wait_ge(lo_done, t - 1)
                sp.dma_start(raw[:, par], w_view[:, :, bass.ds(col, P)]).then_inc(raw_in[par], 16)

            load(c_q, 0, 0, True)
            load(c_q + P, 1, 1, True)

            def store_qkv(t):
                sp.wait_ge(act_out, t + 1)
                sp.dma_start(qkv_hi[bass.ds(t * P, P), :], stage[:, 0]).then_inc(stored[0], 16)
                sp.wait_ge(dve_out, t + 1)
                sp.dma_start(qkv_lo[bass.ds(t * P, P), :], stage[:, 1]).then_inc(stored[1], 16)

            with sp.Fori(0, QKV // 2 - 1) as i:
                for par in range(2):
                    t = 2 * i + par
                    load(c_q + (t + 2) * P, par, t + 2)
                    store_qkv(t)
            load(c_cx, 0, QKV)
            store_qkv(QKV - 2)
            load(c_cc, 1, QKV + 1)
            store_qkv(QKV - 1)

            def conv_round(j, half, last=False):
                t = QKV + 3 * j
                base = 3 * half
                load(c_cb + j * P, (base + 2) % 2, t + 2)
                nxt = (c_ga, c_ga + P) if last else (c_cx + (j + 1) * P, c_cc + (j + 1) * P)
                load(nxt[0], (base + 3) % 2, t + 3)
                load(nxt[1], (base + 4) % 2, t + 4)
                sp.wait_ge(dve_out, QKV + 2 * j + 2)
                sp.dma_start(conv_t[bass.ds(j * P, P), :], stage[:, half]).then_inc(stored[half], 16)

            with sp.Fori(0, KC // 2 - 1) as i:
                for half in range(2):
                    conv_round(2 * i + half, half)
            conv_round(KC - 2, 0)
            conv_round(KC - 1, 1, last=True)

            def store_gate(n, par):
                sp.wait_ge(act_out, QKV + KC + n + 1)
                sp.dma_start(gate_t[bass.ds(n * P, P), :], stage[:, par]).then_inc(stored[par], 16)

            with sp.Fori(0, GATES // 2 - 1) as i:
                for par in range(2):
                    n = 2 * i + par
                    load(c_ga + (n + 2) * P, par, FIRST_G + n + 2)
                    store_gate(n, par)
            for par in range(2):
                store_gate(GATES - 2 + par, par)
            for par in range(2):
                sp.wait_ge(stored[par], 16 * (QKV + (KC + GATES) // 2))

        @block.tensor
        def _(pe):
            def tile(t, par):
                pe.wait_ge(lo_done, t + 1)
                for k in range(KD):
                    for w, us in ((w_hi, (u_hi, u_lo)), (w_lo, (u_hi,))):
                        for n, u in enumerate(us):
                            for tb in range(TB):
                                mm = pe.matmul(acc[:, par, tb], w[:, par, k], u[:, k, bank(tb)],
                                               start=k == 0 and w is w_hi and n == 0,
                                               stop=k == KD - 1 and w is w_lo, skip_group_check=True)
                mm.then_inc(pe_done, 1)

            tile(0, 0)
            tile(1, 1)
            with pe.Fori(1, QKV // 2) as i:
                for par in range(2):
                    pe.wait_ge(act_out, 2 * i + par - 1)
                    pe.wait_ge(dve_out, 2 * i + par - 1)
                    tile(2 * i + par, par)
            with pe.Fori(0, KC // 2) as i:
                for half in range(2):
                    j = 2 * i + half
                    t = QKV + 3 * j
                    pe.wait_ge(act_out, QKV - 1)
                    pe.wait_ge(dve_out, QKV - 1 + 2 * j)
                    tile(t, (3 * half) % 2)
                    pe.wait_ge(act_out, QKV)
                    pe.wait_ge(dve_out, QKV + 2 * j)
                    tile(t + 1, (3 * half + 1) % 2)
                    pe.wait_ge(act_out, QKV + j + 1)
                    tile(t + 2, (3 * half + 2) % 2)
            pe.wait_ge(dve_out, QKV + 2 * KC)
            with pe.Fori(0, GATES // 2) as i:
                for par in range(2):
                    n = 2 * i + par
                    pe.wait_ge(act_out, QKV + KC - 1 + n)
                    tile(FIRST_G + n, par)

        @block.scalar
        def _(act):
            def high(t, par, rnd, first=False):
                act.wait_ge(raw_in[par], 16 * rnd + 16)
                if not first:
                    act.wait_ge(pe_done, t - 1)
                act.activation(w_hi[:, par], raw[:, par], ACT.Copy).then_inc(hi_done, 1)

            def out_qkv(t, par, first=False):
                act.wait_ge(pe_done, t + 1)
                if not first:
                    act.wait_ge(stored[0], 16 * t)
                    act.wait_ge(stored[1], 16 * t)
                for tb in range(TB):
                    ins = act.activation(stage[:, 0, bank(tb)].bitcast(F32R), acc[:, par, tb], ACT.Copy)
                ins.then_inc(act_out, 1)

            high(0, 0, 0, True)
            high(1, 1, 0, True)
            out_qkv(0, 0, True)
            high(2, 0, 1)
            out_qkv(1, 1)
            with act.Fori(1, QKV // 2) as i:
                high(2 * i + 1, 1, i)
                out_qkv(2 * i, 0)
                high(2 * i + 2, 0, i + 1)
                out_qkv(2 * i + 1, 1)
            with act.Fori(0, KC // 2) as i:
                for half in range(2):
                    j = 2 * i + half
                    t = QKV + 3 * j
                    b = 3 * half
                    rnd = QKV // 2 + 3 * i
                    high(t + 1, (b + 1) % 2, rnd + (b + 1) // 2)
                    act.wait_ge(pe_done, t + 1)
                    act.wait_ge(dve_out, QKV - 1 + 2 * j)
                    for tb in range(TB):
                        ins = act.activation(cx[:, bank(tb)], acc[:, b % 2, tb], ACT.Copy)
                    ins.then_inc(act_out, 1)
                    high(t + 2, (b + 2) % 2, rnd + (b + 2) // 2)
                    high(t + 3, (b + 3) % 2, rnd + (b + 3) // 2)

            def out_gate(n, par, rnd):
                act.wait_ge(pe_done, FIRST_G + n + 1)
                act.wait_ge(stored[par], 16 * (rnd + QKV + KC // 2))
                for tb in range(TB):
                    ins = act.activation(stage[:, par, bank(tb)], acc[:, par, tb], ACT.Sigmoid)
                ins.then_inc(act_out, 1)

            with act.Fori(0, GATES // 2 - 1) as i:
                for par in range(2):
                    n = 2 * i + par
                    high(FIRST_G + n + 1, 1 - par, FIRST_G // 2 + i + par)
                    out_gate(n, par, i)
            n = GATES - 2
            high(FIRST_G + n + 1, 1, FIRST_G // 2 + n // 2)
            out_gate(n, 0, n // 2)
            out_gate(n + 1, 1, n // 2)

        @block.vector
        def _(dve):
            dve.memset(gated[:, 0:2], 0.0).then_inc(padded, 1)

            def low(t, par):
                dve.wait_ge(hi_done, t + 1)
                dve.tensor_tensor(w_lo[:, par], raw[:, par], f32(w_hi[:, par]), ALU.subtract).then_inc(lo_done, 1)

            def out_qkv(t, par):
                dve.wait_ge(act_out, t + 1)
                for tb in range(TB):
                    ins = dve.tensor_tensor(stage[:, 1, bank(tb)], acc[:, par, tb], stage[:, 0, bank(tb)],
                                            ALU.subtract)
                ins.then_inc(dve_out, 1)

            low(0, 0)
            low(1, 1)
            out_qkv(0, 0)
            low(2, 0)
            out_qkv(1, 1)
            with dve.Fori(1, QKV // 2) as i:
                low(2 * i + 1, 1)
                out_qkv(2 * i, 0)
                low(2 * i + 2, 0)
                out_qkv(2 * i + 1, 1)
            dve.wait_ge(padded, 1)
            with dve.Fori(0, KC // 2) as i:
                for half in range(2):
                    j = 2 * i + half
                    t = QKV + 3 * j
                    b = 3 * half
                    low(t + 1, (b + 1) % 2)
                    low(t + 2, (b + 2) % 2)
                    dve.wait_ge(pe_done, t + 2)
                    dve.wait_ge(act_out, QKV + j + 1)
                    for tb in range(TB):
                        ins = dve.tensor_tensor(gated[:, 2 + tb * NB:2 + (tb + 1) * NB], acc[:, (b + 1) % 2, tb],
                                                cx[:, bank(tb)], ALU.mult)
                    ins.then_inc(dve_out, 1)
                    dve.wait_ge(dve_out, QKV + 2 * j + 1)
                    dve.tensor_scalar(conv[:], gated[:, 2:S + 2], conv_cols[:, bass.ds(2 * KC + j, 1)], None,
                                      ALU.mult).then_inc(conv_step, 1)
                    for tap in (1, 0):
                        dve.wait_ge(conv_step, 3 * j + 2 - tap)
                        dve.scalar_tensor_tensor(out=conv[:], in0=gated[:, tap:S + tap],
                                                 scalar=conv_cols[:, bass.ds(tap * KC + j, 1)], in1=conv[:],
                                                 op0=ALU.mult, op1=ALU.add).then_inc(conv_step, 1)
                    low(t + 3, (b + 3) % 2)
                    dve.wait_ge(conv_step, 3 * j + 3)
                    dve.wait_ge(pe_done, t + 3)
                    dve.wait_ge(stored[half], 16 * (QKV + i))
                    for tb in range(TB):
                        ins = dve.tensor_tensor(stage[:, half, bank(tb)], acc[:, (b + 2) % 2, tb], conv[:, bank(tb)],
                                                ALU.mult)
                    ins.then_inc(dve_out, 1)
            with dve.Fori(0, GATES // 2 - 1) as i:
                for par in range(2):
                    low(FIRST_G + 2 * i + par + 1, 1 - par)
            low(TILES - 1, 1)


def attention(nc, used, keep, qkv_hi, qkv_lo, w_ada, o_t, mod_rows):
    ident, mod, csilu, marks = keep["ident"], keep["mod"], keep["csilu"], keep["marks"]
    PAIR = 2 * P
    SCALE = HD ** -0.5
    ZW = 2 * NB
    UNITS = [-(-(t + 1) * P // ZW) for t in range(NT)]
    UN_BEFORE = [sum(UNITS[:t]) for t in range(NT + 1)]
    GROUPS = [-(-(t + 1) // 4) for t in range(NT)]
    GR_BEFORE = [sum(GROUPS[:t]) for t in range(NT + 1)]
    NZ = UN_BEFORE[NT]
    ZB, TR = 2, 2
    AHEAD = 3
    SIZES = [(t + 1) * P + 1 for t in range(AHEAD)] + [S + 1 - P * ((NT - 1 - n) % AHEAD) for n in range(AHEAD)]
    PLACE = [sum(SIZES[:t if t < AHEAD else AHEAD + t % AHEAD]) for t in range(NT)]
    MOD_W = NB // 2
    MOD_AT = (NT // 2 - 2, NT - 2)
    NJ = 6 * KD
    with ExitStack() as ctx:
        s = Scope(nc, ctx, "att", used)
        q_parts = s.sb("q_parts", [P, 2, S], F32R)
        k_hi, k_lo = s.sb("k_hi", [P, 2, S], F32R), s.sb("k_lo", [P, 2, S], F32R)
        v_stack = s.sb("v_stack", [P, S])
        v_parts = s.sb("v_parts", [P, 2, NT, P], F32R)
        rest = s.sb("rest", [P, sum(SIZES)])
        wt = s.sb("wt", [P, sum(SIZES)])
        wt_hi, wt_lo = s.sb("wt_hi", [P, 2, NT, PAIR], F32R), s.sb("wt_lo", [P, 2, NT, PAIR], F32R)
        mask = s.sb("mask", [P, P], F32R)
        ident_r = s.sb("ident_r", [P, P], F32R)
        mask_f = s.sb("mask_f", [P, P])
        zero = s.sb("zero", [P, 1])
        low_half = s.sb("low_half", [HD, PAIR])
        o_out = s.sb("o_out", [HD, 2, PAIR])
        w_mod = s.sb("w_mod", [P, KD, MOD_W])
        mod_t = s.sb("mod_t", [NJ, P])
        p_z, p_t, p_o = s.ps("p_z", [P, ZB, ZW]), s.ps("p_t", [P, TR, NB]), s.ps("p_o", [P, 2, NB])
        names = ("mask_step", "const_done", "z_done", "z_used", "rest_done", "scan_done", "weights_done",
                 "turned", "hi_done", "lo_done", "o_done", "o_low", "o_used", "v_in", "mod_in",
                 "mod_done", "mod_step", "row_turned", "row_out", "row_stored")
        m = {n: s.sem(n) for n in names}
        qk_in = [s.sem(f"qk_in{i}") for i in range(2)]
        o_stored = [s.sem(f"o_stored{i}") for i in range(2)]
        block = ctx.enter_context(nc.Block())
        VB = NT // 4
        NR = VB + GR_BEFORE[NT]
        NG = NT // 2
        mod_view = w_ada.rearrange("l (k p) (b n) -> (l p) b k n", p=P, n=MOD_W)
        MOD_0 = FIRST_MOD * NB // MOD_W

        def heads(eng, run_head):
            with eng.Fori(0, HEADS // 2 - 1) as i:
                for sl in range(2):
                    run_head(i, sl, True)
            for sl in range(2):
                run_head(HEADS // 2 - 1, sl, sl == 0)

        @block.sync
        def _(sp):
            for i in range(2):
                sp.sem_inc(o_stored[i], 16)

            def load_qk(h, sl):
                for half in range(2):
                    rows = slice(half * HD, (half + 1) * HD)
                    src = (qkv_hi, qkv_lo)[half]
                    sp.dma_start(f32(q_parts[rows, sl]), src[bass.ds(h * HD, HD), :]).then_inc(qk_in[sl], 16)
                    sp.dma_start(f32(k_hi[rows, sl]), qkv_hi[bass.ds(h * HD + AW, HD), :]).then_inc(qk_in[sl], 16)
                    sp.dma_start(f32(k_lo[rows, sl]), qkv_lo[bass.ds(h * HD + AW, HD), :]).then_inc(qk_in[sl], 16)

            def load_v(h):
                for half, src in enumerate((qkv_hi, qkv_lo)):
                    sp.dma_start(v_stack[half * HD:(half + 1) * HD, :], src[bass.ds(h * HD + 2 * AW, HD), :]
                                 ).then_inc(m["v_in"], 16)

            load_qk(0, 0)
            load_v(0)
            sp.dma_start(w_mod[:], mod_view[:, MOD_0]).then_inc(m["mod_in"], 16)

            def run_head(i, sl, more):
                h = 2 * i + sl
                if more:
                    sp.wait_ge(m["o_done"], h * NG + 2)
                    load_qk(h + 1, 1 - sl)
                    sp.wait_ge(m["turned"], h * NR + VB)
                    load_v(h + 1)
                for g in range(NG):
                    for n, t in enumerate(MOD_AT):
                        if g == t // 2 and (more or n == 0):
                            sp.wait_ge(m["mod_done"], 2 * h + (n + 1))
                            sp.dma_start(w_mod[:], mod_view[:, bass.ds(2 * h + (MOD_0 + n + 1), 1)].rearrange(
                                "p b k n -> p (b k) n")).then_inc(m["mod_in"], 16)
                    sp.wait_ge(m["o_used"], h * NG + g + 3)
                    sp.dma_start(o_t[bass.ds(h * HD, HD), g * PAIR:(g + 1) * PAIR], o_out[:, g % 2]
                                 ).then_inc(o_stored[g % 2], 16)

            heads(sp, run_head)
            sp.wait_ge(m["row_out"], 1)
            sp.dma_start(mod_rows.rearrange("(r p) -> r p", p=P), mod_t[:]).then_inc(m["row_stored"], 16)
            sp.wait_ge(m["row_stored"], 16)
            for i in range(2):
                sp.wait_ge(o_stored[i], 16 * (HEADS * NG // 2 + 1))

        @block.gpsimd
        def _(pool):
            pool.memset(mask_f[:], 0.0).then_inc(m["mask_step"], 1)
            pool.wait_ge(m["mask_step"], 1)
            pool.affine_select(out=mask_f[:], in_=mask_f[:], compare_op=ALU.is_gt, fill=-BIG, base=0,
                               pattern=[[-1, P]], channel_multiplier=1).then_inc(m["mask_step"], 1)
            pool.wait_ge(m["mask_step"], 2)
            pool.tensor_copy(mask[:], mask_f[:]).then_inc(m["const_done"], 1)
            pool.tensor_copy(ident_r[:], ident[:]).then_inc(m["const_done"], 1)
            pool.memset(rest[:], 1.0).then_inc(m["const_done"], 1)
            with pool.Fori(0, HEADS) as h:
                for t in range(NT):
                    w = (t + 1) * P
                    pool.wait_ge(m["z_used"], h * NZ + UN_BEFORE[t + 1] + ZB)
                    pool.wait_ge(m["scan_done"], h * NT + t + 1)
                    o = PLACE[t]
                    pool.tensor_tensor(wt[:, o:o + w], wt[:, o:o + w], rest[:, o + 1:o + w + 1], ALU.mult
                                       ).then_inc(m["weights_done"], 1)

        @block.tensor
        def _(pe):
            pe.sem_inc(m["o_done"], 2)
            pe.wait_ge(m["const_done"], 3)

            def scores(h, sl, t, banks):
                w = (t + 1) * P
                q = q_parts[:, sl, t * P:(t + 1) * P]
                for c in banks:
                    u, a, b = c * NB // ZW, c * NB, min(w, (c + 1) * NB)
                    n = UN_BEFORE[t] + u
                    if a == u * ZW:
                        pe.wait_ge(m["z_used"], h * NZ + n + 1)
                    out = p_z[:, n % ZB, a - u * ZW:b - u * ZW]
                    pe.matmul(out, q, k_hi[:, sl, a:b], start=True, stop=False, skip_group_check=True)
                    mm = pe.matmul(out, q, k_lo[:, sl, a:b], start=False, stop=b < w, skip_group_check=True)
                    if b == w:
                        mm = pe.matmul(p_z[:, n % ZB, b - u * ZW - P:b - u * ZW], ident_r[:], mask[:],
                                       start=False, stop=True, skip_group_check=True)
                    if b == min(w, (u + 1) * ZW):
                        mm.then_inc(m["z_done"], 1)

            def turn_values(h):
                pe.wait_ge(m["v_in"], 32 * h + 32)
                for n in range(VB):
                    pe.wait_ge(m["lo_done"], h * NR + n + 1)
                    for j in range(4):
                        mm = pe.transpose(p_t[:, n % TR, j * P:(j + 1) * P],
                                          v_stack[:, (4 * n + j) * P:(4 * n + j + 1) * P], ident[:])
                    mm.then_inc(m["turned"], 1)

            def turn(h, t, r):
                if r == 0:
                    pe.wait_ge(m["weights_done"], h * NT + t + 1)
                n = VB + GR_BEFORE[t] + r
                pe.wait_ge(m["lo_done"], h * NR + n + 1)
                for j in range(4 * r, min(4 * r + 4, t + 1)):
                    mm = pe.transpose(p_t[:, n % TR, (j - 4 * r) * P:(j - 4 * r + 1) * P],
                                      wt[:, PLACE[t] + j * P:PLACE[t] + (j + 1) * P], ident[:])
                mm.then_inc(m["turned"], 1)

            def values(h, sl, g, blocks):
                for j in blocks:
                    if j == 0:
                        pe.wait_ge(m["lo_done"], h * NR + VB + GR_BEFORE[2 * g + 2] + TR)
                        pe.wait_ge(m["o_used"], h * NG + g + 1)
                    first = P if j == 2 * g + 1 else 0
                    for n, part in enumerate((wt_hi, wt_lo)):
                        mm = pe.matmul(p_o[:, g % 2, first:PAIR], v_parts[:, sl, j], part[:, g % 2, j, first:PAIR],
                                       start=j == 0 and n == 0, stop=j == 2 * g + 1 and n == 1, skip_group_check=True)
                    if j == 2 * g + 1:
                        mm.then_inc(m["o_done"], 1)

            def share(count, r, parts):
                return range(count * r // parts, count * (r + 1) // parts)

            pe.wait_ge(qk_in[0], 96)
            for t in range(AHEAD):
                scores(0, 0, t, range(GROUPS[t]))
            turn_values(0)

            def run_head(i, sl, more):
                h = 2 * i + sl
                for t in range(NT):
                    ahead = (t + AHEAD) % NT
                    g = t // 2 - 1
                    if t + AHEAD == NT and more:
                        pe.wait_ge(qk_in[1 - sl], 96 * (i + sl) + 96)
                    for r in range(GROUPS[t]):
                        turn(h, t, r)
                        if t + AHEAD < NT:
                            scores(h, sl, ahead, share(GROUPS[ahead], r, GROUPS[t]))
                        elif more:
                            scores(h + 1, 1 - sl, ahead, share(GROUPS[ahead], r, GROUPS[t]))
                        if g >= 0:
                            values(h, sl, g, [t % 2 * (g + 1) + j for j in share(g + 1, r, GROUPS[t])])
                    if t in MOD_AT:
                        n = MOD_AT.index(t)
                        pe.wait_ge(m["mod_in"], 32 * h + (16 * n + 16))
                        for c in range(MOD_W // P):
                            out = p_o[:, 0, bass.ds((2 * h + n) * (MOD_W // P) + (PAIR + c), 1)]
                            for k in range(KD):
                                mm = pe.matmul(out, w_mod[:, k, c * P:(c + 1) * P], csilu[:, k:k + 1],
                                               start=k == 0, stop=k == KD - 1, skip_group_check=True)
                        mm.then_inc(m["mod_done"], 1)
                if more:
                    turn_values(h + 1)
                values(h, sl, NG - 1, range(NT))

            heads(pe, run_head)
            pe.wait_ge(m["mod_step"], 2)
            pe.wait_ge(m["lo_done"], HEADS * NR + TR)
            pe.transpose(p_t[0:NJ, 0, 0:P], mod[:], ident[:]).then_inc(m["row_turned"], 1)

        @block.scalar
        def _(act):
            act.sem_inc(m["z_used"], ZB)
            act.wait_ge(m["const_done"], 3)

            def sigmoids(h, t):
                w, o = (t + 1) * P, PLACE[t]
                spans = [(n, u * ZW, min(w, (u + 1) * ZW)) for u, n in enumerate(range(UN_BEFORE[t], UN_BEFORE[t + 1]))]
                for n, a, b in spans:
                    act.wait_ge(m["z_done"], h * NZ + n + 1)
                    ins = act.activation(rest[:, o + a:o + b], p_z[:, n % ZB, 0:b - a], ACT.Sigmoid, scale=-SCALE)
                ins.then_inc(m["rest_done"], 1)
                for n, a, b in spans:
                    act.activation(wt[:, o + a:o + b], p_z[:, n % ZB, 0:b - a], ACT.Sigmoid, scale=SCALE
                                   ).then_inc(m["z_used"], 1)

            def high(h, t):
                act.wait_ge(m["o_done"], h * NG + t // 2 + 1)
                for r in range(GROUPS[t]):
                    n = VB + GR_BEFORE[t] + r
                    j, k = 4 * r, min(4 * r + 4, t + 1)
                    act.wait_ge(m["turned"], h * NR + n + 1)
                    act.activation(wt_hi[:, t // 2 % 2, j:k, t % 2 * P:(t % 2 + 1) * P],
                                   p_t[:, n % TR, 0:(k - j) * P].rearrange("p (j t) -> p j t", t=P), ACT.Copy
                                   ).then_inc(m["hi_done"], 1)

            def copy_values(h, sl):
                for n in range(VB):
                    act.wait_ge(m["turned"], h * NR + n + 1)
                    act.activation(v_parts[:, sl, 4 * n:4 * n + 2], p_t[:, n % TR, 0:2 * P].rearrange(
                        "p (j d) -> p j d", d=P), ACT.Copy).then_inc(m["hi_done"], 1)

            for t in range(AHEAD):
                sigmoids(0, t)
            copy_values(0, 0)

            def run_head(i, sl, more):
                h = 2 * i + sl
                for t in range(NT):
                    high(h, t)
                    if t + AHEAD < NT or more:
                        sigmoids(h if t + AHEAD < NT else h + 1, (t + AHEAD) % NT)
                if more:
                    copy_values(h + 1, 1 - sl)

            heads(act, run_head)

        @block.vector
        def _(dve):
            dve.sem_inc(m["lo_done"], TR)
            dve.sem_inc(m["o_used"], 2)
            dve.memset(zero[:], 0.0).then_inc(m["o_low"], 1)
            dve.wait_ge(m["o_low"], 1)

            def scan(h, t):
                w = (t + 1) * P
                dve.wait_ge(m["rest_done"], h * NT + t + 1)
                r = rest[:, PLACE[t]:PLACE[t] + w]
                dve.tensor_tensor_scan(r[:, ::-1], r[:, ::-1], zero[:].to_broadcast([P, w]), 1.0, ALU.mult, ALU.max
                                       ).then_inc(m["scan_done"], 1)

            def low(h, t):
                for r in range(GROUPS[t]):
                    n = VB + GR_BEFORE[t] + r
                    j, k = 4 * r, min(4 * r + 4, t + 1)
                    cols = (slice(None), t // 2 % 2, slice(j, k), slice(t % 2 * P, (t % 2 + 1) * P))
                    dve.wait_ge(m["hi_done"], h * NR + n + 1)
                    dve.tensor_tensor(wt_lo[cols], p_t[:, n % TR, 0:(k - j) * P].rearrange("p (j t) -> p j t", t=P),
                                      f32(wt_hi[cols]), ALU.subtract).then_inc(m["lo_done"], 1)

            def output(h, g):
                dve.wait_ge(m["o_done"], h * NG + g + 3)
                dve.wait_ge(m["o_used"], h * NG + g + 2)
                dve.tensor_copy(low_half[:], p_o[HD:P, g % 2, 0:PAIR]).then_inc(m["o_low"], 1)
                dve.wait_ge(m["o_low"], h * NG + g + 2)
                dve.wait_ge(o_stored[g % 2], 16 * (h * (NG // 2) + g // 2 + 1))
                dve.tensor_tensor(o_out[:, g % 2], p_o[0:HD, g % 2, 0:PAIR], low_half[:], ALU.add
                                  ).then_inc(m["o_used"], 1)

            def copy_values(h, sl):
                for n in range(VB):
                    dve.wait_ge(m["hi_done"], h * NR + n + 1)
                    dve.tensor_copy(v_parts[:, sl, 4 * n + 2:4 * n + 4], p_t[:, n % TR, 2 * P:4 * P].rearrange(
                        "p (j d) -> p j d", d=P)).then_inc(m["lo_done"], 1)

            for t in range(AHEAD - 1):
                scan(0, t)
            copy_values(0, 0)

            def run_head(i, sl, more):
                h = 2 * i + sl
                for t in range(NT):
                    ahead = t + AHEAD - 1
                    low(h, t)
                    if ahead < NT:
                        scan(h, ahead)
                    elif more:
                        scan(h + 1, ahead - NT)
                    if t % 2 == 1 and t > 1:
                        output(h, t // 2 - 1)
                if more:
                    copy_values(h + 1, 1 - sl)
                output(h, NG - 1)

            heads(dve, run_head)
            n = FIRST_MOD * NB // P
            dve.wait_ge(m["mod_done"], 2 * HEADS)
            dve.tensor_tensor(mod[:, n:NJ], mod[:, n:NJ], p_o[:, 0, PAIR:PAIR + NJ - n], ALU.add
                              ).then_inc(m["mod_step"], 1)
            dve.wait_ge(m["mod_step"], 1)
            dve.tensor_scalar(mod[:, SC2:SC2 + KD], mod[:, SC2:SC2 + KD], 1.0, None, ALU.add
                              ).then_inc(m["mod_step"], 1)
            dve.wait_ge(m["row_turned"], 1)
            dve.tensor_copy(mod_t[:], p_t[0:NJ, 0, 0:P]).then_inc(m["row_out"], 1)


def branch_outputs(nc, used, keep, conv_t, o_t, gate_t, w_a, w_b, m_t):
    RB = 4
    WQ = 4
    QW = D // WQ
    with ExitStack() as ctx:
        s = Scope(nc, ctx, "br", used)
        w_raw = s.sb("w_raw", [P, WQ, 2, KC, QW])
        w_hi, w_lo = s.sb("w_hi", [P, WQ, 2, KC, QW], F32R), s.sb("w_lo", [P, WQ, 2, KC, QW], F32R)
        b_raw = s.sb("b_raw", [P, 2, KC, NB])
        b_hi, b_lo = s.sb("b_hi", [P, 2, 2, KC, NB], F32R), s.sb("b_lo", [P, 2, 2, KC, NB], F32R)
        gates = s.sb("gates", [P, RB, 2, NB])
        acc = s.ps("acc", [P, RB, 2, NB])
        names = ("w_hi_done", "w_lo_done", "b_hi_done", "b_lo_done", "pe_done", "prod_done", "sum_done", "b_in")
        m = {n: s.sem(n) for n in names}
        w_in = [s.sem(f"w_in{i}") for i in range(WQ)]
        g_in = [s.sem(f"g_in{i}") for i in range(RB)]
        stored = [s.sem(f"stored{i}") for i in range(RB)]
        block = ctx.enter_context(nc.Block())
        gate_v = gate_t.rearrange("(b r) t -> r b t", b=2)

        @block.sync
        def _(sp):
            def load_w(q):
                for n, w in enumerate((w_a, w_b)):
                    sp.dma_start(w_raw[:, q, n], w.rearrange("l (k p) n -> (l p) k n", p=P)[:, :, q * QW:(q + 1) * QW]
                                 ).then_inc(w_in[q], 16)

            def load_b(tb):
                for n, src in enumerate((conv_t, o_t)):
                    sp.dma_start(b_raw[:, n], src.rearrange("(k p) t -> p k t", p=P)[:, :, bass.ds(tb * NB, NB)]
                                 ).then_inc(m["b_in"], 16)

            def load_gates(tb, d):
                sp.wait_ge(stored[d % RB], 16 * (tb * (KD // RB) + d // RB + 1))
                sp.dma_start(gates[:, d % RB], gate_v[d * P:(d + 1) * P, :, bass.ds(tb * NB, NB)]
                             ).then_inc(g_in[d % RB], 16)

            load_w(0)
            load_b(0)
            load_w(1)
            for d in range(2):
                load_gates(0, d)
            for q in range(2, WQ):
                load_w(q)
            for d in range(2, RB):
                load_gates(0, d)

            def rest_of(tb):
                sp.wait_ge(m["b_lo_done"], 2 * tb + 2)
                load_b(tb + 1)
                for d in range(RB, KD):
                    load_gates(tb, d)

            rest_of(0)
            with sp.Fori(1, TB - 1) as tb:
                for d in range(RB):
                    load_gates(tb, d)
                rest_of(tb)
            for d in range(KD):
                load_gates(TB - 1, d)

        @block.tensor
        def _(pe):
            with pe.Fori(0, TB // 2) as i:
                for par in range(2):
                    tb = 2 * i + par
                    pe.wait_ge(m["b_lo_done"], 2 * tb + 2)
                    for d in range(KD):
                        pe.wait_ge(m["w_lo_done"], d * P // QW + 1)
                        pe.wait_ge(m["prod_done"], 2 * (tb * KD + d) + 2)
                        q, cols = d * P // QW, slice(d * P % QW, d * P % QW + P)
                        for n in range(2):
                            for k in range(KC):
                                hi, lo = w_hi[:, q, n, k, cols], w_lo[:, q, n, k, cols]
                                mm = product(pe, acc[:, d % RB, n], ((hi, b_hi[:, par, n, k]), (hi, b_lo[:, par, n, k]),
                                                                     (lo, b_hi[:, par, n, k])), k == 0, k == KC - 1)
                        mm.then_inc(m["pe_done"], 1)

        @block.scalar
        def _(act):
            def high_w(q):
                act.wait_ge(w_in[q], 32)
                act.activation(w_hi[:, q], w_raw[:, q], ACT.Copy).then_inc(m["w_hi_done"], 1)

            def high_b(tb, par):
                act.wait_ge(m["b_in"], 32 * tb + 32)
                for n in range(2):
                    act.activation(b_hi[:, par, n], b_raw[:, n], ACT.Copy).then_inc(m["b_hi_done"], 1)

            def stores(tb):
                for d in range(KD):
                    act.wait_ge(m["sum_done"], tb * KD + d + 1)
                    act.dma_start(m_t[d * P:(d + 1) * P, bass.ds(tb * NB, NB)], gates[:, d % RB, 0]
                                  ).then_inc(stored[d % RB], 16)

            high_w(0)
            high_b(0, 0)
            for q in range(1, WQ):
                high_w(q)
            with act.Fori(0, TB // 2) as i:
                high_b(2 * i + 1, 1)
                stores(2 * i)
                with act.If(i < TB // 2 - 1):
                    high_b(2 * i + 2, 0)
                stores(2 * i + 1)
            for i in range(RB):
                act.wait_ge(stored[i], 16 * (TB * KD // RB + 1))

        @block.vector
        def _(dve):
            dve.sem_inc(m["prod_done"], 2 * RB)

            def low_w(q):
                dve.wait_ge(m["w_hi_done"], q + 1)
                dve.tensor_tensor(w_lo[:, q], w_raw[:, q], f32(w_hi[:, q]), ALU.subtract).then_inc(m["w_lo_done"], 1)

            def low_b(tb, par):
                for n in range(2):
                    dve.wait_ge(m["b_hi_done"], 2 * tb + n + 1)
                    dve.tensor_tensor(b_lo[:, par, n], b_raw[:, n], f32(b_hi[:, par, n]), ALU.subtract
                                      ).then_inc(m["b_lo_done"], 1)

            def gate(tb):
                for d in range(KD):
                    dve.wait_ge(m["pe_done"], tb * KD + d + 1)
                    dve.wait_ge(g_in[d % RB], 16 * (tb * (KD // RB) + d // RB + 1))
                    for n in range(2):
                        dve.tensor_tensor(gates[:, d % RB, n], acc[:, d % RB, n], gates[:, d % RB, n], ALU.mult
                                          ).then_inc(m["prod_done"], 1)

            low_w(0)
            low_b(0, 0)
            for q in range(1, WQ):
                low_w(q)
            with dve.Fori(0, TB // 2) as i:
                low_b(2 * i + 1, 1)
                gate(2 * i)
                with dve.If(i < TB // 2 - 1):
                    low_b(2 * i + 2, 0)
                gate(2 * i + 1)

        @block.gpsimd
        def _(pool):
            for i in range(RB):
                pool.sem_inc(stored[i], 16)
            with pool.Fori(0, TB) as tb:
                for d in range(KD):
                    u = tb * KD + d
                    pool.wait_ge(m["prod_done"], 2 * u + 2 + 2 * RB)
                    pool.tensor_tensor(gates[:, d % RB, 0], gates[:, d % RB, 0], gates[:, d % RB, 1], ALU.add
                                       ).then_inc(m["sum_done"], 1)


class Tile:

    def __init__(self, i, o):
        self.n, self.half, self.quarter = 4 * i + o, 2 * i + o // 2, i + o // 4
        self.s2, self.s4 = o % 2, o % 4
        self.live = not isinstance(i, int) or 0 <= 4 * i + o < NT
        self.i, self.o = i, o

    def __add__(self, k):
        return Tile(self.i, self.o + k)


def pipeline(eng, step, lag):
    for o in range(4):
        step(Tile(0, o))
    with eng.Fori(1, NT // 4 - 1) as i:
        for o in range(4):
            step(Tile(i, o))
    for o in range(4 + lag):
        step(Tile(NT // 4 - 1, o))


class Chain:

    def __init__(self, eng, sem, base):
        self.eng, self.sem, self.base, self.n = eng, sem, base, 0

    def link(self, ins, mark=None):
        self.n += 1
        ins.then_inc(self.sem, 1)
        if mark is None:
            self.eng.wait_ge(self.sem, self.base + self.n)
        else:
            wait_apart(self.eng, mark, self.sem, self.base + self.n)


def mix_norm_route(nc, used, keep, m_t, w_o, x, mod_rows, ln1_g, ln1_b, w_router, b_router, x1, rows, results):
    ident, dest, gate_w, table, marks = (keep[n] for n in ("ident", "dest", "gate_w", "table", "marks"))
    A_OPS, C_OPS, R1_OPS, R2_OPS = 3, 2, 22, 3
    WR = 4
    with ExitStack() as ctx:
        s = Scope(nc, ctx, "mix", used)
        w_raw = s.sb("w_raw", [P, WR, D])
        w_hi, w_lo = s.sb("w_hi", [P, KD, D], F32R), s.sb("w_lo", [P, KD, D], F32R)
        a_raw = s.sb("a_raw", [P, 2, KD, P])
        a_hi, a_lo = s.sb("a_hi", [P, 2, KD, P], F32R), s.sb("a_lo", [P, 2, KD, P], F32R)
        xt, y, x1t = s.sb("xt", [P, 2, D]), s.sb("y", [P, D]), s.sb("x1t", [P, 2, D])
        u2, u2t = s.sb("u2", [P, 4, D]), s.sb("u2t", [P, KD, P])
        g1r, ln_g, ln_b, sc2r, sh2r = (s.sb(n, [P, D]) for n in ("g1r", "ln_g", "ln_b", "sc2r", "sh2r"))
        wr, br = s.sb("wr", [P, KD, E]), s.sb("br", [P, E])
        stats, mv = s.sb("stats", [P, 2, 6]), s.sb("mv", [P, 2])
        var, rstd, minus_half = s.sb("var", [P, 1]), s.sb("rstd", [P, 1]), s.sb("minus_half", [P, 1])
        tri, ones = s.sb("tri", [P, P]), s.sb("ones", [P, P])
        no_twin = s.sb("no_twin", [P, G, EG, EG])
        down_i, down = s.sb("down_i", [P, E], I32), s.sb("down", [P, E])
        base_i, base = s.sb("base_i", [P, E], I32), s.sb("base", [P, E])
        aff, sel, pairs = s.sb("aff", [P, E]), s.sb("sel", [P, E]), s.sb("pairs", [P, G, EG, EG])
        g_score, g_key, g_off = s.sb("g_score", [P, G]), s.sb("g_key", [P, G]), s.sb("g_off", [P, G])
        top, left, key = s.sb("top", [P, 1]), s.sb("left", [P, 2, E]), s.sb("key", [P, E])
        chosen = s.sb("chosen", [P, 2, 2, E])
        all_chosen = s.sb("all_chosen", [P, NT, 2, E])
        all_at = s.sb("all_at", [P, 2 * NT, E])
        moved = s.sb("moved", [P, 2 * NT])
        all_dest, shift = s.sb("all_dest", [P, 2 * NT]), s.sb("shift", [P, E])
        both, seen = s.sb("both", [P, 2, E]), s.sb("seen", [P, 2, E])
        picked, gates, g_sum = s.sb("picked", [P, 2, E]), s.sb("gates", [P, 2]), s.sb("g_sum", [P, 1])
        place, at, dest_f = s.sb("place", [P, E]), s.sb("at", [P, 2, E]), s.sb("dest_f", [P, 2])
        dest_now = s.sb("dest_now", [P, 2, 2], U32)
        n_rows, n_blk, tab_i, tab_f = (s.sb("n_rows", [P, E]), s.sb("n_blk", [P, E], I32), s.sb("tab_i", [P, E], I32),
                                       s.sb("tab_f", [P, E]))
        tab_l = s.sb("tab_l", [P, E])
        p_mix, p_t, p_r = s.ps("p_mix", [P, 2, 2, NB]), s.ps("p_t", [P, 2, NB]), s.ps("p_r", [P, 2, NB])
        names = ("const_in", "w_hi_done", "w_lo_done", "a_hi_done", "a_lo_done", "mix_done", "mix_used",
                 "a_step", "c_step", "var_done", "var_step", "rstd_done", "x1_done", "u2_step", "u2_done", "turned",
                 "u2t_done", "logits_done", "aff_done", "r1_step", "recip_done", "both_done", "r1_done", "ranked", "rank_used", "r2_step",
                 "dest_done", "const_step", "const_done", "tail_step")
        m = {n: s.sem(n) for n in names}
        w_in = [s.sem(f"w_in{i}") for i in range(WR)]
        a_in = [s.sem(f"a_in{i}") for i in range(2)]
        x_in = [s.sem(f"x_in{i}") for i in range(2)]
        x1_stored = [s.sem(f"x1_stored{i}") for i in range(2)]
        scattered = [s.sem(f"scattered{i}") for i in range(4)]
        block = ctx.enter_context(nc.Block())

        def mod_row(j):
            return mod_rows[j * P:j * P + D].rearrange("(a d) -> a d", a=1).to_broadcast([P, D])


        @block.sync
        def _(sp):
            for i in range(2):
                sp.sem_inc(x1_stored[i], 16)
            w_view = w_o.rearrange("l (k p) n -> (l p) k n", p=P)

            def load_w(k):
                if k >= WR:
                    sp.wait_ge(m["w_lo_done"], k - WR + 1)
                sp.dma_start(w_raw[:, k % WR], w_view[:, k]).then_inc(w_in[k % WR], 16)

            def load_a(t):
                sp.dma_start(a_raw[:, t.s2], m_t.rearrange("(k p) t -> p k t", p=P)[:, :, bass.ds(t.n * P, P)]
                             ).then_inc(a_in[t.s2], 16)

            def load_x(t):
                sp.dma_start(xt[:, t.s2], x.rearrange("b t d -> (b t) d")[bass.ds(t.n * P, P), :]
                             ).then_inc(x_in[t.s2], 16)

            load_a(Tile(0, 0))
            for k in range(KD):
                load_w(k)
            load_x(Tile(0, 0))
            load_a(Tile(0, 1))
            load_x(Tile(0, 1))
            for dst, src in ((g1r, mod_row(G1)), (sc2r, mod_row(SC2)), (sh2r, mod_row(SH2)),
                             (ln_g, ln1_g.to_broadcast([P, D])), (ln_b, ln1_b.to_broadcast([P, D])),
                             (wr, w_router.rearrange("(k p) e -> p k e", p=P)),
                             (br, b_router.rearrange("(a e) -> a e", a=1).to_broadcast([P, E]))):
                sp.dma_start(dst[:], src).then_inc(m["const_in"], 16)

            def step(t):
                if (t + 2).live:
                    sp.wait_ge(m["a_lo_done"], t.n + 1)
                    load_a(t + 2)
                sp.wait_ge(m["x1_done"], t.n + 1)
                sp.dma_start(x1[bass.ds(t.n * P, P), :], x1t[:, t.s2]).then_inc(x1_stored[t.s2], 16)
                if (t + 2).live:
                    load_x(t + 2)

            pipeline(sp, step, 0)
            for i in range(2):
                sp.wait_ge(x1_stored[i], 16 * (NT // 2 + 1))

        @block.tensor
        def _(pe):
            pe.sem_inc(m["mix_done"], 2)
            pe.sem_inc(m["logits_done"], 1)

            def step(t):
                if t.live:
                    pe.wait_ge(m["a_lo_done"], t.n + 1)
                    pe.wait_ge(m["mix_used"], 2 * t.n + 2)
                    for k in range(KD):
                        pe.wait_ge(m["w_lo_done"], k + 1)
                        for n in range(2):
                            w = slice(n * NB, (n + 1) * NB)
                            mm = product(pe, p_mix[:, t.s2, n], ((a_hi[:, t.s2, k], w_hi[:, k, w]),
                                                                 (a_hi[:, t.s2, k], w_lo[:, k, w]),
                                                                 (a_lo[:, t.s2, k], w_hi[:, k, w])), k == 0, k == KD - 1)
                    mm.then_inc(m["mix_done"], 1)
                b = t + -2
                if b.live:
                    pe.wait_ge(m["u2_done"], b.n + 3)
                    pe.wait_ge(m["u2t_done"], b.n + 1)
                    for k in range(KD):
                        mm = pe.transpose(p_t[:, k // 4, k % 4 * P:(k % 4 + 1) * P], u2[:, b.s4, k * P:(k + 1) * P], ident[:])
                    mm.then_inc(m["turned"], 1)
                c = t + -3
                if c.live:
                    pe.wait_ge(m["const_done"], 1)
                    pe.wait_ge(m["r1_done"], c.n + 2)
                    pe.wait_ge(m["rank_used"], c.n + 1)
                    pe.matmul(p_r[:, 1, 0:E], tri[:], both[:, c.s2], start=True, stop=False)
                    pe.matmul(p_r[:, 1, 0:E], ones[:], seen[:, c.s2], start=False, stop=True).then_inc(m["ranked"], 1)
                if b.live:
                    pe.wait_ge(m["u2t_done"], b.n + 2)
                    pe.wait_ge(m["aff_done"], b.n + 1)
                    pe.wait_ge(m["const_in"], 16 * 7)
                    for k in range(KD):
                        mm = pe.matmul(p_r[:, 0, 0:E], u2t[:, k], wr[:, k], start=k == 0, stop=k == KD - 1)
                    mm.then_inc(m["logits_done"], 1)

            pipeline(pe, step, 3)
            pe.wait_ge(m["rank_used"], NT + 1)
            pe.matmul(p_r[:, 1, 0:E], ones[:], seen[:, NT % 2], start=True, stop=True).then_inc(m["ranked"], 1)

        @block.scalar
        def _(act):
            act.sem_inc(m["u2t_done"], 1)
            act.sem_inc(m["aff_done"], 1)

            def high(t):
                act.wait_ge(a_in[t.s2], 16 * t.half + 16)
                act.wait_ge(m["mix_done"], t.n + 1)
                act.activation(a_hi[:, t.s2], a_raw[:, t.s2], ACT.Copy).then_inc(m["a_hi_done"], 1)

            high(Tile(0, 0))
            for k in range(KD):
                act.wait_ge(w_in[k % WR], 16 * (k // WR) + 16)
                act.activation(w_hi[:, k], w_raw[:, k % WR], ACT.Copy).then_inc(m["w_hi_done"], 1)

            def step(t):
                if (t + 1).live:
                    high(t + 1)
                b = t + -2
                if b.live:
                    act.wait_ge(m["turned"], b.n + 1)
                    act.wait_ge(m["logits_done"], b.n + 1)
                    for n in range(2):
                        ins = act.activation(u2t[:, 4 * n:4 * n + 4], p_t[:, n].rearrange("p (k t) -> p k t", t=P), ACT.Copy)
                    ins.then_inc(m["u2t_done"], 1)
                    act.wait_ge(m["logits_done"], b.n + 2)
                    act.wait_ge(m["r1_done"], b.n + 1)
                    act.activation(aff[:], p_r[:, 0, 0:E], ACT.Sigmoid).then_inc(m["aff_done"], 1)

            pipeline(act, step, 2)

        @block.gpsimd
        def _(pool):
            pool.sem_inc(m["u2_done"], 2)
            cs = Chain(pool, m["const_step"], 0)
            cs.link(pool.memset(tri[:], 1.0))
            cs.link(pool.affine_select(out=tri[:], in_=tri[:], compare_op=ALU.is_gt, fill=0.0, base=0,
                                       pattern=[[1, P]], channel_multiplier=-1))
            cs.link(pool.memset(ones[:], 1.0))
            cs.link(pool.memset(minus_half[:], -0.5))
            cs.link(pool.memset(no_twin[:], 0.0))
            cs.link(pool.affine_select(out=no_twin[:], in_=no_twin[:], compare_op=ALU.not_equal, fill=-BIG, base=0,
                                       pattern=[[0, G], [1, EG], [-1, EG]], channel_multiplier=0))
            cs.link(pool.iota(down_i[:], pattern=[[-1, E]], base=E, channel_multiplier=0))
            cs.link(pool.tensor_copy(down[:], down_i[:]))
            cs.link(pool.iota(base_i[:], pattern=[[CAP, E]], base=0, channel_multiplier=0))
            cs.link(pool.tensor_copy(base[:], base_i[:]))
            pool.memset(seen[:], 0.0).then_inc(m["const_done"], 1)

            def low(t):
                pool.wait_ge(m["a_hi_done"], t.n + 1)
                pool.tensor_tensor(a_lo[:, t.s2], a_raw[:, t.s2], f32(a_hi[:, t.s2]), ALU.subtract
                                   ).then_inc(m["a_lo_done"], 1)

            low(Tile(0, 0))

            def step(t):
                if (t + 1).live:
                    low(t + 1)
                if t.live:
                    wait_apart(pool, marks["pool"], m["var_done"], t.n + 1)
                    pool.tensor_scalar(var[:], mv[:, 1:2], EPS, None, ALU.add).then_inc(m["var_step"], 1)
                    pool.wait_ge(m["var_step"], t.n + 1)
                    pool.tensor_tensor(rstd[:], var[:], minus_half[:], ALU.pow).then_inc(m["rstd_done"], 1)
                c = t + -3
                if c.live:
                    wait_apart(pool, marks["pool"], m["dest_done"], c.n + 1)
                    for k in range(2):
                        pool.indirect_dma_start(out=rows, out_offset=bass.IndirectOffsetOnAxis(
                            ap=dest_now[:, c.s2, k:k + 1], axis=0), in_=u2[:, c.s4], in_offset=None
                        ).then_inc(scattered[c.s4], 16)
                if t.live:
                    pool.wait_ge(m["x1_done"], t.n + 1)
                    if (t + -4).live:
                        pool.wait_ge(scattered[t.s4], 32 * t.quarter)
                    pool.tensor_tensor(u2[:, t.s4], x1t[:, t.s2], sc2r[:], ALU.mult).then_inc(m["u2_step"], 1)
                    pool.wait_ge(m["u2_step"], t.n + 1)
                    pool.tensor_tensor(u2[:, t.s4], u2[:, t.s4], sh2r[:], ALU.add).then_inc(m["u2_done"], 1)

            pool.wait_ge(m["const_in"], 16 * 7)
            pipeline(pool, step, 3)
            for i in range(4):
                pool.wait_ge(scattered[i], 32 * (NT // 4))

        @block.vector
        def _(dve):
            dve.sem_inc(m["mix_used"], 4)
            dve.sem_inc(m["r1_done"], 1)
            dve.sem_inc(m["rank_used"], 1)
            for k in range(KD):
                dve.wait_ge(m["w_hi_done"], k + 1)
                dve.tensor_tensor(w_lo[:, k], w_raw[:, k % WR], f32(w_hi[:, k]), ALU.subtract
                                  ).then_inc(m["w_lo_done"], 1)
            dve.wait_ge(m["const_in"], 16 * 7)
            dve.wait_ge(m["const_done"], 1)

            def norm(t):
                ch = Chain(dve, m["a_step"], A_OPS * t.n)
                dve.wait_ge(m["mix_done"], t.n + 3)
                for n in range(2):
                    w = slice(n * NB, (n + 1) * NB)
                    dve.tensor_tensor(y[:, w], p_mix[:, t.s2, n], g1r[:, w], ALU.mult).then_inc(m["mix_used"], 1)
                dve.wait_ge(m["mix_used"], 2 * t.n + 6)
                dve.wait_ge(x_in[t.s2], 16 * t.half + 16)
                ch.link(dve.scalar_tensor_tensor(out=y[:], in0=xt[:, t.s2], scalar=ALPHA, in1=y[:], op0=ALU.mult, op1=ALU.add))
                for n in range(2):
                    ch.link(dve.bn_stats(stats[:, n], y[:, n * NB:(n + 1) * NB]), mark=marks["dve"] if n == 1 else None)
                dve.bn_aggr(mv[:], stats[:].rearrange("p a b -> p (a b)")).then_inc(m["var_done"], 1)

            def affine(t):
                ch = Chain(dve, m["c_step"], C_OPS * t.n)
                dve.wait_ge(m["rstd_done"], t.n + 1)
                dve.wait_ge(m["var_done"], t.n + 1)
                dve.wait_ge(x1_stored[t.s2], 16 * t.half + 16)
                dve.wait_ge(m["u2_done"], t.n + 1)
                ch.link(dve.tensor_scalar(x1t[:, t.s2], y[:], mv[:, 0:1], rstd[:], ALU.subtract, ALU.mult))
                ch.link(dve.tensor_tensor(x1t[:, t.s2], x1t[:, t.s2], ln_g[:], ALU.mult))
                dve.tensor_tensor(x1t[:, t.s2], x1t[:, t.s2], ln_b[:], ALU.add).then_inc(m["x1_done"], 1)

            def choose(t):
                ch = Chain(dve, m["r1_step"], R1_OPS * t.n)
                dve.wait_ge(m["aff_done"], t.n + 2)
                ch.link(dve.tensor_tensor(sel[:], aff[:], br[:], ALU.add))
                by_group = sel[:].rearrange("p (g e) -> p g e", g=G)
                ch.link(dve.tensor_tensor(pairs[:], by_group.unsqueeze(3).to_broadcast([P, G, EG, EG]),
                                          by_group.unsqueeze(2).to_broadcast([P, G, EG, EG]), ALU.add))
                ch.link(dve.tensor_tensor(pairs[:], pairs[:], no_twin[:], ALU.add))
                ch.link(dve.tensor_reduce(g_score[:], pairs[:].rearrange("p g a b -> p g (a b)"), AX.X, ALU.max))
                ch.link(dve.tensor_reduce(top[:], g_score[:], AX.X, ALU.max))
                ch.link(dve.scalar_tensor_tensor(out=g_key[:], in0=g_score[:], scalar=top[:], in1=down[:, 0:G],
                                                 op0=ALU.is_ge, op1=ALU.mult))
                ch.link(dve.tensor_reduce(top[:], g_key[:], AX.X, ALU.max))
                ch.link(dve.tensor_scalar(g_off[:], g_key[:], top[:], -BIG, ALU.not_equal, ALU.mult))
                ch.link(dve.tensor_tensor(left[:, 0].rearrange("p (g e) -> p g e", g=G), by_group,
                                          g_off[:].unsqueeze(2).to_broadcast([P, G, EG]), ALU.add))
                for n in range(2):
                    hot = chosen[:, t.s2, n]
                    ch.link(dve.tensor_reduce(top[:], left[:, n], AX.X, ALU.max))
                    ch.link(dve.scalar_tensor_tensor(out=key[:], in0=left[:, n], scalar=top[:], in1=down[:],
                                                     op0=ALU.is_ge, op1=ALU.mult))
                    ch.link(dve.tensor_reduce(top[:], key[:], AX.X, ALU.max))
                    ch.link(dve.tensor_scalar(hot, key[:], top[:], None, ALU.is_equal))
                    if n == 0:
                        ch.link(dve.scalar_tensor_tensor(out=left[:, 1], in0=hot, scalar=-2 * BIG, in1=left[:, 0],
                                                         op0=ALU.mult, op1=ALU.add))
                hots = chosen[:, t.s2]
                ch.link(dve.tensor_tensor(picked[:], hots, aff[:].unsqueeze(1).to_broadcast([P, 2, E]), ALU.mult))
                ch.link(dve.tensor_reduce(gates[:], picked[:], AX.X, ALU.add))
                ch.link(dve.tensor_reduce(g_sum[:], gates[:], AX.X, ALU.add))
                ch.link(dve.tensor_copy(all_chosen[:, bass.ds(t.n, 1)].rearrange("p a n e -> p (a n) e"), hots))
                assert ch.n == R1_OPS, ch.n
                dve.reciprocal(g_sum[:], g_sum[:]).then_inc(m["recip_done"], 1)
                dve.wait_ge(m["recip_done"], t.n + 1)
                dve.tensor_scalar(gate_w[:, bass.ds(2 * t.n, 2)], gates[:], g_sum[:], None, ALU.mult)
                dve.tensor_tensor(both[:, t.s2], hots[:, 0], hots[:, 1], ALU.add).then_inc(m["both_done"], 1)
                dve.wait_ge(m["both_done"], t.n + 1)
                dve.tensor_tensor(seen[:, 1 - t.s2], seen[:, t.s2], both[:, t.s2], ALU.add).then_inc(m["r1_done"], 1)

            def put(t):
                ch = Chain(dve, m["r2_step"], R2_OPS * t.n)
                dve.wait_ge(m["ranked"], t.n + 1)
                dve.tensor_tensor(place[:], p_r[:, 1, 0:E], base[:], ALU.add).then_inc(m["rank_used"], 1)
                dve.wait_ge(m["rank_used"], t.n + 2)
                ch.link(dve.tensor_tensor(at[:], chosen[:, t.s2], place[:].unsqueeze(1).to_broadcast([P, 2, E]), ALU.mult))
                ch.link(dve.tensor_reduce(dest_f[:], at[:], AX.X, ALU.add))
                if (t + -2).live:
                    dve.wait_ge(scattered[(t + -2).s4], 32 * (t + -2).quarter + 32)
                ch.link(dve.tensor_copy(all_dest[:, bass.ds(2 * t.n, 2)], dest_f[:]))
                dve.tensor_copy(dest_now[:, t.s2], dest_f[:]).then_inc(m["dest_done"], 1)

            def step(t):
                if t.live:
                    norm(t)
                if (t + -2).live:
                    choose(t + -2)
                if (t + -3).live:
                    put(t + -3)
                if t.live:
                    affine(t)

            pipeline(dve, step, 3)
            ch = Chain(dve, m["tail_step"], 0)
            dve.wait_ge(m["ranked"], NT + 1)
            ch.link(dve.tensor_copy(n_rows[:], p_r[:, 1, 0:E]))
            ch.link(dve.tensor_tensor(tab_f[:], n_rows[:], base[:], ALU.add))
            ch.link(dve.tensor_copy(table[:, 2], tab_f[:]))
            ch.link(dve.tensor_scalar(tab_f[:], n_rows[:], float(P - 1), None, ALU.add))
            ch.link(dve.tensor_copy(tab_i[:], tab_f[:]))
            ch.link(dve.tensor_scalar(n_blk[:], tab_i[:], 7, None, ALU.logical_shift_right))
            ch.link(dve.tensor_copy(n_rows[:], n_blk[:]))
            ch.link(dve.tensor_tensor_scan(tab_f[:], ones[:, 0:E], n_rows[:], 0.0, ALU.mult, ALU.add))
            ch.link(dve.tensor_copy(table[:, 1], tab_f[:]))
            ch.link(dve.tensor_scalar(tab_l[:], tab_f[:], -1.0, 0.0, ALU.add, ALU.max))
            ch.link(dve.tensor_copy(table[:, 3], tab_l[:]))
            ch.link(dve.tensor_tensor(n_rows[:], tab_f[:], n_rows[:], ALU.subtract))
            ch.link(dve.tensor_copy(table[:, 0], n_rows[:]))
            ch.link(dve.scalar_tensor_tensor(out=shift[:], in0=n_rows[:], scalar=float(P), in1=base[:], op0=ALU.mult,
                                             op1=ALU.subtract))
            ch.link(dve.tensor_tensor(all_at[:], all_chosen[:].rearrange("p t n e -> p (t n) e"),
                                      shift[:].unsqueeze(1).to_broadcast([P, 2 * NT, E]), ALU.mult))
            ch.link(dve.tensor_reduce(moved[:], all_at[:], AX.X, ALU.add))
            dve.tensor_tensor(dest[:], all_dest[:], moved[:], ALU.add)


def experts(nc, used, keep, w_gate, w_up, w_down, rows, results):
    ident, table, marks = keep["ident"], keep["table"], keep["marks"]
    CHUNKS = KD + KF
    PIECE = 2
    PIECES = CHUNKS // PIECE
    with ExitStack() as ctx:
        s = Scope(nc, ctx, "moe", used)
        gu_raw, dn_raw = s.sb("gu_raw", [P, KD, 2, FF]), s.sb("dn_raw", [P, KF, D])
        gu_hi, gu_lo = s.sb("gu_hi", [P, KD, 2, FF], F32R), s.sb("gu_lo", [P, KD, 2, FF], F32R)
        dn_hi, dn_lo = s.sb("dn_hi", [P, KF, D], F32R), s.sb("dn_lo", [P, KF, D], F32R)
        x_raw = s.sb("x_raw", [P, D])
        x_hi, x_lo = s.sb("x_hi", [P, KD, P], F32R), s.sb("x_lo", [P, KD, P], F32R)
        act_g, h = s.sb("act_g", [P, FF]), s.sb("h", [P, FF])
        h_hi, h_lo = s.sb("h_hi", [P, KF, P], F32R), s.sb("h_lo", [P, KF, P], F32R)
        y = s.sb("y", [P, D])
        zeros = s.sb("zeros", [P, D])
        p_gu, p_y = s.ps("p_gu", [P, 2, FF]), s.ps("p_y", [P, 2, NB])
        p_x, p_h = s.ps("p_x", [P, 2, NB]), s.ps("p_h", [P, 2, NB])
        names = ("hi_done", "lo_done", "x_in", "x_turned", "x_hi_done", "x_lo_done", "gu_used", "dn_used",
                 "silu_done", "h_done", "h_turned", "h_hi_done", "h_lo_done", "y_out", "y_stored", "zeros_set",
                 "tails_written", "unused_filled")
        m = {n: s.sem(n) for n in names}
        piece_in = [s.sem(f"piece_in{i}") for i in range(PIECES)]
        block = ctx.enter_context(nc.Block())

        def span(eng, e):
            first = eng.value_load(table[0:1, 0, bass.ds(e, 1)], min_val=0, max_val=BLOCKS)
            end = eng.value_load(table[0:1, 1, bass.ds(e, 1)], min_val=0, max_val=BLOCKS)
            return first, end

        def chunk(c):
            if c < KD:
                return tuple(w[:, c].rearrange("p g f -> p (g f)") for w in (gu_raw, gu_hi, gu_lo))
            return tuple(w[:, c - KD] for w in (dn_raw, dn_hi, dn_lo))

        def row_of(shifted):
            return nc.s_assert_within(shifted - BLOCKS * P, 0, E * CAP, skip_runtime_bounds_check_because=
                                      "a block of an expert lies in the expert's region")

        def expert_blocks(eng, e, run_block, split, last):
            first, end = span(eng, e)
            with eng.If(end > first + 1):
                with eng.Fori(first, end - 1) as b:
                    run_block(b, None)
            with eng.If(end > first):
                run_block(eng.value_load(table[0:1, 3, bass.ds(e, 1)], min_val=0, max_val=BLOCKS - 1),
                          None if last else e + 1)
            if not last:
                with eng.If(end == first):
                    split(e + 1, end, range(CHUNKS))

        @block.sync
        def _(sp):
            def load_weights(e, first=False):
                for i in range(PIECES):
                    a, b = i * PIECE, (i + 1) * PIECE
                    if not first:
                        sp.wait_ge(m["lo_done"], (e - 1) * CHUNKS + b)
                    if a < KD:
                        for g, w in enumerate((w_gate, w_up)):
                            sp.dma_start(gu_raw[:, a:b, g], w.rearrange("l e (k p) f -> (l e) p k f", p=P)[
                                bass.ds(e, 1), :, a:b].rearrange("e p k f -> p (e k) f")).then_inc(piece_in[i], 16)
                    else:
                        sp.dma_start(dn_raw[:, a - KD:b - KD], w_down.rearrange("l e (k p) d -> (l e) p k d", p=P)[
                            bass.ds(e, 1), :, a - KD:b - KD].rearrange("e p k d -> p (e k) d")
                                     ).then_inc(piece_in[i], 16)

            def load_x(b, row):
                wait_apart(sp, marks["sp"], m["x_turned"], b + 1)
                sp.dma_start(x_raw[:], rows[bass.ds(row, P), :]).then_inc(m["x_in"], 16)

            def load_blocks(e, at_first=False, last=False):
                first, end = span(sp, e)
                shift = sp.snap(e * CAP - first * P + BLOCKS * P)
                

                def row(b):
                    return row_of(sp.snap(b * P + shift))

                wait_apart(sp, marks["sp"], m["tails_written"], e * 16 + 16)
                with sp.If(end > first):
                    load_x(first, row(first))
                if at_first:
                    load_weights(e, True)
                with sp.If(end > first + 1):
                    load_x(first + 1, row(first + 1))
                if not last:
                    load_weights(e + 1)
                with sp.If(end > first + 2):
                    with sp.Fori(first + 2, end) as b:
                        load_x(b, row(b))
                return end

            load_blocks(0, at_first=True)
            with sp.Fori(1, E - 1) as e:
                load_blocks(e)
            end = load_blocks(E - 1, last=True)
            sp.wait_ge(m["tails_written"], 16 * E + 16)
            load_x(end, E * CAP)
            with sp.Fori(end, BLOCKS) as b:
                sp.dma_start(results[bass.ds(b * P, P), :], zeros[:]).then_inc(m["unused_filled"], 16)
            with sp.Fori(0, end):
                sp.sem_inc(m["unused_filled"], 16)
            sp.wait_ge(m["unused_filled"], BLOCKS * 16)

        @block.gpsimd
        def _(pool):
            pool.memset(zeros[:], 0.0).then_inc(m["zeros_set"], 1)
            pool.wait_ge(m["zeros_set"], 1)
            with pool.Fori(0, E) as e:
                at_row = pool.value_load(table[0:1, 2, bass.ds(e, 1)], min_val=0, max_val=E * CAP)
                pool.dma_start(rows[bass.ds(at_row, P), :], zeros[:]).then_inc(m["tails_written"], 16)
                pool.wait_ge(m["tails_written"], 16 * e + 16)
            pool.dma_start(rows[E * CAP:E * CAP + P, :], zeros[:]).then_inc(m["tails_written"], 16)

        @block.tensor
        def _(pe):
            pe.sem_inc(m["gu_used"], KD)
            pe.sem_inc(m["dn_used"], KF)
            pe.sem_inc(m["x_turned"], 1)

            def turn_x(b):
                pe.wait_ge(m["x_in"], 16 * b + 16)
                for k in range(KD):
                    mm = pe.transpose(p_x[:, k // 4, k % 4 * P:(k % 4 + 1) * P], x_raw[:, k * P:(k + 1) * P], ident[:])
                mm.then_inc(m["x_turned"], 1)

            turn_x(0)
            with pe.Fori(0, E) as e:
                first, end = span(pe, e)
                with pe.If(end > first):
                    with pe.Fori(first, end) as b:
                        pe.wait_ge(m["x_lo_done"], b + 1)
                        for k in range(KD):
                            pe.wait_ge(m["lo_done"], e * CHUNKS + (k + 1))
                            for g in range(2):
                                mm = product(pe, p_gu[:, g], ((x_hi[:, k], gu_hi[:, k, g]), (x_hi[:, k], gu_lo[:, k, g]),
                                                              (x_lo[:, k], gu_hi[:, k, g])), k == 0, k == KD - 1)
                            mm.then_inc(m["gu_used"], 1)
                        turn_x(b + 1)
                        for i in range(2):
                            pe.wait_ge(m["h_done"], 2 * b + (i + 1))
                            for j in range(2):
                                f = 2 * i + j
                                mm = pe.transpose(p_h[:, i, j * P:(j + 1) * P], h[:, f * P:(f + 1) * P], ident[:])
                            mm.then_inc(m["h_turned"], 1)
                        pe.wait_ge(m["y_out"], 2 * b + 2)
                        for k in range(KF):
                            pe.wait_ge(m["h_lo_done"], 2 * b + (k // 2 + 1))
                            pe.wait_ge(m["lo_done"], e * CHUNKS + (KD + k + 1))
                            for n in range(2):
                                w = slice(n * NB, (n + 1) * NB)
                                mm = product(pe, p_y[:, n], ((h_hi[:, k], dn_hi[:, k, w]), (h_hi[:, k], dn_lo[:, k, w]),
                                                             (h_lo[:, k], dn_hi[:, k, w])), k == 0, k == KF - 1)
                            mm.then_inc(m["dn_used"], 1)

        @block.scalar
        def _(act):
            act.sem_inc(m["y_out"], 2)
            act.sem_inc(m["y_stored"], 16)

            def split(e, first, chunks):
                for c in chunks:
                    raw, hi, lo = chunk(c)
                    if c % PIECE == 0:
                        dmas = 32 if c < KD else 16
                        act.wait_ge(piece_in[c // PIECE], dmas * e + dmas)
                    if first is not None:
                        if c < KD:
                            act.wait_ge(m["gu_used"], first * KD + (c + 1))
                        else:
                            act.wait_ge(m["dn_used"], first * KF + (c - KD + 1))
                    act.activation(hi, raw, ACT.Copy).then_inc(m["hi_done"], 1)

            def high_x(b):
                act.wait_ge(m["x_turned"], b + 2)
                for n in range(2):
                    act.activation(x_hi[:, 4 * n:4 * n + 4], p_x[:, n].rearrange("p (k t) -> p k t", t=P), ACT.Copy
                                   ).then_inc(m["x_hi_done"], 1)

            def run_block(b, e_next):
                act.wait_ge(m["gu_used"], b * KD + 2 * KD)
                for i in range(2):
                    act.activation(act_g[:, i * 256:(i + 1) * 256], p_gu[:, 0, i * 256:(i + 1) * 256], ACT.Silu
                                   ).then_inc(m["silu_done"], 1)
                for i in range(2):
                    act.wait_ge(m["h_turned"], 2 * b + (i + 1))
                    act.activation(h_hi[:, 2 * i:2 * i + 2], p_h[:, i, 0:2 * P].rearrange("p (k t) -> p k t", t=P),
                                   ACT.Copy).then_inc(m["h_hi_done"], 1)
                high_x(b + 1)
                if e_next is not None:
                    split(e_next, b + 1, range(KD))
                act.wait_ge(m["dn_used"], b * KF + 2 * KF)
                act.wait_ge(m["y_stored"], 16 * b + 16)
                for n in range(2):
                    act.activation(y[:, n * NB:(n + 1) * NB], p_y[:, n], ACT.Copy).then_inc(m["y_out"], 1)
                act.wait_ge(m["y_out"], 2 * b + 4)
                act.dma_start(results[bass.ds(b * P, P), :], y[:]).then_inc(m["y_stored"], 16)
                if e_next is not None:
                    split(e_next, b + 1, range(KD, CHUNKS))

            high_x(0)
            split(0, None, range(CHUNKS))
            with act.Fori(0, E - 1) as e:
                expert_blocks(act, e, run_block, split, False)
            expert_blocks(act, E - 1, run_block, split, True)
            total = act.value_load(table[0:1, 1, E - 1:E], min_val=0, max_val=BLOCKS)
            wait_apart(act, marks["act"], m["y_stored"], total * 16 + 16)

        @block.vector
        def _(dve):
            def split(e, first, chunks):
                for c in chunks:
                    raw, hi, lo = chunk(c)
                    dve.wait_ge(m["hi_done"], e * CHUNKS + (c + 1))
                    dve.tensor_tensor(lo, raw, f32(hi), ALU.subtract).then_inc(m["lo_done"], 1)

            def low_x(b):
                for n in range(2):
                    dve.wait_ge(m["x_hi_done"], 2 * b + (n + 1))
                    part = (slice(None), slice(4 * n, 4 * n + 4))
                    ins = dve.tensor_tensor(x_lo[part], p_x[:, n].rearrange("p (k t) -> p k t", t=P), f32(x_hi[part]),
                                            ALU.subtract)
                ins.then_inc(m["x_lo_done"], 1)

            def run_block(b, e_next):
                for i in range(2):
                    w = slice(i * 256, (i + 1) * 256)
                    dve.wait_ge(m["silu_done"], 2 * b + (i + 1))
                    dve.tensor_tensor(h[:, w], p_gu[:, 1, w], act_g[:, w], ALU.mult).then_inc(m["h_done"], 1)
                for i in range(2):
                    part = (slice(None), slice(2 * i, 2 * i + 2))
                    dve.wait_ge(m["h_hi_done"], 2 * b + (i + 1))
                    dve.tensor_tensor(h_lo[part], p_h[:, i, 0:2 * P].rearrange("p (k t) -> p k t", t=P),
                                      f32(h_hi[part]), ALU.subtract).then_inc(m["h_lo_done"], 1)
                low_x(b + 1)
                if e_next is not None:
                    split(e_next, None, range(CHUNKS))

            low_x(0)
            split(0, None, range(CHUNKS))
            with dve.Fori(0, E - 1) as e:
                expert_blocks(dve, e, run_block, split, False)
            expert_blocks(dve, E - 1, run_block, split, True)


def combine_norm(nc, used, keep, results, x1, mod_rows, ln2_g, ln2_b, out):
    dest, gate_w, marks = keep["dest"], keep["gate_w"], keep["marks"]
    A_OPS, V_OPS = 5, 2
    with ExitStack() as ctx:
        s = Scope(nc, ctx, "fin", used)
        g2r, ln_g, ln_b = (s.sb(n, [P, D]) for n in ("g2r", "ln_g", "ln_b"))
        idx = s.sb("idx", [P, 4, 2], U32)
        yy, xt = s.sb("yy", [P, 4, 2, D]), s.sb("xt", [P, 2, D])
        first, y, res = s.sb("first", [P, 2, D]), s.sb("y", [P, 2, D]), s.sb("res", [P, 2, D])
        stats, mv = s.sb("stats", [P, 2, 6]), s.sb("mv", [P, 2, 2])
        var, rstd, offset = s.sb("var", [P, 1]), s.sb("rstd", [P, 2]), s.sb("offset", [P, 2])
        minus_half = s.sb("minus_half", [P, 1])
        names = ("const_in", "half_set", "idx_done", "first_done", "a_step", "summed", "var_step", "rstd_done",
                 "normed", "scaled", "res_done")
        m = {n: s.sem(n) for n in names}
        x_in, stored = ([s.sem(f"{n}{i}") for i in range(2)] for n in ("x_in", "stored"))
        y_in = [s.sem(f"y_in{i}") for i in range(4)]
        block = ctx.enter_context(nc.Block())

        @block.sync
        def _(sp):
            def load_x(t):
                if (t + -2).live:
                    sp.wait_ge(m["summed"], t.n - 1)
                sp.dma_start(xt[:, t.s2], x1[bass.ds(t.n * P, P), :]).then_inc(x_in[t.s2], 16)

            for dst, src in ((g2r, mod_rows[G2 * P:G2 * P + D].rearrange("(a d) -> a d", a=1).to_broadcast([P, D])),
                             (ln_g, ln2_g.to_broadcast([P, D])), (ln_b, ln2_b.to_broadcast([P, D]))):
                sp.dma_start(dst[:], src).then_inc(m["const_in"], 16)
            pipeline(sp, load_x, 0)

        @block.gpsimd
        def _(pool):
            def gather(t):
                if (t + -4).live:
                    wait_apart(pool, marks["pool"], m["summed"], t.n - 3)
                pool.tensor_copy(idx[:, t.s4], dest[:, bass.ds(2 * t.n, 2)]).then_inc(m["idx_done"], 1)
                wait_apart(pool, marks["pool"], m["idx_done"], t.n + 1)
                for k in range(2):
                    pool.indirect_dma_start(out=yy[:, t.s4, k], out_offset=None, in_=results, in_offset=bass.IndirectOffsetOnAxis(
                        ap=idx[:, t.s4, k:k + 1], axis=0)).then_inc(y_in[t.s4], 16)

            def deviation(t):
                ch = Chain(pool, m["var_step"], V_OPS * t.n)
                if (t + -2).live:
                    pool.wait_ge(m["normed"], t.n - 1)
                wait_apart(pool, marks["pool"], m["summed"], t.n + 1)
                ch.link(pool.tensor_scalar(var[:], mv[:, t.s2, 1:2], EPS, None, ALU.add))
                ch.link(pool.tensor_tensor(rstd[:, t.s2:t.s2 + 1], var[:], minus_half[:], ALU.pow), marks["pool"])
                pool.tensor_scalar(offset[:, t.s2:t.s2 + 1], mv[:, t.s2, 0:1], rstd[:, t.s2:t.s2 + 1], -1.0, ALU.mult,
                                   ALU.mult).then_inc(m["rstd_done"], 1)

            def add_bias(t):
                pool.wait_ge(m["scaled"], t.n + 1)
                pool.tensor_tensor(res[:, t.s2], res[:, t.s2], ln_b[:], ALU.add).then_inc(m["res_done"], 1)

            def step(t):
                if t.live:
                    deviation(t)
                if (t + 4).live:
                    gather(t + 4)
                if (t + -1).live:
                    add_bias(t + -1)

            for o in range(4):
                gather(Tile(0, o))
            pool.memset(minus_half[:], -0.5).then_inc(m["half_set"], 1)
            pool.wait_ge(m["const_in"], 48)
            pool.wait_ge(m["half_set"], 1)
            pipeline(pool, step, 1)

        @block.scalar
        def _(act):
            def weigh(t):
                act.wait_ge(y_in[t.s4], 32 * t.quarter + 32)
                if (t + -2).live:
                    act.wait_ge(m["summed"], t.n - 1)
                act.activation(first[:, t.s2], yy[:, t.s4, 0], ACT.Copy, scale=gate_w[:, bass.ds(2 * t.n, 1)]
                               ).then_inc(m["first_done"], 1)

            def norm(t):
                act.wait_ge(m["rstd_done"], t.n + 1)
                if (t + -2).live:
                    act.wait_ge(stored[t.s2], 16 * t.half)
                act.activation(res[:, t.s2], y[:, t.s2], ACT.Identity, bias=offset[:, t.s2:t.s2 + 1],
                               scale=rstd[:, t.s2:t.s2 + 1]).then_inc(m["normed"], 1)

            def store(t):
                act.wait_ge(m["res_done"], t.n + 1)
                act.dma_start(out.rearrange("b t d -> (b t) d")[bass.ds(t.n * P, P), :], res[:, t.s2]
                              ).then_inc(stored[t.s2], 16)

            def step(t):
                if (t + 1).live:
                    weigh(t + 1)
                if (t + -1).live:
                    store(t + -1)
                if t.live:
                    norm(t)

            weigh(Tile(0, 0))
            pipeline(act, step, 1)
            for i in range(2):
                act.wait_ge(stored[i], 16 * (NT // 2))

        @block.vector
        def _(dve):
            dve.wait_ge(m["const_in"], 48)

            def total(t):
                ch = Chain(dve, m["a_step"], A_OPS * t.n)
                dve.wait_ge(m["first_done"], t.n + 1)
                dve.wait_ge(x_in[t.s2], 16 * t.half + 16)
                if (t + -2).live:
                    dve.wait_ge(m["normed"], t.n - 1)
                yt = y[:, t.s2]
                ch.link(dve.scalar_tensor_tensor(out=yt, in0=yy[:, t.s4, 1], scalar=gate_w[:, bass.ds(2 * t.n + 1, 1)],
                                                 in1=first[:, t.s2], op0=ALU.mult, op1=ALU.add))
                ch.link(dve.tensor_tensor(yt, yt, g2r[:], ALU.mult))
                ch.link(dve.scalar_tensor_tensor(out=yt, in0=xt[:, t.s2], scalar=ALPHA, in1=yt, op0=ALU.mult,
                                                 op1=ALU.add))
                for n in range(2):
                    ch.link(dve.bn_stats(stats[:, n], y[:, t.s2, n * NB:(n + 1) * NB]), marks["dve"] if n == 1 else None)
                dve.bn_aggr(mv[:, t.s2], stats[:].rearrange("p a b -> p (a b)")).then_inc(m["summed"], 1)

            def step(t):
                if t.live:
                    total(t)
                b = t + -1
                if b.live:
                    dve.wait_ge(m["normed"], b.n + 1)
                    dve.tensor_tensor(res[:, b.s2], res[:, b.s2], ln_g[:], ALU.mult).then_inc(m["scaled"], 1)

            pipeline(dve, step, 1)


def hybrid_layer(nc, x, c, w_ada, b_ada, w_in, w_conv, w_a, w_b, w_o, ln1_g, ln1_b, w_router, b_router, w_gate, w_up,
                 w_down, ln2_g, ln2_b, out):
    def scratch(name, shape):
        return nc.dram_tensor(name, shape, F32, kind="Internal").ap()

    mod_rows = scratch("mod_rows", [6 * D])
    qkv_hi, qkv_lo = scratch("qkv_hi", [3 * AW, S]), scratch("qkv_lo", [3 * AW, S])
    conv_t, gate_t = scratch("conv_t", [CH, S]), scratch("gate_t", [2 * D, S])
    o_t, m_t, x1 = scratch("o_t", [AW, S]), scratch("m_t", [D, S]), scratch("x1", [S, D])
    rows, results = scratch("rows", [E * CAP + P, D]), scratch("results", [BLOCKS * P, D])
    used = []
    with ExitStack() as ctx:
        s = Scope(nc, ctx, "keep", [])
        keep = {
            "ident": s.sb("ident", [P, P]), "mod": s.sb("mod", [P, 6 * KD]), "conv_cols": s.sb("conv_cols", [P, 3 * KC]),
            "dest": s.sb("dest", [P, 2 * NT], U32), "gate_w": s.sb("gate_w", [P, 2 * NT]),
            "table": s.sb("table", [P, 4, E], I32),
            "csilu": s.sb("csilu", [P, KD]),
            "marks": {n: s.sem(f"mark_{n}") for n in ("sp", "act", "pool", "pe", "dve")},
        }
        modulation(nc, used, keep, c, w_ada, b_ada, w_conv)
        with ExitStack() as uctx:
            us = Scope(nc, uctx, "u", [])
            u_hi, u_lo = us.sb("hi", [P, KD, S], F32R), us.sb("lo", [P, KD, S], F32R)
            modulated_input(nc, used, keep, x, u_hi, u_lo)
            input_projection(nc, used, keep, u_hi, u_lo, w_in, qkv_hi, qkv_lo, conv_t, gate_t)
        attention(nc, used, keep, qkv_hi, qkv_lo, w_ada, o_t, mod_rows)
        clear_semaphores(nc, used)
        branch_outputs(nc, used, keep, conv_t, o_t, gate_t, w_a, w_b, m_t)
        mix_norm_route(nc, used, keep, m_t, w_o, x, mod_rows, ln1_g, ln1_b, w_router, b_router, x1, rows, results)
        experts(nc, used, keep, w_gate, w_up, w_down, rows, results)
        combine_norm(nc, used, keep, results, x1, mod_rows, ln2_g, ln2_b, out)


_INS = ["x", "c", "w_ada", "b_ada", "w_in", "w_conv", "w_a", "w_b", "w_o", "ln1_g", "ln1_b", "w_router", "b_router",
        "w_gate", "w_up", "w_down", "ln2_g", "ln2_b"]


def kernel(**inputs):
    import numpy as np
    import concourse.bacc as bacc
    from concourse.bass_utils import run_bass_kernel_spmd

    nc = bacc.Bacc("TRN2", target_bir_lowering=False, num_devices=1)
    arrays, args = {}, []
    for name in _INS:
        a = np.ascontiguousarray(inputs[name])
        arrays[f"in_{name}"] = a
        args.append(nc.dram_tensor(f"in_{name}", a.shape, mybir.dt.from_np(a.dtype), kind="ExternalInput").ap())
    out = nc.dram_tensor("out", (1, S, D), F32, kind="ExternalOutput").ap()
    hybrid_layer(nc, *args, out)
    r = run_bass_kernel_spmd(nc, [arrays], core_ids=[0])
    return r.results[0]["out"]
```
